# Optimizing a Trainium2 kernel written in Bass

```python
import math
import jax, jax.numpy as jnp
from jax import lax
import numpy as np

D_MODEL = 2048
BATCH = 1
SEQ = 256
DEPTH = 1

MEM_LEN = 256
MEM_HEADS = 4
MEM_HEAD_DIM = D_MODEL // MEM_HEADS

SC_W = D_MODEL // 4
SC_K = 3

RW_HEAD_DIM = 64
RW_W = D_MODEL // 4
RW_HEADS = RW_W // RW_HEAD_DIM
RW_LORA_W = 96
RW_LORA_A = 96
RW_LORA_G = 256
RW_DECAY_SCALE = math.exp(-0.5)
RW_LN_EPS = 64e-5

RET_HEADS = 4
RET_DK = 128
RET_DV = 2 * RET_DK
RET_CHUNK = 128
RET_LN_EPS = 1e-5

NSA_HEADS = 8
NSA_KV_HEADS = 2
NSA_DH = 64
NSA_GROUP = NSA_HEADS // NSA_KV_HEADS
CMP_LEN = 32
CMP_STRIDE = 16
CMP_HIDDEN = 256
SEL_BLOCK = 64
SEL_TOP = 16
WINDOW = 512
Q_BLOCK = 128

FFN_DIM = 5632
FFN_K = 3

ROPE_THETA = 10000.0
EPS = 1e-6
N_BRANCH = 4

SC_SIZES = (SC_W, SC_W, SC_W)
RW_SIZES = (RW_W, RW_W, RW_W, RW_LORA_W, RW_LORA_A, RW_LORA_G)
RET_SIZES = (RET_HEADS * RET_DK, RET_HEADS * RET_DK, RET_HEADS * RET_DV, RET_HEADS * RET_DV)
NSA_SIZES = (NSA_HEADS * NSA_DH,) + (NSA_KV_HEADS * NSA_DH,) * 6 + (NSA_HEADS * 3,)
GATE_SIZES = (D_MODEL,) * N_BRANCH
GROUP_SIZES = (sum(SC_SIZES), sum(RW_SIZES), sum(RET_SIZES), sum(NSA_SIZES), sum(GATE_SIZES))
N_IN = sum(GROUP_SIZES)
RW_TOTAL = sum(RW_SIZES)
BR_SIZES = (SC_W, RW_W, RET_HEADS * RET_DV, NSA_HEADS * NSA_DH)
N_BR = sum(BR_SIZES)

kernel_name = "hybrid_gated_parallel_mixer_trunk"

def _split(x, sizes, axis=-1):
    return jnp.split(x, [int(c) for c in np.cumsum(sizes)[:-1]], axis=axis)

def rms_norm(x, g):
    xf = x.astype(jnp.float32)
    y = xf * lax.rsqrt(jnp.mean(xf * xf, axis=-1, keepdims=True) + EPS)
    return (y * g.astype(jnp.float32)).astype(x.dtype)

def head_norm(x, eps):
    xf = x.astype(jnp.float32)
    mu = jnp.mean(xf, axis=-1, keepdims=True)
    var = jnp.mean(jnp.square(xf - mu), axis=-1, keepdims=True)
    return (xf - mu) * lax.rsqrt(var + eps)

def causal_dwconv(x, w):
    k_w = w.shape[0]
    s = x.shape[1]
    xp = jnp.pad(x, ((0, 0), (k_w - 1, 0), (0, 0)))
    y = w[0] * xp[:, 0:s]
    for j in range(1, k_w):
        y = y + w[j] * xp[:, j:j + s]
    return y

def rope_freqs(d):
    return ROPE_THETA ** (-jnp.arange(0, d, 2, dtype=jnp.float32) / d)

def retnet_freqs(d):
    return 1.0 / (ROPE_THETA ** jnp.linspace(0.0, 1.0, d // 2, dtype=jnp.float32))

def rope(x, pos, inv_freq):
    ang = pos.astype(jnp.float32)[..., None] * inv_freq
    cos = jnp.cos(ang)[:, :, None, :].astype(x.dtype)
    sin = jnp.sin(ang)[:, :, None, :].astype(x.dtype)
    x1, x2 = jnp.split(x, 2, axis=-1)
    return jnp.concatenate([x1 * cos - x2 * sin, x2 * cos + x1 * sin], axis=-1)

def masked_softmax(s, mask):
    s = jnp.where(mask, s.astype(jnp.float32), -jnp.inf)
    m = jnp.max(s, axis=-1, keepdims=True)
    m = jnp.where(jnp.isfinite(m), m, 0.0)
    e = jnp.where(mask, jnp.exp(s - m), 0.0)
    return e / jnp.maximum(jnp.sum(e, axis=-1, keepdims=True), 1e-30)

def short_conv_mixer(b_gate, c_gate, xin, w_conv):
    return b_gate * causal_dwconv(c_gate * xin, w_conv)

def wkv7_scan(r, w, k, v, kk, a):
    bsz, _, nh, nd = r.shape
    xs = tuple(jnp.moveaxis(t, 1, 0) for t in (r, w, k, v, kk, a))

    def step(state, inp):
        r_t, w_t, k_t, v_t, kk_t, a_t = inp
        sa = jnp.einsum('bhvk,bhk->bhv', state, -kk_t)
        state = (state * w_t[:, :, None, :]
                 + sa[..., None] * (kk_t * a_t)[:, :, None, :]
                 + v_t[..., None] * k_t[:, :, None, :])
        return state, jnp.einsum('bhvk,bhk->bhv', state, r_t)

    s0 = jnp.zeros((bsz, nh, nd, nd), jnp.float32)
    _, y = lax.scan(step, s0, xs)
    return jnp.moveaxis(y, 0, 1)

def rwkv7_mixer(z, mu, w0, w_w2, a0, w_a2, w_g2, k_k, k_a, r_k, lnx_g, lnx_b):
    bsz, s, _ = z.shape
    z_prev = jnp.pad(z, ((0, 0), (1, 0), (0, 0)))[:, :-1]
    z = z + (z_prev - z) * mu
    r, k, v, zw, za, zg = _split(z, RW_SIZES)
    d = w0 + jnp.tanh(zw) @ w_w2
    w = jnp.exp(-RW_DECAY_SCALE * jax.nn.sigmoid(d.astype(jnp.float32)))
    a = jax.nn.sigmoid(a0 + za @ w_a2)
    g = jax.nn.sigmoid(zg) @ w_g2
    heads = lambda t: t.reshape(bsz, s, RW_HEADS, RW_HEAD_DIM).astype(jnp.float32)
    kk = heads(k * k_k)
    kk = kk / jnp.maximum(jnp.sqrt(jnp.sum(kk * kk, axis=-1, keepdims=True)), 1e-12)
    k = k * (1.0 + (a - 1.0) * k_a)
    rh, kh, vh, ah, wh = heads(r), heads(k), heads(v), heads(a), heads(w)
    y = wkv7_scan(rh, wh, kh, vh, kk, ah)
    y = head_norm(y, RW_LN_EPS) * lnx_g.reshape(RW_HEADS, RW_HEAD_DIM) + lnx_b.reshape(RW_HEADS, RW_HEAD_DIM)
    bonus = jnp.sum(rh * kh * r_k, axis=-1, keepdims=True) * vh
    return (y + bonus).reshape(bsz, s, RW_W).astype(z.dtype) * g

def retention_mixer(q, k, v, gate, positions):
    bsz, s, _ = q.shape
    nh, dk, dv, c = RET_HEADS, RET_DK, RET_DV, RET_CHUNK
    n = s // c
    inv = retnet_freqs(dk)
    q = rope(q.reshape(bsz, s, nh, dk), positions, inv)
    k = rope(k.reshape(bsz, s, nh, dk), positions, inv) * (dk ** -0.5)
    v = v.reshape(bsz, s, nh, dv)
    chunk = lambda t: t.reshape(bsz, n, c, nh, t.shape[-1]).transpose(0, 3, 1, 2, 4)
    qc, kc, vc = chunk(q), chunk(k), chunk(v)
    lg = jnp.log(1.0 - 2.0 ** (-5.0 - jnp.arange(nh, dtype=jnp.float32)))
    idx = jnp.arange(c, dtype=jnp.float32)
    diff = idx[:, None] - idx[None, :]
    decay_in = jnp.where(diff >= 0, jnp.exp(jnp.maximum(diff, 0.0) * lg[:, None, None]), 0.0)
    scores = jnp.einsum('bhncd,bhnmd->bhncm', qc, kc) * decay_in[:, None]
    o_inner = jnp.einsum('bhncm,bhnme->bhnce', scores, vc)
    zeta = jnp.exp((c - 1 - idx)[None, :] * lg[:, None])
    xi = jnp.exp((idx + 1.0)[None, :] * lg[:, None])
    u = jnp.einsum('bhnmd,bhnme->bhnde', kc * zeta[:, None, :, None], vc)
    chunk_decay = jnp.exp(c * lg)[:, None, None]

    def step(state, u_i):
        return state * chunk_decay + u_i, state

    _, r_prev = lax.scan(step, jnp.zeros((bsz, nh, dk, dv), u.dtype), jnp.moveaxis(u, 2, 0))
    r_prev = jnp.moveaxis(r_prev, 0, 2)
    o_cross = jnp.einsum('bhncd,bhnde->bhnce', qc * xi[:, None, :, None], r_prev)
    o = (o_inner + o_cross).transpose(0, 2, 3, 1, 4).reshape(bsz, s, nh, dv)
    o = head_norm(o, RET_LN_EPS).reshape(bsz, s, nh * dv).astype(gate.dtype)
    return o * jax.nn.silu(gate)

def nsa_mixer(q, kc, vc, ks, vs, kw, vw, gates, positions, cmp_pos, cmp_w1, cmp_w2):
    bsz, s, _ = q.shape
    nh, ng, hpg, dh = NSA_HEADS, NSA_KV_HEADS, NSA_GROUP, NSA_DH
    inv = rope_freqs(dh)
    scale = dh ** -0.5
    q = rope(q.reshape(bsz, s, nh, dh), positions, inv)
    kv_shape = (bsz, s, ng, dh)
    kc, vc, vs, vw = kc.reshape(kv_shape), vc.reshape(kv_shape), vs.reshape(kv_shape), vw.reshape(kv_shape)
    ks = rope(ks.reshape(kv_shape), positions, inv)
    kw = rope(kw.reshape(kv_shape), positions, inv)

    n_cmp = (s - CMP_LEN) // CMP_STRIDE + 1
    starts = np.arange(n_cmp) * CMP_STRIDE
    tok = starts[:, None] + np.arange(CMP_LEN)[None, :]
    cmp_end = starts + CMP_LEN - 1

    def compress(t, pos_emb, w1, w2):
        blk = t[:, tok] + pos_emb[:, None, :]
        blk = blk.transpose(0, 1, 3, 2, 4).reshape(bsz, n_cmp, ng, CMP_LEN * dh)
        return jax.nn.gelu(blk @ w1) @ w2

    k_cmp = rope(compress(kc, cmp_pos[0], cmp_w1[0], cmp_w2[0]), positions[:, cmp_end], inv)
    v_cmp = compress(vc, cmp_pos[1], cmp_w1[1], cmp_w2[1])
    qg = q.reshape(bsz, s, ng, hpg, dh)
    t_idx = np.arange(s)
    cmask = cmp_end[None, :] <= t_idx[:, None]
    s_cmp = jnp.einsum('bsgqd,bcgd->bgqsc', qg, k_cmp) * scale
    p_cmp = masked_softmax(s_cmp, cmask)
    o_cmp = jnp.einsum('bgqsc,bcgd->bsgqd', p_cmp.astype(v_cmp.dtype), v_cmp).reshape(bsz, s, nh, dh)

    n_sel = s // SEL_BLOCK
    jb = np.arange(n_sel)
    overlap = ((starts[:, None] < (jb[None, :] + 1) * SEL_BLOCK)
               & (starts[:, None] + CMP_LEN > jb[None, :] * SEL_BLOCK)).astype(np.float32)
    imp = jnp.einsum('bgqsc,cj->bgsj', p_cmp, overlap)
    cur = t_idx // SEL_BLOCK
    valid = jb[None, :] <= cur[:, None]
    forced = (jb[None, :] == 0) | (jb[None, :] == cur[:, None]) | (jb[None, :] == cur[:, None] - 1)
    imp = jnp.where(forced, jnp.inf, jnp.where(valid, imp, -jnp.inf))
    n_top = min(SEL_TOP, n_sel)
    _, sel_idx = lax.top_k(imp, n_top)

    qh = qg.transpose(0, 2, 3, 1, 4) * scale
    ks_blk = ks.transpose(0, 2, 1, 3).reshape(bsz, ng, n_sel, SEL_BLOCK, dh)
    vs_blk = vs.transpose(0, 2, 1, 3).reshape(bsz, ng, n_sel, SEL_BLOCK, dh)
    pad = ((0, 0), (0, 0), (WINDOW, 0), (0, 0))
    kw_pad = jnp.pad(kw.transpose(0, 2, 1, 3), pad)
    vw_pad = jnp.pad(vw.transpose(0, 2, 1, 3), pad)
    b_ix = jnp.arange(bsz)[:, None, None, None]
    g_ix = jnp.arange(ng)[None, :, None, None]

    def block(qb):
        q0 = qb * Q_BLOCK
        qblk = lax.dynamic_slice_in_dim(qh, q0, Q_BLOCK, axis=3)
        tq = q0 + jnp.arange(Q_BLOCK)
        idx = lax.dynamic_slice_in_dim(sel_idx, q0, Q_BLOCK, axis=2)
        kg = ks_blk[b_ix, g_ix, idx]
        vg = vs_blk[b_ix, g_ix, idx]
        tok_pos = idx[..., None] * SEL_BLOCK + jnp.arange(SEL_BLOCK)
        smask = (tok_pos <= tq[:, None, None]).reshape(bsz, ng, 1, Q_BLOCK, n_top * SEL_BLOCK)
        s_sel = jnp.einsum('bgqtd,bgtkld->bgqtkl', qblk, kg).reshape(bsz, ng, hpg, Q_BLOCK, n_top * SEL_BLOCK)
        p_sel = masked_softmax(s_sel, smask).reshape(bsz, ng, hpg, Q_BLOCK, n_top, SEL_BLOCK)
        o_sel = jnp.einsum('bgqtkl,bgtkld->bgqtd', p_sel.astype(vg.dtype), vg)
        kwb = lax.dynamic_slice_in_dim(kw_pad, q0, Q_BLOCK + WINDOW, axis=2)
        vwb = lax.dynamic_slice_in_dim(vw_pad, q0, Q_BLOCK + WINDOW, axis=2)
        kpos = q0 - WINDOW + jnp.arange(Q_BLOCK + WINDOW)
        dlt = tq[:, None] - kpos[None, :]
        wmask = (dlt >= 0) & (dlt < WINDOW) & (kpos[None, :] >= 0)
        s_win = jnp.einsum('bgqtd,bgkd->bgqtk', qblk, kwb)
        p_win = masked_softmax(s_win, wmask)
        o_win = jnp.einsum('bgqtk,bgkd->bgqtd', p_win.astype(vwb.dtype), vwb)
        return o_sel, o_win

    o_sel, o_win = lax.map(block, jnp.arange(s // Q_BLOCK))
    unblock = lambda o: o.transpose(1, 0, 4, 2, 3, 5).reshape(bsz, s, nh, dh)
    o_sel, o_win = unblock(o_sel), unblock(o_win)
    gt = jax.nn.sigmoid(gates.reshape(bsz, s, nh, 3))
    o = gt[..., 0:1] * o_cmp + gt[..., 1:2] * o_sel + gt[..., 2:3] * o_win
    return o.reshape(bsz, s, nh * dh)

def hybrid_mixer(h, positions, w_in, sc_conv, rw_mu, rw_w0, rw_w2, rw_a0, rw_a2, rw_g2,
                 rw_k_k, rw_k_a, rw_r_k, rw_lnx_g, rw_lnx_b, nsa_cmp_pos, nsa_cmp_w1, nsa_cmp_w2,
                 w_branch, w_out):
    z = h @ w_in
    z_sc, z_rw, z_ret, z_nsa, z_gate = _split(z, GROUP_SIZES)
    o_a = short_conv_mixer(*_split(z_sc, SC_SIZES), sc_conv)
    o_b = rwkv7_mixer(z_rw, rw_mu, rw_w0, rw_w2, rw_a0, rw_a2, rw_g2, rw_k_k, rw_k_a, rw_r_k, rw_lnx_g, rw_lnx_b)
    o_c = retention_mixer(*_split(z_ret, RET_SIZES), positions)
    o_d = nsa_mixer(*_split(z_nsa, NSA_SIZES), positions, nsa_cmp_pos, nsa_cmp_w1, nsa_cmp_w2)
    g_a, g_b, g_c, g_d = [jax.nn.sigmoid(g) for g in _split(z_gate, GATE_SIZES)]
    w_a, w_b, w_c, w_d = _split(w_branch, BR_SIZES, axis=0)
    merged = g_a * (o_a @ w_a) + g_b * (o_b @ w_b) + g_c * (o_c @ w_c) + g_d * (o_d @ w_d)
    return merged @ w_out

def memory_cross_attention(h, mem_n, wq, wkv, wo):
    bsz, s, _ = h.shape
    m = mem_n.shape[1]
    q = (h @ wq).reshape(bsz, s, MEM_HEADS, MEM_HEAD_DIM)
    k, v = jnp.split(mem_n @ wkv, 2, axis=-1)
    k = k.reshape(bsz, m, MEM_HEADS, MEM_HEAD_DIM)
    v = v.reshape(bsz, m, MEM_HEADS, MEM_HEAD_DIM)
    sc = jnp.einsum('bshd,bmhd->bhsm', q, k) * (MEM_HEAD_DIM ** -0.5)
    p = jax.nn.softmax(sc.astype(jnp.float32), axis=-1).astype(v.dtype)
    o = jnp.einsum('bhsm,bmhd->bshd', p, v).reshape(bsz, s, D_MODEL)
    return o @ wo

def conv_ffn(h, w_up, w_conv, b_conv, w_down):
    u = causal_dwconv(h @ w_up, w_conv) + b_conv
    a, b = jnp.split(u, 2, axis=-1)
    return (jax.nn.gelu(a, approximate=True) * b) @ w_down

def setup_inputs(seed: int = 0) -> dict:
    key = jax.random.key(seed)
    ks = iter(jax.random.split(key, 40))
    nrm = lambda shape, sc: sc * jax.random.normal(next(ks), shape, jnp.float32)
    gain = lambda shape: 1.0 + nrm(shape, 0.05)
    L = DEPTH
    return {
        "x": nrm((BATCH, SEQ, D_MODEL), 1.0),
        "mem": nrm((BATCH, MEM_LEN, D_MODEL), 1.0),
        "positions": jnp.tile(jnp.arange(SEQ, dtype=jnp.int32)[None, :], (BATCH, 1)),
        "ln_mix_pre": gain((L, D_MODEL)),
        "ln_mix_post": gain((L, D_MODEL)),
        "ln_mem_q": gain((L, D_MODEL)),
        "ln_mem_kv": gain((L, D_MODEL)),
        "ln_mem_post": gain((L, D_MODEL)),
        "ln_ffn_pre": gain((L, D_MODEL)),
        "ln_ffn_post": gain((L, D_MODEL)),
        "w_in": nrm((L, D_MODEL, N_IN), D_MODEL ** -0.5),
        "sc_conv": nrm((L, SC_K, SC_W), SC_K ** -0.5),
        "rw_mu": jax.random.uniform(next(ks), (L, RW_TOTAL), jnp.float32),
        "rw_w0": nrm((L, RW_W), 1.0),
        "rw_w2": nrm((L, RW_LORA_W, RW_W), 0.1),
        "rw_a0": nrm((L, RW_W), 0.5),
        "rw_a2": nrm((L, RW_LORA_A, RW_W), 0.5 * RW_LORA_A ** -0.5),
        "rw_g2": nrm((L, RW_LORA_G, RW_W), RW_LORA_G ** -0.5),
        "rw_k_k": 0.85 + nrm((L, RW_W), 0.05),
        "rw_k_a": 1.0 + nrm((L, RW_W), 0.05),
        "rw_r_k": nrm((L, RW_HEADS, RW_HEAD_DIM), 0.1),
        "rw_lnx_g": gain((L, RW_W)),
        "rw_lnx_b": nrm((L, RW_W), 0.01),
        "nsa_cmp_pos": nrm((L, 2, CMP_LEN, NSA_DH), 0.1),
        "nsa_cmp_w1": nrm((L, 2, CMP_LEN * NSA_DH, CMP_HIDDEN), (CMP_LEN * NSA_DH) ** -0.5),
        "nsa_cmp_w2": nrm((L, 2, CMP_HIDDEN, NSA_DH), CMP_HIDDEN ** -0.5),
        "w_branch": nrm((L, N_BR, D_MODEL), SC_W ** -0.5),
        "w_out": nrm((L, D_MODEL, D_MODEL), D_MODEL ** -0.5),
        "mem_wq": nrm((L, D_MODEL, D_MODEL), D_MODEL ** -0.5),
        "mem_wkv": nrm((L, D_MODEL, 2 * D_MODEL), D_MODEL ** -0.5),
        "mem_wo": nrm((L, D_MODEL, D_MODEL), D_MODEL ** -0.5),
        "ffn_w_up": nrm((L, D_MODEL, 2 * FFN_DIM), D_MODEL ** -0.5),
        "ffn_conv_w": nrm((L, FFN_K, 2 * FFN_DIM), FFN_K ** -0.5),
        "ffn_conv_b": nrm((L, 2 * FFN_DIM), 0.01),
        "ffn_w_down": nrm((L, FFN_DIM, D_MODEL), FFN_DIM ** -0.5),
    }

def reference(x, mem, positions, ln_mix_pre, ln_mix_post, ln_mem_q, ln_mem_kv, ln_mem_post,
              ln_ffn_pre, ln_ffn_post, w_in, sc_conv, rw_mu, rw_w0, rw_w2, rw_a0, rw_a2, rw_g2,
              rw_k_k, rw_k_a, rw_r_k, rw_lnx_g, rw_lnx_b, nsa_cmp_pos, nsa_cmp_w1, nsa_cmp_w2,
              w_branch, w_out, mem_wq, mem_wkv, mem_wo, ffn_w_up, ffn_conv_w, ffn_conv_b, ffn_w_down):
    for l in range(DEPTH):
        h = rms_norm(x, ln_mix_pre[l])
        y = hybrid_mixer(h, positions, w_in[l], sc_conv[l], rw_mu[l], rw_w0[l], rw_w2[l], rw_a0[l],
                         rw_a2[l], rw_g2[l], rw_k_k[l], rw_k_a[l], rw_r_k[l], rw_lnx_g[l], rw_lnx_b[l],
                         nsa_cmp_pos[l], nsa_cmp_w1[l], nsa_cmp_w2[l], w_branch[l], w_out[l])
        x = x + rms_norm(y, ln_mix_post[l])
        h = rms_norm(x, ln_mem_q[l])
        y = memory_cross_attention(h, rms_norm(mem, ln_mem_kv[l]), mem_wq[l], mem_wkv[l], mem_wo[l])
        x = x + rms_norm(y, ln_mem_post[l])
        h = rms_norm(x, ln_ffn_pre[l])
        y = conv_ffn(h, ffn_w_up[l], ffn_conv_w[l], ffn_conv_b[l], ffn_w_down[l])
        x = x + rms_norm(y, ln_ffn_post[l])
    return x


_drawn_inputs = setup_inputs


def setup_inputs(seed=0):
    import zlib

    import numpy as np

    out = dict(_drawn_inputs(seed))
    spreads = {}
    factors = {'rw_k_k': 57.812,
     'rw_k_a': 3.297,
     'rw_lnx_g': 3.979,
     'rw_lnx_b': 35.943,
     'nsa_cmp_pos': 3.33,
     'ffn_conv_b': 7.99}
    for name, (base, spread) in spreads.items():
        noise = np.random.default_rng([zlib.crc32(name.encode()), seed]).standard_normal(out[name].shape)
        drawn = base * np.exp(spread * noise) if base else spread * noise
        out[name] = __import__('jax').numpy.asarray(drawn.astype(out[name].dtype))
    for name, factor in factors.items():
        out[name] = (out[name] * factor).astype(out[name].dtype)
    return out
```

```python
import math
from contextlib import ExitStack

import numpy as np
import concourse.bass as bass
from concourse import mybir

D = 2048
T = 256
P = 128
KT = D // P
MEM_HEADS, MEM_DH = 4, 512
RW_TILES, RW_CH = 4, 64
NCH = T // RW_CH
RW_DECAY = math.exp(-0.5)
RET_HEADS = 4
NSA_SCALE = 64 ** -0.5
NCMP = (T - 32) // 16 + 1
FFN = 5632
FT = FFN // P
EPS = 1e-6
NSLOT = 4
NEG = -1e30
MAGIC = 1.5 * 2.0 ** 23
TWO_PI = (6.28125, 0.0019340515136718750, 1.2556659146e-6)



def constant_columns():
    p = np.arange(P)
    i = np.arange(P)[None, :]
    cols = {}
    cols["ident"] = np.eye(P)
    rot = np.zeros((P, P))
    for m in range(P):
        rot[(m + 64) % P, m] = -1.0 if m < 64 else 1.0
    cols["rot128"] = rot
    rot = np.zeros((P, P))
    for m in range(P):
        b, r = m // 64 * 64, m % 64
        rot[b + (r + 32) % 64, m] = -1.0 if r < 32 else 1.0
    cols["rot64"] = rot
    cols["ones64"] = (p[:, None] // 64 == i // 64).astype(float)
    cols["ones128"] = np.ones((P, P))
    for g in range(2):
        cols[f"dup{g}"] = (p[:, None] == 64 * g + i % 64).astype(float)
    s, t = (p % 64)[:, None], np.arange(64)[None, :]
    cols["strict"] = (s < t).astype(float)
    cols["incl"] = (s <= t).astype(float)
    for n in range(6):
        b = 1 << n
        cols[f"up{n}"] = ((s // (2 * b) == t // (2 * b)) & (s // b % 2 == 0) & (t // b % 2 == 1)).astype(float)
    cols["low0"] = ((s // 2 == t // 2) & (s % 2 == 1) & (t % 2 == 0)).astype(float)
    cols["eye64"] = (s == t).astype(float)
    cols["causal"] = np.where(i <= p[:, None], 0.0, NEG)
    c = np.arange(NCMP)[None, :]
    seen = np.concatenate([(16 * c + 31 <= 128 * k + p[:, None]) for k in range(2)], 1)
    cols["cmp_neg"] = np.where(seen, 0.0, NEG)
    cols["cmp_seen"] = seen.astype(float)
    cols["inv_ret"] = (1.0 / 10000.0 ** np.linspace(0.0, 1.0, 64))[p % 64][:, None]
    cols["inv_nsa"] = (10000.0 ** (-np.arange(0, 64, 2) / 64.0))[p % 32][:, None]
    return cols


def decay_table():
    d = np.arange(T)[None, :] - np.arange(P)[:, None]
    out = []
    for h in range(RET_HEADS):
        lg = math.log(1.0 - 2.0 ** (-5.0 - h))
        dec = np.where(d >= 0, np.exp(np.maximum(d, 0) * lg), 0.0) * 128 ** -0.5
        out += [dec, dec[:, :P]]
    return np.concatenate(out, 1).astype(np.float32)


def build_constants():
    cols = constant_columns()
    at, out = {}, 0
    for k, v in cols.items():
        at[k] = (out, v.shape[1])
        out += v.shape[1]
    return np.concatenate([v for v in cols.values()], 1).astype(np.float32), at


VEC = [("ln_mix_pre", 16), ("ln_mix_post", 16), ("ln_mem_q", 16), ("ln_mem_kv", 16), ("ln_mem_post", 16),
       ("ln_ffn_pre", 16), ("ln_ffn_post", 16), ("rw_mu", 16), ("rw_w0", 4), ("rw_a0", 4), ("rw_k_k", 4),
       ("rw_k_a", 4), ("rw_r_k", 4), ("rw_lnx_g", 4), ("rw_lnx_b", 4), ("sc_conv", 12), ("cmp_pos", 32),
       ("ffn_conv_w", 264), ("ffn_conv_b", 88)]
VEC_AT = {}
for _n, _c in VEC:
    VEC_AT[_n] = (sum(c for _, c in VEC[:len(VEC_AT)]), _c)
NVEC = sum(c for _, c in VEC)

MIX = ([("rw", i) for i in range(12)] + [("zw", 0), ("za", 0), ("rw", 12), ("rw", 13)]
       + [("sc", i) for i in range(12)] + [("kv", i) for i in range(6)] + [("cmp", i) for i in range(4)]
       + [("q", i) for i in range(4)] + [("gate", 0)]
       + [("rq", i) for i in range(4)] + [("rk", i) for i in range(4)] + [("rv", i) for i in range(8)]
       + [("rg", i) for i in range(8)] + [("mk", i) for i in range(16)])
NMIX = len(MIX)
AT = {}
for _n, _c in enumerate(MIX):
    AT[_c] = _n
N_MERGE = NMIX
N_WOUT = N_MERGE + 96
N_MV = N_WOUT + 16
N_WQ = N_MV + 16
N_WO = N_WQ + 16
N_UP = N_WO + 16
N_DOWN = N_UP + 88
N_END = N_DOWN + 64


def program(nc, A, const_dram, decay_dram, const_at, out):
    f32, i32 = mybir.dt.float32, mybir.dt.int32
    ALU, ACT, AX = mybir.AluOpType, mybir.ActivationFunctionType, mybir.AxisListType
    MUL, ADD, SUB, MAX, MIN = ALU.mult, ALU.add, ALU.subtract, ALU.max, ALU.min
    ctx = ExitStack()
    with ctx:
        def sb(name, shape, dt=f32):
            return ctx.enter_context(nc.sbuf_tensor(name, shape, dt))

        sems = {}

        def sem(name):
            if name not in sems:
                sems[name] = ctx.enter_context(nc.semaphore(name))
            return sems[name]

        NC = const_dram.shape[1]
        cst = sb("cst", [P, NC])
        vec = sb("vec", [P, NVEC])
        lora = sb("lora", [P, 4, 512])
        cw2 = sb("cw2", [P, 2, 2, P])
        trig = sb("trig", [P, 2, 2, T])
        posi = sb("posi", [P, T], i32)
        posf = sb("posf", [P, T])
        ring = sb("ring", [P, NSLOT, KT, P])
        hT = sb("hT", [P, KT, T])
        obr = sb("obr", [P, 20, T])
        small = sb("small", [P, 400])
        rstd = sb("rstd", [P, T])
        hidV = sb("hidV", [P, 2, 2, 2, 32])
        vcx = sb("vcx", [64, 2, P])
        gsig = sb("gsig", [32, T])
        arena = sb("arena", [P, 27600])
        decay = lora[:, :, :].rearrange("p a b -> p (a b)")[:, 0:1536].rearrange("p (h c) -> p h c", h=4)

        def cc(name):
            a, n = const_at[name]
            return cst[:, a:a + n]

        def vv(name, i=0, n=1, rows=P):
            a, _ = VEC_AT[name]
            return vec[0:rows, a + i:a + i + n]

        def slab(a, n, t=None):
            ap = arena[:, a:a + n]
            return ap if t is None else ap.rearrange("p (i t) -> p i t", t=t)

        bank = ctx.enter_context(nc.psum_tensor("bank", [P, 2, 512], f32))
        big = bank[:, :, 0:T]
        sm = ctx.enter_context(nc.psum_tensor("sm", [P, 6, 512], f32))

        xT, sq0 = slab(0, 4096, T), slab(4096, 4096, T)
        kmul = slab(8208, 1024).rearrange("p (a b t) -> p a b t", a=2, b=2)
        zp = slab(0, 4112, 257)
        Z = slab(4112, 4096, T)
        sA = [slab(1024 * i, 1024) for i in range(4)]
        sB = [slab(8208 + 1024 * i, 1024) for i in range(4)]
        QR = slab(12304, 2048).rearrange("p (g two t) -> p g two t", two=2, t=64)
        sD = [slab(14352 + 1024 * i, 1024) for i in range(2)]
        sE = [slab(16400 + 1024 * i, 1024) for i in range(3)]
        scb = slab(19472, 2048).rearrange("p (b s t) -> p b s t", b=2, t=T)
        kvr = slab(21520, 1536, T)
        qn = slab(23056, 1024, T)
        kx = slab(24080, 2048).rearrange("p (b g h t) -> p b g h t", b=2, g=2, h=2)
        vtok = slab(26128, 512).rearrange("p (b s c) -> p b s c", b=2, s=2)
        blk = slab(26640, 960).rearrange("p (k i g c) -> p k i g c", k=2, i=16, g=2)
        s4 = lambda a: a.rearrange("p (i t) -> p i t", t=T)
        g16 = lambda a: a.rearrange("p (g t) -> p g t", t=64)
        sig, cs, dW, aa = sA
        gl, kk, tmp, bonus = sB
        Bd, Cd = sD
        Zr, Zk, Zv, Zl = [slab(4112 + 1024 * i, 1024) for i in range(4)]
        M1, L2, M2, Nm = Zl, sE[0], sE[1], sE[2]
        seg = sE[0]
        Lm, Xm, Zm, P1 = sA
        Vt, Bt, Ct, Yc = kk, tmp, Zr, Zk
        X0, U, S0 = [sD[0][:, 256 * i:256 * i + 256] for i in range(3)]
        scr = sD[1]
        WC = small[:, 0:16]
        gtok = small[:, 32:80].rearrange("p (s c) -> p s c", s=2)
        hidK = small[:, 80:140].rearrange("p (k c) -> p k c", k=2)
        kc0, kcr, krt = small[:, 140:170], small[:, 170:200], small[:, 200:230]
        kcx = small[:, 230:290].rearrange("p (g h c) -> p g h c", g=2, h=2)
        cmx, csum = small[:, 290:306], small[:, 306:322]
        umax, unb, usum, uscl = [small[:, 338 + 4 * i:342 + 4 * i] for i in range(4)]
        mmax, mnb, msum = [small[:, 354 + 2 * i:356 + 2 * i] for i in range(3)]
        esc = slab(0, 240, 15)
        pcs = slab(256, 512, 32)
        pcT = scr[0:64, :].rearrange("p (q t) -> p q t", q=4)
        pu = slab(19472, 768)
        pT = slab(20240, 768)
        rqk = slab(2048, 2048, T)
        rv = slab(4112, 2048).rearrange("p (s c) -> p s c", s=2)
        rg = slab(6160, 2048, T)
        rt1, rt2 = slab(8208, 2048, T), slab(10256, 2048, T)
        sT = slab(12304, 1536).rearrange("p (h c) -> p h c", h=4)
        oc, osq = slab(13840, 2048, T), slab(15888, 2048, T)
        rstd4 = slab(17936, 1024, T)
        msq = slab(12304, 4096, T)
        memK, memn = slab(18960, 4096, T), slab(23056, 4096, T)
        merged = slab(0, 4096, T)
        gts = slab(4096, 2048).rearrange("p (b k t) -> p b k t", b=2, k=4)
        mtmp = slab(6144, 1024, T)
        yT, res = slab(7168, 4096, T), slab(11264, 4096, T)
        ysq = obr[:, 0:16, :]
        memV = slab(0, 4096).rearrange("p (s c) -> p s c", s=2)
        qT = slab(23056, 4096, T)
        pm = slab(4096, 512).rearrange("p (s t) -> p s t", s=2)
        pmT = slab(4608, 1024).rearrange("p (b s t) -> p b s t", b=2, s=2)
        gT = slab(15872, 11264, T)
        ub = slab(0, 1024).rearrange("p (b s t) -> p b s t", b=2, s=2)

        def bc(ap, n):
            return ap.unsqueeze(1).to_broadcast([ap.shape[0], n, ap.shape[1]])

        def bl(ap, n):
            return ap.unsqueeze(2).to_broadcast([ap.shape[0], ap.shape[1], n])

        def ready(n):
            return sem(f"chunk_loaded{n % NSLOT}"), 16 * (n // NSLOT + 1)

        for name in ([f"chunk_loaded{i}" for i in range(4)] + ["chunk_used", "chunk_out"]):
            sem(name)

        block = ctx.enter_context(nc.Block())

        @block.sync
        def _(sp):
            used, loaded = sem("chunk_used"), [sem(f"chunk_loaded{i}") for i in range(NSLOT)]
            sp.dma_start(xT, A["xT"]).then_inc(sem("x_loaded"), 16)
            sp.dma_start(posi[:, :], A["positions"].to_broadcast([P, T])).then_inc(sem("pos_loaded"), 16)
            flat = ring[:, :, :, :].rearrange("p s k c -> p s (k c)")
            for n, (what, i) in enumerate(MIX):
                if n >= NSLOT:
                    sp.wait_ge(used, n - NSLOT + 1)
                if n == AT[("kv", 0)]:
                    sp.wait_ge(sem("rw_g_mm"), 1)
                    sp.dma_start(decay.rearrange("p h c -> p (h c)"), decay_dram).then_inc(sem("decay_loaded"), 16)
                s = n % NSLOT
                src = {"rw": "w_rw", "zw": "w_zwa", "za": "w_zwa", "sc": "w_sc", "kv": "w_kv", "cmp": "w_cmp1",
                       "q": "w_nq", "gate": "w_ngate", "rq": "w_rq", "rk": "w_rk", "rv": "w_rv", "rg": "w_rg",
                       "mk": "w_mk"}[what]
                j = {"zw": 0, "za": 1}.get(what, i)
                w = A[src][j]
                sp.dma_start(flat[:, s, 0:w.shape[1]], w).then_inc(loaded[s], 16)

            def loop(base, count, per, sources):
                with sp.Fori(0, count) as i:
                    for j in range(per):
                        s = (base + j) % NSLOT
                        sp.wait_ge(used, i * per + (base + j - NSLOT + 1))
                        w = sources[j](i)
                        sp.dma_start(flat[:, s, 0:w.shape[1]], w).then_inc(loaded[s], 16)

            loop(N_MERGE, 8, 12, [
                (lambda i, t=t, j=j: A[f"w_g{j}"][i * 2 + t] if j < 4 else A[["w_brab", "w_brcd"][j - 4]][i * 2 + t])
                for t in range(2) for j in range(6)])
            sp.wait_ge(sem("branches"), 4)
            sp.dma_start(res, A["xT"]).then_inc(sem("x_loaded"), 16)
            loop(N_WOUT, 4, 4, [(lambda i, j=j: A["w_out"][i * 4 + j]) for j in range(4)])
            loop(N_MV, 4, 4, [(lambda i, j=j: A["w_mv"][i * 4 + j]) for j in range(4)])
            loop(N_WQ, 4, 4, [(lambda i, j=j: A["w_q"][i * 4 + j]) for j in range(4)])
            loop(N_WO, 4, 4, [(lambda i, j=j: A["w_o"][i * 4 + j]) for j in range(4)])
            loop(N_UP, 22, 4, [(lambda i, j=j: A["w_up"][i * 4 + j]) for j in range(4)])
            loop(N_DOWN, 16, 4, [(lambda i, j=j: A["w_dn"][i * 4 + j]) for j in range(4)])
            for q in range(4):
                sp.wait_ge(sem("res_ready"), 8 + q + 1)
                sp.dma_start(out[:, 4 * q:4 * q + 4, :], res[:, 4 * q:4 * q + 4, :]).then_inc(sem("stored"), 16)
            sp.wait_ge(sem("stored"), 64)

        @block.tensor
        def _(pe):
            used, outd = sem("chunk_used"), sem("chunk_out")

            def take(n):
                pe.wait_ge(*ready(n))
                if n >= 2:
                    pe.wait_ge(outd, n - 1)

            def project(n, rhs=None, M=P, rhs_n=T):
                take(n)
                x = hT if rhs is None else rhs
                w = ring[:, n % NSLOT, :, :].rearrange("p k c -> p (k c)")
                for k in range(KT):
                    mm = pe.matmul(big[0:M, n % 2, 0:rhs_n], w[:, k * M:(k + 1) * M], x[:, k, :],
                                   start=k == 0, stop=k == KT - 1)
                mm.then_inc(used, 1)

            def project_tokens(n, x, dst):
                for s in range(2):
                    for k in range(KT):
                        mm = pe.matmul(dst[:, s * P:(s + 1) * P], x[:, k, s * P:(s + 1) * P],
                                       ring[:, n % NSLOT, k, :], start=k == 0, stop=k == KT - 1)
                mm.then_inc(used, 1)

            def sumsq(src, need, first, done):
                for k in range(KT):
                    if k % 4 == 0:
                        pe.wait_ge(sem(need), first + k // 4)
                    mm = pe.matmul(sm[:, 5, 0:T], cc("ones128"), src[:, k, :], start=k == 0, stop=k == KT - 1)
                mm.then_inc(sem(done), 1)

            def per_head(fn):
                for h in range(2):
                    for g in range(16):
                        mm = fn(slice(64 * h, 64 * h + 64), g)
                return mm

            def b64(base, g, w=64):
                per = 512 // w
                return base + g // per, g % per * w

            def small_mm(base, rows, g, lhsT, rhs, w=64, start=True, stop=True):
                b, c = b64(base, g, w)
                return pe.matmul(sm[rows, b, c:c + w], lhsT, rhs, start=start, stop=stop)

            G = {k: g16(v) for k, v in dict(B=Bd, C=Cd, N=Nm, L=Lm, X=Xm, Z=Zm, P1=P1, V=Vt, Bt=Bt, Ct=Ct,
                                             M1=M1, M2=M2, L2=L2, Vc=Zv).items()}
            eye = lambda r: cst[r, const_at["ident"][0] + r.start:const_at["ident"][0] + r.stop]
            lv = sem("rw_level")

            def rw_lora():
                pe.wait_ge(sem("rw_lora_in"), 1)
                for i in range(4):
                    pe.matmul(sm[:, i // 2, i % 2 * T:i % 2 * T + T], lora[0:96, 0, i * P:(i + 1) * P],
                              Z[0:96, 12, :], start=True, stop=True)
                for i in range(4):
                    mm = pe.matmul(sm[:, 2 + i // 2, i % 2 * T:i % 2 * T + T], lora[0:96, 1, i * P:(i + 1) * P],
                                   Z[0:96, 13, :], start=True, stop=True)
                mm.then_inc(sem("rw_lora_mm"), 1)

            def rw_g():
                pe.wait_ge(sem("rw_sigmoids"), 1)
                pe.wait_ge(sem("rw_kk_sq"), 1)
                for i in range(4):
                    for k in range(2):
                        mm = pe.matmul(sm[:, i // 2, i % 2 * T:i % 2 * T + T], lora[:, 2 + k, i * P:(i + 1) * P],
                                       Z[:, 14 + k, :], start=k == 0, stop=k == 1)
                mm.then_inc(sem("rw_g_mm"), 1)
                for j in range(2):
                    mm = pe.matmul(sm[:, 2 + j, :], cc("ones64"), tmp[:, j * 512:(j + 1) * 512], start=True, stop=True)
                mm.then_inc(sem("rw_kk_mm"), 1)

            def rw_bonus():
                pe.wait_ge(sem("rw_g_out"), 1)
                pe.wait_ge(sem("rw_rk"), 1)
                for j in range(2):
                    mm = pe.matmul(sm[:, j, :], cc("ones64"), Zr[:, j * 512:(j + 1) * 512], start=True, stop=True)
                mm.then_inc(sem("rw_bonus_mm"), 1)

            def rw_s1():
                pe.wait_ge(sem("rw_operands"), 1)
                pe.wait_ge(sem("rw_bonus_out"), 1)
                per_head(lambda r, g: small_mm(0, r, g, G["B"][r, g], QR[r, g, :, :], w=128)) \
                    .then_inc(sem("rw_s1_mm"), 1)

            def rw_s2():
                pe.wait_ge(sem("rw_s1_out"), 1)
                per_head(lambda r, g: small_mm(0, r, g, G["C"][r, g], QR[r, g, :, :], w=128)) \
                    .then_inc(sem("rw_s2_mm"), 1)

            def rw_s3():
                pe.wait_ge(sem("rw_s2_out"), 1)
                per_head(lambda r, g: small_mm(0, r, g, QR[r, g, 0, :], G["B"][r, g])).then_inc(sem("rw_s3_mm"), 1)
                per_head(lambda r, g: small_mm(2, r, g, G["Vc"][r, g], eye(r))).then_inc(sem("rw_s3_mm"), 1)

            def rw_s4():
                pe.wait_ge(sem("rw_l_out"), 1)
                pe.wait_ge(sem("rw_v_out"), 1)
                per_head(lambda r, g: small_mm(0, r, g, G["B"][r, g], eye(r))).then_inc(sem("rw_s4_mm"), 1)
                per_head(lambda r, g: small_mm(2, r, g, G["C"][r, g], eye(r))).then_inc(sem("rw_s4_mm"), 1)

            def rw_level(n):
                if n == 1:
                    pe.wait_ge(sem("rw_s4_out"), 2)
                pe.wait_ge(sem("rw_x_ready"), n)
                per_head(lambda r, g: small_mm(0, r, g, G["L"][r, g], G["X"][r, g])).then_inc(sem("rw_p1_mm"), 1)

            def rw_level2(n):
                pe.wait_ge(sem("rw_p1_out"), n)
                per_head(lambda r, g: small_mm(2, r, g, G["Z"][r, g], G["P1"][r, g])).then_inc(sem("rw_p2_mm"), 1)
                if n < 5:
                    per_head(lambda r, g: small_mm(0, r, g, G["P1"][r, g], G["Z"][r, g])) \
                        .then_inc(sem("rw_p2_mm"), 1)

            def four(base, off, fn):
                for h in range(2):
                    r = slice(64 * h, 64 * h + 64)
                    for i in range(4):
                        pairs = fn(r, i)
                        for q, (a, b) in enumerate(pairs):
                            mm = pe.matmul(sm[r, base + i // 2, off + i % 2 * 64:off + i % 2 * 64 + 64], a, b,
                                           start=q == 0, stop=q == len(pairs) - 1)
                return mm

            v4 = lambda a: a.rearrange("p (i t) -> p i t", t=64)
            X04, U4, S4 = v4(X0), v4(U), v4(S0)

            def rw_chunk_a(c):
                if c == 0:
                    pe.wait_ge(sem("rw_x_ready"), 6)
                else:
                    pe.wait_ge(sem("rw_state"), c)
                    pe.wait_ge(sem("rw_y_out"), c)
                four(0, 0, lambda r, i: ([(QR[r, 4 * i + c, 0, :], S4[r, i])] if c else [])
                     + [(G["L2"][r, 4 * i + c], G["V"][r, 4 * i + c])]).then_inc(sem("rw_rhs_mm"), 1)

            def rw_chunk_b(c):
                pe.wait_ge(sem("rw_rhs_out"), c + 1)
                four(2, 0, lambda r, i: [(G["X"][r, 4 * i + c], X04[r, i])]).then_inc(sem("rw_u_mm"), 1)

            def rw_chunk_c(c):
                pe.wait_ge(sem("rw_u_out"), c + 1)
                if c < NCH - 1:
                    four(2, 128, lambda r, i: [(G["Bt"][r, 4 * i + c], U4[r, i]),
                                               (G["Ct"][r, 4 * i + c], G["V"][r, 4 * i + c])]) \
                        .then_inc(sem("rw_ds_mm"), 1)
                four(0, 128, lambda r, i: ([(S4[r, i], QR[r, 4 * i + c, 1, :])] if c else [])
                     + [(U4[r, i], G["M1"][r, 4 * i + c]), (G["V"][r, 4 * i + c], G["M2"][r, 4 * i + c])]) \
                    .then_inc(sem("rw_y_mm"), 1)

            def rw_mean():
                pe.wait_ge(sem("rw_y_out"), NCH)
                for j in range(2):
                    mm = pe.matmul(sm[:, j, :], cc("ones64"), Yc[:, j * 512:(j + 1) * 512], start=True, stop=True)
                mm.then_inc(sem("rw_mean_mm"), 1)

            def rw_var():
                pe.wait_ge(sem("rw_ysq"), 1)
                for j in range(2):
                    mm = pe.matmul(sm[:, 2 + j, :], cc("ones64"), Xm[:, j * 512:(j + 1) * 512], start=True, stop=True)
                mm.then_inc(sem("rw_var_mm"), 1)

            def nsa_dup():
                pe.wait_ge(outd, AT[("kv", 1)] + 1)
                for kv in range(2):
                    for g in range(2):
                        mm = pe.matmul(sm[:, 4 + kv, g * T:(g + 1) * T], cc(f"dup{g}"), kvr[:, kv, :],
                                       start=True, stop=True)
                mm.then_inc(sem("nsa_dup_mm"), 1)

            def nsa_rot_k():
                pe.wait_ge(outd, AT[("kv", 5)] + 1)
                pe.wait_ge(sem("nsa_blk"), 2)
                pe.matmul(sm[:, 4, 0:T], cc("rot64"), kvr[:, 2, :], start=True, stop=True)
                mm = pe.matmul(sm[:, 4, T:2 * T], cc("rot64"), kvr[:, 4, :], start=True, stop=True)
                mm.then_inc(sem("nsa_rotk_mm"), 1)

            def nsa_dup_k():
                pe.wait_ge(sem("nsa_k_roped"), 1)
                for b in range(2):
                    for g in range(2):
                        mm = pe.matmul(sm[:, 4 + b, g * T:(g + 1) * T], cc(f"dup{g}"), kvr[:, 2 + 2 * b, :],
                                       start=True, stop=True)
                mm.then_inc(sem("nsa_dupk_mm"), 1)

            def nsa_vtok():
                pe.wait_ge(sem("nsa_kx"), 1)
                for b in range(2):
                    for s in range(2):
                        mm = pe.matmul(sm[:, 4, (2 * b + s) * P:(2 * b + s + 1) * P], kvr[:, 3 + 2 * b, s * P:(s + 1) * P],
                                       cc("ident"), start=True, stop=True)
                mm.then_inc(sem("nsa_vtok_mm"), 1)

            def nsa_cmp_hidden(i):
                kv, ht = divmod(i, 2)
                n = AT[("cmp", i)]
                take(n)
                if i == 0:
                    pe.wait_ge(sem("nsa_blk"), 2)
                for k in range(16):
                    mm = pe.matmul(big[:, n % 2, 0:30], ring[:, n % NSLOT, k, :],
                                   blk[:, kv, k].rearrange("p g c -> p (g c)"), start=k == 0, stop=k == 15)
                mm.then_inc(used, 1)

            def nsa_cmp_out():
                pe.wait_ge(outd, AT[("cmp", 3)] + 1)
                pe.wait_ge(sem("nsa_hidV"), 1)
                pe.wait_ge(sem("nsa_vtok"), 1)
                for k in range(2):
                    mm = pe.matmul(sm[:, 4, 0:30], cw2[:, 0, k, :], hidK[:, k, :], start=k == 0, stop=k == 1)
                mm.then_inc(sem("nsa_cmp_mm"), 1)
                for g in range(2):
                    for k in range(2):
                        mm = pe.matmul(sm[0:64, 5, g * 64:g * 64 + 64],
                                       hidV[:, k, g].rearrange("p h c -> p (h c)"), cw2[:, 1, k, 0:64],
                                       start=k == 0, stop=k == 1)
                mm.then_inc(sem("nsa_cmp_mm"), 1)

            def nsa_rot_kc():
                pe.wait_ge(sem("nsa_kc0"), 1)
                pe.matmul(sm[:, 4, 64:94], cc("rot64"), kc0, start=True, stop=True).then_inc(sem("nsa_rotkc_mm"), 1)

            def nsa_rot_q():
                pe.wait_ge(outd, AT[("q", 3)] + 1)
                pe.wait_ge(sem("nsa_kcx"), 1)
                pe.wait_ge(sem("nsa_vcx"), 1)
                for j in range(2):
                    mm = pe.matmul(sm[:, 4 + j, :], cc("rot64"), qn[:, 2 * j:2 * j + 2, :], start=True, stop=True)
                mm.then_inc(sem("nsa_rotq_mm"), 1)

            def nsa_cmp_scores():
                pe.wait_ge(sem("nsa_q_roped"), 1)
                pe.wait_ge(outd, AT[("gate", 0)] + 1)
                for s in range(2):
                    mm = pe.matmul(sm[:, 5, 256 + s * 24:256 + s * 24 + 24], gsig[0:24, s * P:(s + 1) * P],
                                   cc("ident")[0:24, 0:24], start=True, stop=True)
                for q in range(4):
                    for s in range(2):
                        mm = pe.matmul(sm[:, 4, (2 * q + s) * 30:(2 * q + s + 1) * 30], qn[:, q, s * P:(s + 1) * P],
                                       kcx[:, q // 2].rearrange("p h c -> p (h c)"), start=True, stop=True)
                mm.then_inc(sem("nsa_cmps_mm"), 1)

            def nsa_cmp_T():
                pe.wait_ge(sem("nsa_pcs"), 1)
                for q in range(4):
                    for s in range(2):
                        u = 4 * q + 2 * s
                        mm = pe.matmul(sm[0:64, 4 + q // 2, (q % 2) * T + s * P:(q % 2) * T + s * P + P],
                                       pcs[:, u:u + 2].rearrange("p h c -> p (h c)"), cc("ident"), start=True, stop=True)
                mm.then_inc(sem("nsa_cmpT_mm"), 1)

            def unit_scores(u):
                q, b = divmod(u, 2)
                if u:
                    pe.wait_ge(sem("nsa_p"), u)
                k = kx[:, b, q // 2]
                pe.matmul(sm[:, 0, 0:256], qn[:, q, 0:P], k[:, :, 0:P], start=True, stop=True)
                pe.matmul(sm[:, 1, :], qn[:, q, P:T], k, start=True, stop=True).then_inc(sem("nsa_s_mm"), 1)

            def unit_T(u):
                pe.wait_ge(sem("nsa_p_scaled"), u + 1)
                if u:
                    pe.wait_ge(sem("nsa_pT"), u)
                for h in range(2):
                    pe.matmul(sm[:, 2, h * T:h * T + P], pu[:, h * P:(h + 1) * P], cc("ident"), start=True, stop=True)
                    pe.matmul(sm[:, 2, h * T + P:h * T + T], pu[:, 256 + h * T:256 + h * T + P], cc("ident"),
                              start=True, stop=True)
                    mm = pe.matmul(sm[:, 3, h * P:(h + 1) * P], pu[:, 256 + h * T + P:256 + h * T + T], cc("ident"),
                                   start=True, stop=True)
                mm.then_inc(sem("nsa_T_mm"), 1)

            def unit_pv(u):
                q, b = divmod(u, 2)
                g = q // 2
                if b == 0:
                    if q == 0:
                        pe.wait_ge(sem("nsa_pcT"), 1)
                    if q >= 2:
                        pe.wait_ge(sem("nsa_o"), q - 1)
                pe.wait_ge(sem("nsa_pT"), u + 1)
                for h in range(2):
                    r = slice(64 * h, 64 * h + 64)
                    pe.matmul(sm[r, 4 + q % 2, 0:T], vtok[:, b, 0, 64 * g:64 * g + 64], pT[:, h * T:(h + 1) * T],
                              start=b == 0, stop=False, skip_group_check=True)
                    mm = pe.matmul(sm[r, 4 + q % 2, P:T], vtok[:, b, 1, 64 * g:64 * g + 64],
                                   pT[:, 512 + h * P:512 + (h + 1) * P], start=False, stop=False,
                                   skip_group_check=True)
                if b == 1:
                    mm = pe.matmul(sm[:, 4 + q % 2, 0:T], vcx[:, g, :], pcT[:, q, :], start=False, stop=True,
                                   skip_group_check=True)
                mm.then_inc(sem("nsa_pv_mm"), 1)

            def ret_rot():
                pe.wait_ge(sem("nsa_o"), 4)
                for j in range(4):
                    mm = pe.matmul(sm[:, j, :], cc("rot128"), rqk[:, 2 * j:2 * j + 2, :], start=True, stop=True)
                mm.then_inc(sem("ret_rot_mm"), 1)

            def ret_scores():
                pe.wait_ge(sem("ret_roped"), 1)
                for h in range(4):
                    pe.matmul(sm[:, h, 0:T], rqk[:, 4 + h, 0:P], rqk[:, h, :], start=True, stop=True)
                    mm = pe.matmul(sm[:, h, T:T + P], rqk[:, 4 + h, P:T], rqk[:, h, P:T], start=True, stop=True)
                mm.then_inc(sem("ret_s_mm"), 1)

            def ret_out():
                pe.wait_ge(sem("ret_sT"), 4)
                for i in range(8):
                    h = i // 2
                    d = sm[:, i // 2, i % 2 * T:i % 2 * T + T]
                    pe.matmul(d[:, 0:P], rv[:, 0, i * P:(i + 1) * P], sT[:, h, 0:P], start=True, stop=True)
                    pe.matmul(d[:, P:], rv[:, 0, i * P:(i + 1) * P], sT[:, h, P:T], start=True, stop=False)
                    mm = pe.matmul(d[:, P:T], rv[:, 1, i * P:(i + 1) * P], sT[:, h, T:T + P], start=False, stop=True)
                mm.then_inc(sem("ret_o_mm"), 1)

            def ret_sum(src, need, val, name):
                pe.wait_ge(sem(need), val)
                for h in range(4):
                    for j in range(2):
                        mm = pe.matmul(sm[:, 4 + h // 2, h % 2 * T:h % 2 * T + T], cc("ones128"), src[:, 2 * h + j, :],
                                       start=j == 0, stop=j == 1)
                mm.then_inc(sem(name), 1)

            pe.wait_ge(sem("consts_loaded"), 16 * 5)
            sumsq(sq0, "x_sq", 1, "norm_mm")
            pe.wait_ge(sem("h_ready"), 1)
            steps = {
                ("sc", 0): [rw_lora], ("sc", 1): [rw_g], ("sc", 3): [rw_bonus, rw_s1],
                ("sc", 4): [rw_s2], ("sc", 5): [rw_s3], ("sc", 6): [rw_s4],
                ("sc", 7): [lambda: rw_level(1)], ("sc", 8): [lambda: rw_level2(1)],
                ("sc", 9): [lambda: rw_level(2)], ("sc", 10): [lambda: rw_level2(2)],
                ("sc", 11): [lambda: rw_level(3)], ("kv", 0): [lambda: rw_level2(3)],
                ("kv", 1): [lambda: rw_level(4)], ("kv", 2): [lambda: rw_level2(4), nsa_dup],
                ("kv", 3): [lambda: rw_level(5)], ("kv", 4): [lambda: rw_level2(5)],
                ("kv", 5): [lambda: rw_chunk_a(0)],
                ("cmp", 0): [nsa_rot_k, lambda: rw_chunk_b(0)], ("cmp", 1): [lambda: rw_chunk_c(0)],
                ("cmp", 2): [nsa_dup_k, lambda: rw_chunk_a(1)], ("cmp", 3): [lambda: rw_chunk_b(1)],
                ("q", 0): [lambda: rw_chunk_c(1), nsa_vtok], ("q", 1): [lambda: rw_chunk_a(2)],
                ("q", 2): [lambda: rw_chunk_b(2), nsa_cmp_out], ("q", 3): [lambda: rw_chunk_c(2), nsa_rot_kc],
                ("gate", 0): [lambda: rw_chunk_a(3), nsa_rot_q],
                ("rq", 0): [lambda: rw_chunk_b(3), nsa_cmp_scores], ("rq", 1): [lambda: rw_chunk_c(3)],
                ("rq", 2): [rw_mean, nsa_cmp_T], ("rq", 3): [rw_var],
                ("mk", 0): [ret_rot], ("mk", 2): [ret_scores], ("mk", 4): [ret_out],
                ("mk", 6): [lambda: ret_sum(oc, "ret_o_out", 1, "ret_mean_mm")],
                ("mk", 9): [lambda: ret_sum(osq, "ret_sq", 1, "ret_var_mm")],
            }
            order = [c for c in MIX if c[0] in ("rk", "rv", "rg")]
            for u in range(8):
                steps.setdefault(order[2 * u + 1], []).append(lambda u=u: unit_scores(u))
                if u:
                    steps[order[2 * u + 1]].insert(0, lambda u=u: unit_pv(u - 1))
                steps.setdefault(order[2 * u + 2], []).append(lambda u=u: unit_T(u))
            steps.setdefault(order[18], []).append(lambda: unit_pv(7))
            for n, (what, i) in enumerate(MIX):
                for s in steps.get((what, i), []):
                    s()
                if what in ("zw", "za"):
                    project(n, M=96)
                elif what == "gate":
                    project(n, M=24)
                elif what == "cmp":
                    nsa_cmp_hidden(i)
                elif what == "rv":
                    take(n)
                    project_tokens(n, hT, big[:, n % 2, :])
                elif what == "mk":
                    if i == 0:
                        sumsq(msq, "mem_sq", 1, "norm_mm")
                        pe.wait_ge(sem("mem_n"), 1)
                    project(n, memn)
                else:
                    project(n)

            pe.wait_ge(sem("branches"), 4)
            pe.wait_ge(outd, NMIX)
            with pe.Fori(0, 8) as i:
                for t in range(2):
                    for j in range(6):
                        m = 6 * t + j
                        n0 = N_MERGE + m
                        slot = n0 % NSLOT
                        pe.wait_ge(sem(f"chunk_loaded{slot}"), i * 48 + 16 * (n0 // NSLOT + 1))
                        if j < 4:
                            pe.wait_ge(sem("gate_free"), i * 8 + 4 * t + j + 1)
                            for k in range(KT):
                                mm = pe.matmul(big[:, j % 2, :], ring[:, slot, k, :], hT[:, k, :],
                                               start=k == 0, stop=k == KT - 1)
                            mm.then_inc(used, 1)
                        else:
                            if j == 4:
                                pe.wait_ge(sem("branch_free"), i * 2 + t + 1)
                            ks = [(0, 4, 0), (4, 8, 1)] if j == 4 else [(0, 8, 2), (8, 12, 3)]
                            for a, z, b in ks:
                                for k in range(a, z):
                                    mm = pe.matmul(sm[:, 2 * t + b // 2, b % 2 * T:b % 2 * T + T],
                                                   ring[:, slot, k, :], obr[:, (0 if j == 4 else 8) + k, :],
                                                   start=k == a, stop=k == z - 1)
                            mm.then_inc(used, 1)

            def stream_loop(base, count, x, adj):
                with pe.Fori(0, count) as i:
                    for j in range(4):
                        slot = (base + j) % NSLOT
                        pe.wait_ge(sem(f"chunk_loaded{slot}"), i * 16 + 16 * ((base + j) // NSLOT + 1))
                        pe.wait_ge(outd, i * 4 + (base + j - 1 - adj))
                        for k in range(KT):
                            mm = pe.matmul(big[:, j % 2, :], ring[:, slot, k, :], x[:, k, :],
                                           start=k == 0, stop=k == KT - 1)
                        mm.then_inc(used, 1)

            def norms(step):
                pe.wait_ge(sem("y_sq"), 16 * (step + 1))
                for k in range(KT):
                    mm = pe.matmul(sm[:, 5, 0:T], cc("ones128"), ysq[:, k, :], start=k == 0, stop=k == KT - 1)
                mm.then_inc(sem("norm_mm"), 1)
                if step < 2:
                    sumsq(ysq, "res_sq", 4 * step + 1, "norm_mm")

            pe.wait_ge(sem("merged"), 16)
            pe.wait_ge(sem("gate_free"), 66)
            stream_loop(N_WOUT, 4, merged, 96)
            norms(0)
            with pe.Fori(0, 4) as i:
                for j in range(4):
                    slot = (N_MV + j) % NSLOT
                    pe.wait_ge(sem(f"chunk_loaded{slot}"), i * 16 + 16 * ((N_MV + j) // NSLOT + 1))
                    pe.wait_ge(outd, i * 4 + (N_MV + j - 1 - 96))
                    for s in range(2):
                        for k in range(KT):
                            mm = pe.matmul(big[:, j % 2, s * P:(s + 1) * P], memn[:, k, s * P:(s + 1) * P],
                                           ring[:, slot, k, :], start=k == 0, stop=k == KT - 1)
                    mm.then_inc(used, 1)
            pe.wait_ge(sem("h_ready"), 2)
            stream_loop(N_WQ, 4, hT, 96)
            pe.wait_ge(outd, N_WO - 96)
            for h in range(MEM_HEADS + 1):
                if h < MEM_HEADS:
                    if h >= 2:
                        pe.wait_ge(sem("ma_p"), h - 1)
                    for s in range(2):
                        for k in range(4):
                            mm = pe.matmul(sm[:, h % 2, s * T:(s + 1) * T], qT[:, 4 * h + k, s * P:(s + 1) * P],
                                           memK[:, 4 * h + k, :], start=k == 0, stop=k == 3)
                    mm.then_inc(sem("ma_s_mm"), 1)
                if h:
                    g = h - 1
                    pe.wait_ge(sem("ma_pn"), g + 1)
                    for m in range(2):
                        for s in range(2):
                            mm = pe.matmul(sm[:, 2, m * T + s * P:m * T + (s + 1) * P], pm[:, s, m * P:(m + 1) * P],
                                           cc("ident"), start=True, stop=True)
                    mm.then_inc(sem("ma_T_mm"), 1)
                    pe.wait_ge(sem("ma_pT"), g + 1)
                    if g:
                        pe.wait_ge(sem("ma_o"), g)
                    for k in range(4):
                        for m in range(2):
                            mm = pe.matmul(sm[:, 3 + k // 2, k % 2 * T:k % 2 * T + T],
                                           memV[:, m, (4 * g + k) * P:(4 * g + k + 1) * P], pmT[:, g % 2, m, :],
                                           start=m == 0, stop=m == 1)
                    mm.then_inc(sem("ma_o_mm"), 1)
            pe.wait_ge(sem("ma_o"), 4)
            stream_loop(N_WO, 4, hT, 96)
            norms(1)
            pe.wait_ge(sem("h_ready"), 3)
            stream_loop(N_UP, 22, hT, 96)
            pe.wait_ge(sem("ffn_buffer_free"), 2 + FT)
            with pe.Fori(0, 8) as i:
                for t in range(2):
                    pe.wait_ge(sem("down_free"), i * 2 + t + 1)
                    for j in range(4):
                        n0 = N_DOWN + 4 * t + j
                        slot = n0 % NSLOT
                        pe.wait_ge(sem(f"chunk_loaded{slot}"), i * 32 + 16 * (n0 // NSLOT + 1))
                        for k in range(11):
                            mm = pe.matmul(big[:, t, :], ring[:, slot, k, :], gT[:, 11 * j + k, :],
                                           start=j == 0 and k == 0, stop=j == 3 and k == 10)
                        mm.then_inc(used, 1)
            norms(2)

        @block.scalar
        def _(act):
            used, outd = sem("chunk_used"), sem("chunk_out")
            act.sem_inc(sem("gate_free"), 2)
            act.sem_inc(sem("down_free"), 2)
            act.sem_inc(sem("branch_free"), 2)
            act.sem_inc(sem("ffn_buffer_free"), 2)
            act.dma_start(cst[:, :], const_dram).then_inc(sem("consts_loaded"), 16)
            act.dma_start(vec[:, :], A["vec"]).then_inc(sem("consts_loaded"), 16)
            act.dma_start(lora[0:96, 0:2, :], A["lora_wa"]).then_inc(sem("consts_loaded"), 16)
            act.dma_start(lora[:, 2:4, :], A["lora_g"]).then_inc(sem("consts_loaded"), 16)
            act.dma_start(cw2[:, :, :, :], A["w_cmp2"]).then_inc(sem("consts_loaded"), 16)
            cp, idt = ACT.Copy, ACT.Identity

            def std(k):
                act.wait_ge(sem("norm_var"), k)
                act.activation(rstd[:, :], rstd[:, :], ACT.Sqrt).then_inc(sem("norm_std"), 1)

            act.wait_ge(sem("x_loaded"), 16)
            for q in range(4):
                act.activation(sq0[:, 4 * q:4 * q + 4, :], xT[:, 4 * q:4 * q + 4, :], ACT.Square) \
                   .then_inc(sem("x_sq"), 1)
            act.wait_ge(sem("trig_arg"), 1)
            act.activation(trig[:, :, :, :], trig[:, :, :, :], ACT.Sin).then_inc(sem("trig_ready"), 1)
            std(1)

            def chunk(n, dst, src=None, func=cp, **kw):
                act.wait_ge(used, n + 1)
                act.activation(dst, big[:, n % 2, :] if src is None else src, func, **kw).then_inc(outd, 1)

            def rw_lora_in():
                act.wait_ge(sem("rw_mixed"), 3)
                act.activation(Z[0:96, 12, :], Z[0:96, 12, :], ACT.Tanh).then_inc(sem("rw_lora_in"), 1)
                act.activation(Z[:, 14:16, :], Z[:, 14:16, :], ACT.Sigmoid).then_inc(sem("rw_zg"), 1)

            def rw_sigmoids():
                act.wait_ge(sem("rw_lora_mm"), 1)
                for i in range(4):
                    act.activation(s4(sig)[:, i, :], sm[:, i // 2, i % 2 * T:i % 2 * T + T], ACT.Sigmoid,
                                   bias=vv("rw_w0", i))
                for i in range(4):
                    mm = act.activation(s4(aa)[:, i, :], sm[:, 2 + i // 2, i % 2 * T:i % 2 * T + T], ACT.Sigmoid,
                                        bias=vv("rw_a0", i))
                mm.then_inc(sem("rw_sigmoids"), 1)

            def rw_exps():
                act.wait_ge(sem("rw_cum"), 2)
                act.activation(dW, cs, ACT.Exp, scale=-RW_DECAY)
                act.activation(sig, sig, ACT.Exp, scale=-RW_DECAY).then_inc(sem("rw_exps"), 1)
                act.wait_ge(sem("rw_exps"), 1)
                act.activation(cs, cs, ACT.Exp, scale=RW_DECAY).then_inc(sem("rw_exps"), 1)

            def rw_gout():
                act.wait_ge(sem("rw_g_mm"), 1)
                act.activation(gl, sm[:, 0:2, :].rearrange("p b t -> p (b t)"), cp).then_inc(sem("rw_g_out"), 1)
                act.wait_ge(sem("rw_kk_mm"), 1)
                act.activation(bonus, sm[:, 2:4, :].rearrange("p b t -> p (b t)"), ACT.Sqrt) \
                   .then_inc(sem("rw_kk_norm"), 1)

            def wide(b, w=64):
                return sm[:, b:b + 2, :].rearrange("p b (g t) -> p (b g) t", t=w)

            def rw_v_out():
                act.wait_ge(sem("rw_s3_mm"), 2)
                act.activation(g16(Vt), wide(2), cp).then_inc(sem("rw_v_out"), 1)

            def rw_c_out():
                act.wait_ge(sem("rw_s4_mm"), 2)
                act.activation(g16(Ct), wide(2), cp).then_inc(sem("rw_s4_out"), 1)

            def quad(base, off):
                return sm[:, base:base + 2, off:off + 128]

            q2 = lambda a: a.rearrange("p (b t) -> p b t", b=2)

            def rw_rhs_out(c):
                act.wait_ge(sem("rw_rhs_mm"), c + 1)
                act.activation(q2(X0), quad(0, 0), cp).then_inc(sem("rw_rhs_out"), 1)

            def rw_y_out(c):
                act.wait_ge(sem("rw_y_mm"), c + 1)
                for b in range(2):
                    mm = act.activation(g16(Yc).rearrange("p (i c) t -> p i c t", c=4)[:, 2 * b:2 * b + 2, c, :],
                                        sm[:, b, 128:256].rearrange("p (j t) -> p j t", t=64), cp)
                mm.then_inc(sem("rw_y_out"), 1)

            def rw_finish():
                act.wait_ge(sem("rw_yc"), 1)
                act.activation(Xm, Yc, ACT.Square).then_inc(sem("rw_ysq"), 1)

            def rw_finish2():
                act.wait_ge(sem("rw_var"), 1)
                act.activation(Nm, Nm, ACT.Sqrt).then_inc(sem("rw_std"), 1)

            def nsa_kx():
                act.wait_ge(sem("nsa_dupk_mm"), 1)
                act.wait_ge(sem("zeroed"), 1)
                for h in range(2):
                    r = slice(64 * h, 64 * h + 64)
                    for b in range(2):
                        mm = act.activation(kx[r, b, :, h, :], sm[r, 4 + b, :].rearrange("p (g t) -> p g t", g=2), cp)
                mm.then_inc(sem("nsa_kx"), 1)

            def nsa_vt():
                act.wait_ge(sem("nsa_vtok_mm"), 1)
                act.activation(vtok.rearrange("p b s c -> p (b s c)"), sm[:, 4, :], cp).then_inc(sem("nsa_vtok"), 1)

            def nsa_vcx():
                act.wait_ge(sem("nsa_cmp_mm"), 2)
                for h in range(2):
                    r = slice(32 * h, 32 * h + 32)
                    mm = act.activation(vcx[r, :, 64 * h:64 * h + 64],
                                        sm[r, 5, 0:128].rearrange("p (g t) -> p g t", g=2), cp)
                mm.then_inc(sem("nsa_vcx"), 1)

            def nsa_cmp_exp():
                act.wait_ge(sem("nsa_cmp_arg"), 1)
                act.activation(esc, esc, ACT.Exp, scale=NSA_SCALE).then_inc(sem("nsa_cmp_e"), 1)

            def nsa_pcT():
                act.wait_ge(sem("nsa_cmpT_mm"), 1)
                act.activation(pcT, sm[0:64, 4:6, :].rearrange("p b (q t) -> p (b q) t", t=T), cp) \
                   .then_inc(sem("nsa_pcT"), 1)

            def unit_exp(u):
                act.wait_ge(sem("nsa_max"), u + 1)
                if u:
                    act.wait_ge(sem("nsa_T_mm"), u)
                for h in range(2):
                    act.activation(pu[:, h * P:(h + 1) * P], sm[:, 0, h * P:(h + 1) * P], ACT.Exp,
                                   bias=unb[:, h:h + 1], scale=NSA_SCALE, accum_out=usum[:, h:h + 1])
                for h in range(2):
                    mm = act.activation(pu[:, 256 + h * T:256 + (h + 1) * T], sm[:, 1, h * T:(h + 1) * T], ACT.Exp,
                                        bias=unb[:, 2 + h:3 + h], scale=NSA_SCALE, accum_out=usum[:, 2 + h:3 + h])
                mm.then_inc(sem("nsa_p"), 1)

            def unit_pT(u):
                act.wait_ge(sem("nsa_T_mm"), u + 1)
                if u:
                    act.wait_ge(sem("nsa_pv_mm"), u)
                act.activation(pT[:, 0:512], sm[:, 2, :], cp)
                act.activation(pT[:, 512:768], sm[:, 3, 0:256], cp).then_inc(sem("nsa_pT"), 1)
                if u % 2 == 0 and u:
                    unit_o(u // 2 - 1)

            def unit_o(q):
                act.wait_ge(sem("nsa_pv_mm"), 2 * q + 2)
                act.activation(obr[:, 16 + q, :], sm[:, 4 + q % 2, 0:T], cp).then_inc(sem("nsa_o"), 1)
                if q == 3:
                    act.dma_start(memn, A["memT"]).then_inc(sem("mem_loaded"), 16)

            def ret_o():
                act.wait_ge(sem("ret_o_mm"), 1)
                act.activation(oc.rearrange("p i t -> p (i t)"), sm[:, 0:4, :].rearrange("p b t -> p (b t)"), cp) \
                   .then_inc(sem("ret_o_out"), 1)

            def ret_sq():
                act.wait_ge(sem("ret_xc"), 1)
                act.activation(osq, oc, ACT.Square).then_inc(sem("ret_sq"), 1)

            def ret_std():
                act.wait_ge(sem("ret_var"), 1)
                act.activation(rstd4, rstd4, ACT.Sqrt).then_inc(sem("ret_std"), 1)

            steps = {
                ("sc", 0): [rw_lora_in, rw_sigmoids], ("sc", 1): [rw_exps, rw_gout], 
                ("sc", 5): [rw_v_out], ("sc", 6): [rw_c_out],
                ("kv", 5): [lambda: rw_rhs_out(0)], ("cmp", 1): [lambda: rw_y_out(0)],
                ("cmp", 2): [nsa_kx, lambda: rw_rhs_out(1)], ("q", 0): [lambda: rw_y_out(1), nsa_vt],
                ("q", 1): [lambda: rw_rhs_out(2)], ("q", 2): [nsa_vcx], ("q", 3): [lambda: rw_y_out(2)],
                ("gate", 0): [lambda: rw_rhs_out(3)], ("rq", 0): [nsa_cmp_exp], ("rq", 1): [lambda: rw_y_out(3)],
                ("rq", 2): [rw_finish, nsa_pcT], ("rq", 3): [rw_finish2],
                ("mk", 4): [ret_o], ("mk", 7): [ret_sq], ("mk", 9): [ret_std],
            }
            order = [c for c in MIX if c[0] in ("rk", "rv", "rg")]
            for u in range(8):
                steps.setdefault(order[2 * u + 1], []).append(lambda u=u: unit_exp(u))
                steps.setdefault(order[2 * u + 2], []).append(lambda u=u: unit_pT(u))
            steps.setdefault(order[18], []).append(lambda: unit_o(3))
            for n, (what, i) in enumerate(MIX):
                for s in steps.get((what, i), []):
                    s()
                if what == "rw":
                    t = i if i < 12 else i + 2
                    if n == 0:
                        act.wait_ge(sem("h_ready"), 1)
                    chunk(n, zp[:, t, 1:257])
                elif what in ("zw", "za"):
                    chunk(n, zp[0:96, 12 + (what == "za"), 1:257], big[0:96, n % 2, :])
                elif what == "sc":
                    if i >= 6 and i % 3 == 0:
                        act.wait_ge(sem("sc_done"), i // 3 - 1)
                    chunk(n, scb[:, i // 3 % 2, i % 3, :])
                elif what == "kv":
                    chunk(n, kvr[:, i, :])
                elif what == "cmp":
                    act.wait_ge(used, n + 1)
                    kv, ht = divmod(i, 2)
                    if kv:
                        act.wait_ge(sem("zeroed"), 1)
                        src = big[:, n % 2, 0:30].rearrange("p (g c) -> p g c", g=2)
                        act.activation(hidV[:, ht, :, 0, 0:NCMP], src, ACT.Gelu_apprx_tanh).then_inc(outd, 1)
                    else:
                        act.activation(hidK[:, ht, :], big[:, n % 2, 0:30], ACT.Gelu_apprx_tanh).then_inc(outd, 1)
                elif what == "q":
                    chunk(n, qn[:, i, :])
                elif what == "gate":
                    chunk(n, gsig[0:24, :], big[0:24, n % 2, :], ACT.Sigmoid)
                elif what == "rq":
                    if i == 0:
                        act.wait_ge(sem("rw_x_ready"), 6)
                    chunk(n, rqk[:, i, :])
                elif what == "rk":
                    chunk(n, rqk[:, 4 + i, :])
                elif what == "rv":
                    if i == 0:
                        act.wait_ge(sem("rw_done"), 1)
                    chunk(n, rv[:, :, i * P:(i + 1) * P], big[:, n % 2, :].rearrange("p (s c) -> p s c", s=2))
                elif what == "rg":
                    chunk(n, rg[:, i, :], func=ACT.Silu)
                elif what == "mk":
                    if i == 0:
                        act.wait_ge(sem("mem_loaded"), 16)
                        for q in range(4):
                            act.activation(msq[:, 4 * q:4 * q + 4, :], memn[:, 4 * q:4 * q + 4, :], ACT.Square) \
                               .then_inc(sem("mem_sq"), 1)
                        std(2)
                    chunk(n, memK[:, i, :])

            act.wait_ge(sem("branches"), 4)
            with act.Fori(0, 8) as i:
                for t in range(2):
                    act.wait_ge(sem("branch_free"), i * 2 + t + 1)
                    for j in range(4):
                        act.wait_ge(used, i * 12 + (N_MERGE + 6 * t + j + 1))
                        act.activation(gts[:, t, j, :], big[:, j % 2, :], ACT.Sigmoid).then_inc(sem("gate_free"), 1)

            def y_loop(base, count, dst, square):
                with act.Fori(0, count) as i:
                    for j in range(4):
                        act.wait_ge(used, i * 4 + (base + j + 1))
                        if square:
                            act.activation(ysq[:, bass.ds(i * 4 + j, 1), :], big[:, j % 2:j % 2 + 1, :], ACT.Square) \
                               .then_inc(sem("y_sq"), 1)
                        act.activation(dst[:, bass.ds(i * 4 + j, 1), :], big[:, j % 2:j % 2 + 1, :], cp).then_inc(outd, 1)

            def norms(step):
                std(3 + 2 * step)
                if step < 2:
                    for q in range(4):
                        act.wait_ge(sem("res_ready"), 4 * step + q + 1)
                        act.activation(ysq[:, 4 * q:4 * q + 4, :], res[:, 4 * q:4 * q + 4, :], ACT.Square) \
                           .then_inc(sem("res_sq"), 1)
                    std(4 + 2 * step)

            y_loop(N_WOUT, 4, yT, True)
            norms(0)
            with act.Fori(0, 4) as i:
                for j in range(4):
                    act.wait_ge(used, i * 4 + (N_MV + j + 1))
                    act.activation(memV[:, :, bass.ds(i * 512 + j * P, P)],
                                   big[:, j % 2, :].rearrange("p (s c) -> p s c", s=2), cp).then_inc(outd, 1)
            y_loop(N_WQ, 4, qT, False)
            for h in range(MEM_HEADS + 1):
                if h < MEM_HEADS:
                    act.wait_ge(sem("ma_max"), h + 1)
                    if h:
                        act.wait_ge(sem("ma_T_mm"), h)
                    for s in range(2):
                        mm = act.activation(pm[:, s, :], sm[:, h % 2, s * T:(s + 1) * T], ACT.Exp,
                                            bias=mnb[:, s:s + 1], scale=MEM_DH ** -0.5, accum_out=msum[:, s:s + 1])
                    mm.then_inc(sem("ma_p"), 1)
                if h:
                    act.wait_ge(sem("ma_o_mm"), h)
                    act.activation(hT[:, 4 * h - 4:4 * h, :],
                                   sm[:, 3:5, :].rearrange("p b (k t) -> p (b k) t", t=T), cp).then_inc(sem("ma_o"), 1)
                if h < MEM_HEADS:
                    act.wait_ge(sem("ma_T_mm"), h + 1)
                    act.activation(pmT[:, h % 2].rearrange("p s t -> p (s t)"), sm[:, 2, :], cp) \
                       .then_inc(sem("ma_pT"), 1)
            y_loop(N_WO, 4, yT, True)
            norms(1)
            with act.Fori(0, 22) as i:
                for p in range(2):
                    act.wait_ge(sem("ffn_buffer_free"), i * 2 + p + 1)
                    for s in range(2):
                        j = 2 * p + s
                        act.wait_ge(used, i * 4 + (N_UP + j + 1))
                        act.activation(ub[:, p, s, :], big[:, j % 2, :], idt,
                                       bias=vec[:, bass.ds(i * 4 + (VEC_AT["ffn_conv_b"][0] + j), 1)],
                                       scale=vec[:, bass.ds(i * 4 + (VEC_AT["ffn_conv_w"][0] + 176 + j), 1)]) \
                           .then_inc(sem("ffn_last_tap"), 1)
                    act.wait_ge(outd, i * 4 + (N_UP - 96 + 2 * p + 1))
                    act.activation(ub[:, p, 0, :], ub[:, p, 0, :], ACT.Gelu_apprx_tanh).then_inc(sem("ffn_act"), 1)
            with act.Fori(0, 8) as i:
                for t in range(2):
                    act.wait_ge(used, i * 8 + (N_DOWN + 4 * t + 4))
                    act.activation(ysq[:, bass.ds(i * 2 + t, 1), :], big[:, t:t + 1, :], ACT.Square) \
                       .then_inc(sem("y_sq"), 1)
                    act.activation(yT[:, bass.ds(i * 2 + t, 1), :], big[:, t:t + 1, :], cp) \
                       .then_inc(sem("down_free"), 1)
            norms(2)

        @block.gpsimd
        def _(pool):
            count = [0]

            def link(ins):
                count[0] += 1
                ins.then_inc(sem("pool_step"), 1)
                pool.wait_ge(sem("pool_step"), count[0])

            for z in (kcx, hidV[:, :, :, :, :], vcx[:, :, :], kx):
                link(pool.memset(z, 0.0))
            pool.memset(seg, 1.0).then_inc(sem("zeroed"), 1)
            pool.wait_ge(sem("zeroed"), 1)
            link(pool.memset(g16(seg)[:, :, 0:1], 0.0))
            pool.wait_ge(sem("h_ready"), 1)
            pool.memset(zp[:, :, 0:1], 0.0).then_inc(sem("zeroed"), 1)
            pool.wait_ge(sem("zeroed"), 2)
            for a, b, rows, last in ((0, 8, P, ("rw", 7)), (8, 12, P, ("rw", 11)), (12, 14, 96, ("za", 0)),
                                     (14, 16, P, ("rw", 13))):
                pool.wait_ge(sem("chunk_out"), AT[last] + 1)
                pool.tensor_tensor(Z[0:rows, a:b, :], zp[0:rows, a:b, 0:256], zp[0:rows, a:b, 1:257], SUB) \
                    .then_inc(sem("rw_diff"), 1)
            pool.wait_ge(sem("rw_kk"), 1)
            pool.tensor_tensor(tmp, kk, kk, MUL).then_inc(sem("rw_kk_sq"), 1)

            def short_conv(i):
                b, c, x, t = [scb[:, i % 2, s, :] for s in range(4)]
                w = [vv("sc_conv", 4 * j + i) for j in range(3)]
                pool.wait_ge(sem("chunk_out"), AT[("sc", 3 * i + 2)] + 1)
                link(pool.tensor_tensor(c, c, x, MUL))
                link(pool.tensor_scalar(x, c, w[2], None, MUL))
                link(pool.tensor_scalar(t, c, w[1], None, MUL))
                link(pool.tensor_tensor(x[:, 1:], x[:, 1:], t[:, :T - 1], ADD))
                link(pool.tensor_scalar(t, c, w[0], None, MUL))
                link(pool.tensor_tensor(x[:, 2:], x[:, 2:], t[:, :T - 2], ADD))
                pool.tensor_tensor(obr[:, i, :], x, b, MUL).then_inc(sem("sc_done"), 1)

            for i in range(4):
                short_conv(i)
            pool.wait_ge(sem("sc_done"), 4)
            pool.sem_inc(sem("branches"), 1)
            pool.wait_ge(sem("chunk_out"), AT[("cmp", 3)] + 1)
            pool.tensor_copy(hidV[:, :, :, 1, :].rearrange("p k g c -> p (k g) c"),
                             hidV[:, :, :, 0, :].rearrange("p k g c -> p (k g) c")).then_inc(sem("nsa_hidV"), 1)
            pool.wait_ge(sem("rw_x_ready"), 6)
            pool.memset(pcs, 0.0).then_inc(sem("pcs_zeroed"), 1)
            pool.wait_ge(sem("chunk_out"), AT[("rk", 3)] + 1)
            pool.wait_ge(sem("rw_done"), 1)
            pool.tensor_tensor(rt1, rqk, bc(trig[:, 0, 0, :], 8), MUL).then_inc(sem("ret_cos"), 1)

        @block.vector
        def _(dve):
            count = [0]

            def link(ins):
                count[0] += 1
                ins.then_inc(sem("dve_step"), 1)
                dve.wait_ge(sem("dve_step"), count[0])

            def mark(ins, name, n):
                ins.then_inc(sem(name), 1)
                dve.wait_ge(sem(name), n)

            stt, tt, ts = dve.scalar_tensor_tensor, dve.tensor_tensor, dve.tensor_scalar

            dve.wait_ge(sem("pos_loaded"), 16)
            dve.wait_ge(sem("consts_loaded"), 16 * 5)
            link(dve.tensor_copy(posf[:, :], posi[:, :]))
            for a, name in enumerate(("inv_ret", "inv_nsa")):
                link(ts(trig[:, a], bc(posf[:, :], 2), cc(name), None, MUL))
            link(ts(kmul[:, :, 0], trig[:, :, 0], 1 / (2 * math.pi), 0.25, MUL, ADD))
            link(ts(kmul[:, :, 1], trig[:, :, 1], 1 / (2 * math.pi), None, MUL))
            link(ts(kmul, kmul, MAGIC, None, ADD))
            link(ts(kmul, kmul, MAGIC, None, SUB))
            link(ts(kmul[:, :, 0], kmul[:, :, 0], 0.25, None, SUB))
            tf = trig[:, :, :, :].rearrange("p a b t -> p (a b t)")
            kf = kmul.rearrange("p a b t -> p (a b t)")
            for c in TWO_PI:
                link(stt(tf, kf, -c, tf, MUL, ADD))
            mark(ts(tf, tf, 3.1415925, -3.1415925, MIN, MAX), "trig_arg", 1)

            def inv_std(k):
                dve.wait_ge(sem("norm_mm"), k)
                mark(ts(rstd[:, :], sm[:, 5, 0:T], 1.0 / D, EPS, MUL, ADD), "norm_var", k)
                dve.wait_ge(sem("norm_std"), k)
                link(dve.reciprocal(rstd[:, :], rstd[:, :]))

            def scaled(dst, src, name, done, n):
                for k in range(KT):
                    mm = stt(dst[:, k, :], src[:, k, :], vv(name, k), rstd[:, :], MUL, MUL)
                mark(mm, done, n)

            inv_std(1)
            scaled(hT, xT, "ln_mix_pre", "h_ready", 1)

            for m, (a, b, rows, n) in enumerate(((0, 8, P, 1), (8, 12, P, 2), (12, 14, 96, 3), (14, 16, P, 4))):
                dve.wait_ge(sem("rw_diff"), n)
                for i in range(a, b):
                    mm = stt(Z[0:rows, i, :], Z[0:rows, i, :], vv("rw_mu", i, rows=rows), zp[0:rows, i, 1:257], MUL, ADD)
                if m != 2:
                    mm.then_inc(sem("rw_mixed"), 1)
                if m == 0:
                    dve.wait_ge(sem("rw_mixed"), 1)
                    for i in range(4):
                        mm = ts(s4(kk)[:, i, :], s4(Zk)[:, i, :], vv("rw_k_k", i), None, MUL)
                    mark(mm, "rw_kk", 1)
            dve.wait_ge(sem("rw_mixed"), 3)
            dve.wait_ge(sem("rw_sigmoids"), 1)
            mark(dve.tensor_tensor_scan(cs, seg, sig, 0.0, MUL, ADD), "rw_cum", 1)
            mark(tt(sig, cs, sig, SUB), "rw_cum", 2)
            dve.wait_ge(sem("rw_kk_norm"), 1)
            link(ts(bonus, bonus, 1e-12, None, MAX))
            link(dve.reciprocal(bonus, bonus))
            link(tt(kk, kk, bonus, MUL))
            for i in range(4):
                mm = ts(s4(tmp)[:, i, :], s4(aa)[:, i, :], -1.0, vv("rw_k_a", i), ADD, MUL)
            link(mm)
            link(stt(Zk, tmp, 1.0, Zk, ADD, MUL))
            dve.wait_ge(sem("rw_exps"), 2)
            tt(QR[:, :, 0, :], g16(kk), g16(sig), MUL)
            link(tt(QR[:, :, 1, :], g16(Zr), g16(dW), MUL))
            for i in range(4):
                mm = stt(s4(Zr)[:, i, :], s4(Zr)[:, i, :], vv("rw_r_k", i), s4(Zk)[:, i, :], MUL, MUL)
            mark(mm, "rw_rk", 1)
            link(tt(kk, kk, aa, MUL))
            tt(Bd, kk, cs, MUL)
            tt(Cd, Zk, cs, MUL)
            mark(dve.tensor_copy(WC.unsqueeze(2), g16(dW)[:, :, 63:64]), "rw_operands", 1)
            dve.wait_ge(sem("rw_bonus_mm"), 1)
            mark(tt(bonus, sm[:, 0:2, :].rearrange("p b t -> p (b t)"), Zv, MUL), "rw_bonus_out", 1)

            def masked(dst, src, name):
                return tt(g16(dst), src, bc(cc(name), 16), MUL)

            def wide(b):
                return sm[:, b:b + 2, :].rearrange("p b (g t) -> p (b g) t", t=64)

            quarter = sm[:, 0:4, :].rearrange("p b (g two t) -> p (b g) two t", two=2, t=64)
            dve.wait_ge(sem("rw_s1_mm"), 1)
            stt(g16(M1), quarter[:, :, 1, :], -1.0, bc(cc("incl"), 16), MUL, MUL)
            mark(dve.tensor_copy(g16(Nm), quarter[:, :, 0, :]), "rw_s1_out", 1)
            link(masked(P1, g16(Nm), "up0"))
            tt(g16(Xm), bc(cc("eye64"), 16), g16(P1), SUB)
            dve.wait_ge(sem("rw_s2_mm"), 1)
            masked(L2, quarter[:, :, 0, :], "strict")
            mark(masked(M2, quarter[:, :, 1, :], "incl"), "rw_s2_out", 1)
            dve.wait_ge(sem("rw_s3_mm"), 1)
            mark(dve.tensor_copy(g16(Lm), wide(0)), "rw_l_out", 1)
            link(masked(Zm, g16(Lm), "low0"))
            mark(tt(g16(Zm), bc(cc("eye64"), 16), g16(Zm), SUB), "rw_x_ready", 1)
            dve.wait_ge(sem("rw_s4_mm"), 2)
            ts(g16(Bt), wide(0), -1.0, None, MUL).then_inc(sem("rw_s4_out"), 1)

            def level(n):
                dve.wait_ge(sem("rw_p1_mm"), n)
                masked(P1, wide(0), f"up{n}").then_inc(sem("rw_p1_out"), 1)
                dve.wait_ge(sem("rw_p2_mm"), 2 * n - 1)
                mm = tt(g16(Xm), g16(Xm), wide(2), SUB)
                if n < 5:
                    dve.wait_ge(sem("rw_p2_mm"), 2 * n)
                    mm = tt(g16(Zm), g16(Zm), wide(0), SUB)
                mark(mm, "rw_x_ready", n + 1)

            def nsa_blocks():
                dve.wait_ge(sem("nsa_dup_mm"), 1)
                for kv in range(2):
                    src = sm[:, 4 + kv, :].rearrange("p (g c l o) -> p g c l o", g=2, l=8, o=2)
                    for o in range(2):
                        r = slice(64 * o, 64 * o + 64)
                        for hi in range(2):
                            for g in range(2):
                                pos = vv("cmp_pos", 16 * kv + 8 * hi, 8)[r]
                                mm = tt(blk[r, kv, 8 * hi:8 * hi + 8, g, :],
                                        src[r, g, hi:hi + NCMP, :, o].rearrange("p c l -> p l c"),
                                        bl(pos, NCMP), ADD)
                    mm.then_inc(sem("nsa_blk"), 1)

            def u_out(c):
                dve.wait_ge(sem("rw_u_mm"), c + 1)
                dve.tensor_copy(q2(U), sm[:, 2:4, 0:128]).then_inc(sem("rw_u_out"), 1)

            q2 = lambda a: a.rearrange("p (b t) -> p b t", b=2)
            wc = WC.rearrange("p (i c) -> p i c", c=4)

            def state(c):
                dve.wait_ge(sem("rw_ds_mm"), c + 1)
                dve.wait_ge(sem("rw_y_mm"), c + 1)
                if c:
                    link(tt(q2(S0), q2(S0), sm[:, 2:4, 128:256], ADD))
                else:
                    link(dve.tensor_copy(q2(S0), sm[:, 2:4, 128:256]))
                s = S0.rearrange("p (i v) -> p i v", v=64)
                mark(tt(s, s, bl(wc[:, :, c], 64), MUL), "rw_state", c + 1)

            def rope_k():
                dve.wait_ge(sem("nsa_rotk_mm"), 1)
                t = scr[:, 0:512].rearrange("p (a t) -> p a t", t=T)
                tt(t, sm[:, 4, :].rearrange("p (a t) -> p a t", t=T), bc(trig[:, 1, 1, :], 2), MUL)
                k = kvr.rearrange("p (a b) t -> p a b t", b=2)[:, 1:3, 0, :]
                link(tt(k, k, bc(trig[:, 1, 0, :], 2), MUL))
                mark(tt(k, k, t, ADD), "nsa_k_roped", 1)

            def kc_out():
                dve.wait_ge(sem("nsa_cmp_mm"), 1)
                mark(dve.tensor_copy(kc0, sm[:, 4, 0:30]), "nsa_kc0", 1)

            def at_end(a):
                e = trig[:, 1, a, :].rearrange("p (c l) -> p c l", l=16)[:, 1:16, 15]
                return bc(e, 2)

            def kc_rope():
                dve.wait_ge(sem("nsa_rotkc_mm"), 1)
                two = lambda a: a.rearrange("p (g c) -> p g c", g=2)
                tt(two(krt), two(sm[:, 4, 64:94]), at_end(1), MUL)
                link(tt(two(kcr), two(kc0), at_end(0), MUL))
                link(tt(kcr, kcr, krt, ADD))
                dve.tensor_copy(kcx[0:64, :, 0, :], two(kcr)[0:64])
                dve.tensor_copy(kcx[64:128, :, 1, :], two(kcr)[64:128]).then_inc(sem("nsa_kcx"), 1)

            def rope_q():
                dve.wait_ge(sem("nsa_rotq_mm"), 1)
                t = s4(scr)
                tt(t, sm[:, 4:6, :].rearrange("p b (i t) -> p (b i) t", t=T), bc(trig[:, 1, 1, :], 4), MUL)
                link(tt(qn, qn, bc(trig[:, 1, 0, :], 4), MUL))
                mark(tt(qn, qn, t, ADD), "nsa_q_roped", 1)

            e5 = esc.rearrange("p (q s h) c -> p q s h c", q=4, s=2)

            def cmp_arg():
                dve.wait_ge(sem("nsa_cmps_mm"), 1)
                link(dve.tensor_copy(gtok.rearrange("p s c -> p (s c)"), sm[:, 5, 256:304]))
                src = sm[:, 4, 0:240].rearrange("p (q s h c) -> p q s h c", q=4, s=2, h=2)
                for s in range(2):
                    for h in range(2):
                        mm = tt(e5[:, :, s, h, :], src[:, :, s, h, :], bc(cc("cmp_neg")[:, 15 * s:15 * s + 15], 4), ADD)
                link(mm)
                link(dve.tensor_reduce(cmx, esc, AX.X, MAX))
                mark(tt(esc, esc, bl(cmx, 15), SUB), "nsa_cmp_arg", 1)

            def cmp_p():
                dve.wait_ge(sem("nsa_cmp_e"), 1)
                for s in range(2):
                    for h in range(2):
                        mm = tt(e5[:, :, s, h, :], e5[:, :, s, h, :], bc(cc("cmp_seen")[:, 15 * s:15 * s + 15], 4), MUL)
                link(mm)
                link(dve.tensor_reduce(csum, esc, AX.X, ADD))
                link(ts(csum, csum, 1e-30, None, MAX))
                link(dve.reciprocal(csum, csum))
                c4 = csum.rearrange("p (q s h) -> p q s h", q=4, s=2)
                g = gtok.rearrange("p s (q h b) -> p s q h b", h=2, b=3)
                for s in range(2):
                    mm = tt(c4[:, :, s, :], c4[:, :, s, :], g[:, s, :, :, 0], MUL)
                link(mm)
                dve.wait_ge(sem("pcs_zeroed"), 1)
                mark(tt(pcs[:, :, 0:15], esc, bl(csum, 15), MUL), "nsa_pcs", 1)

            def unit_max(u):
                dve.wait_ge(sem("nsa_s_mm"), u + 1)
                two = lambda a: a.rearrange("p (h t) -> p h t", h=2)
                t0, t1 = two(sm[:, 0, 0:256]), two(sm[:, 1, :])
                tt(t0, t0, bc(cc("causal"), 2), ADD)
                link(tt(t1[:, :, P:T], t1[:, :, P:T], bc(cc("causal"), 2), ADD))
                dve.tensor_reduce(umax[:, 0:2], t0, AX.X, MAX)
                link(dve.tensor_reduce(umax[:, 2:4], t1, AX.X, MAX))
                mark(ts(unb, umax, -NSA_SCALE, None, MUL), "nsa_max", u + 1)

            def unit_scale(u):
                q, b = divmod(u, 2)
                dve.wait_ge(sem("nsa_p"), u + 1)
                link(dve.reciprocal(uscl, usum))
                g = gtok.rearrange("p s (q h b) -> p s q h b", h=2, b=3)[:, :, q, :, b + 1]
                us = uscl.rearrange("p (s h) -> p s h", s=2)
                link(tt(us, us, g, MUL))
                p0 = pu[:, 0:256].rearrange("p (h t) -> p h t", h=2)
                p1 = pu[:, 256:768].rearrange("p (h t) -> p h t", h=2)
                tt(p0, p0, bl(uscl[:, 0:2], P), MUL)
                mark(tt(p1, p1, bl(uscl[:, 2:4], T), MUL), "nsa_p_scaled", u + 1)

            for n in range(1, 5):
                level(n)
            nsa_blocks()
            level(5)
            rope_k()
            u_out(0)
            state(0)
            u_out(1)
            state(1)
            u_out(2)
            kc_out()
            state(2)
            kc_rope()
            rope_q()
            u_out(3)
            cmp_arg()
            cmp_p()
            dve.wait_ge(sem("rw_mean_mm"), 1)
            flat2 = lambda b: sm[:, b:b + 2, :].rearrange("p b t -> p (b t)")
            mark(stt(Yc, flat2(0), -1.0 / 64, Yc, MUL, ADD), "rw_yc", 1)
            dve.wait_ge(sem("rw_var_mm"), 1)
            mark(ts(Nm, flat2(2), 1.0 / 64, 64e-5, MUL, ADD), "rw_var", 1)
            dve.wait_ge(sem("rw_std"), 1)
            link(dve.reciprocal(Nm, Nm))
            link(tt(Yc, Yc, Nm, MUL))
            for i in range(4):
                mm = ts(s4(Yc)[:, i, :], s4(Yc)[:, i, :], vv("rw_lnx_g", i), vv("rw_lnx_b", i), MUL, ADD)
            link(mm)
            link(tt(Yc, Yc, bonus, ADD))
            mark(tt(obr[:, 4:8, :], s4(Yc), s4(gl), MUL), "rw_done", 1)
            dve.sem_inc(sem("branches"), 1)
            for u in range(8):
                unit_max(u)
                unit_scale(u)
            inv_std(2)
            scaled(memn, memn, "ln_mem_kv", "mem_n", 1)
            dve.wait_ge(sem("ret_rot_mm"), 1)
            link(tt(rt2, sm[:, 0:4, :].rearrange("p b (i t) -> p (b i) t", t=T), bc(trig[:, 0, 1, :], 8), MUL))
            dve.wait_ge(sem("ret_cos"), 1)
            mark(tt(rqk, rt1, rt2, ADD), "ret_roped", 1)
            dve.wait_ge(sem("ret_s_mm"), 1)
            dve.wait_ge(sem("decay_loaded"), 16)
            for h in range(4):
                tt(sT[:, h, :], sm[:, h, 0:384], decay[:, h, :], MUL).then_inc(sem("ret_sT"), 1)
            dve.wait_ge(sem("ret_mean_mm"), 1)
            o2 = oc.rearrange("p (h j) t -> p h j t", j=2)
            four = sm[:, 4:6, :].rearrange("p b (i t) -> p (b i) t", t=T)
            for j in range(2):
                mm = stt(o2[:, :, j, :], four, -1.0 / 256, o2[:, :, j, :], MUL, ADD)
            mark(mm, "ret_xc", 1)
            dve.wait_ge(sem("ret_var_mm"), 1)
            mark(ts(rstd4, four, 1.0 / 256, 1e-5, MUL, ADD), "ret_var", 1)
            dve.wait_ge(sem("ret_std"), 1)
            link(dve.reciprocal(rstd4, rstd4))
            for j in range(2):
                mm = tt(o2[:, :, j, :], o2[:, :, j, :], rstd4, MUL)
            link(mm)
            mark(tt(obr[:, 8:16, :], oc, rg, MUL), "ret_done", 1)
            dve.wait_ge(sem("nsa_o"), 4)
            dve.sem_inc(sem("branches"), 2)

            with dve.Fori(0, 8) as i:
                for t in range(2):
                    dve.wait_ge(sem("chunk_used"), i * 12 + (N_MERGE + 6 * t + 6))
                    dve.wait_ge(sem("gate_free"), i * 8 + (4 * t + 6))
                    tt(mtmp, gts[:, t], sm[:, 2 * t:2 * t + 2, :].rearrange("p b (k t) -> p (b k) t", t=T), MUL) \
                        .then_inc(sem("branch_free"), 1)
                    dve.wait_ge(sem("branch_free"), i * 2 + (t + 3))
                    tt(mtmp[:, 0:2], mtmp[:, 0:2], mtmp[:, 2:4], ADD).then_inc(sem("merge_half"), 1)
                    dve.wait_ge(sem("merge_half"), i * 2 + (t + 1))
                    tt(merged[:, bass.ds(i * 2 + t, 1), :], mtmp[:, 0:1, :], mtmp[:, 1:2, :], ADD) \
                        .then_inc(sem("merged"), 1)
                    dve.wait_ge(sem("merged"), i * 2 + (t + 1))

            def norms(step, post, pre):
                inv_std(3 + 2 * step)
                if step == 0:
                    dve.wait_ge(sem("x_loaded"), 32)
                dve.wait_ge(sem("chunk_out"), [N_WOUT, N_WO, N_UP + 88 - 16][step] - 96 + 16)
                if step == 2:
                    dve.wait_ge(sem("down_free"), 18)
                for q in range(4):
                    for k in range(4 * q, 4 * q + 4):
                        mm = stt(yT[:, k, :], yT[:, k, :], vv(post, k), rstd[:, :], MUL, MUL)
                    link(mm)
                    mark(tt(res[:, 4 * q:4 * q + 4, :], res[:, 4 * q:4 * q + 4, :], yT[:, 4 * q:4 * q + 4, :], ADD),
                         "res_ready", 4 * step + q + 1)
                if step < 2:
                    inv_std(4 + 2 * step)
                    scaled(hT, res, pre, "h_ready", step + 2)

            norms(0, "ln_mix_post", "ln_mem_q")
            for h in range(MEM_HEADS):
                dve.wait_ge(sem("ma_s_mm"), h + 1)
                if h:
                    dve.wait_ge(sem("ma_p"), h)
                link(dve.tensor_reduce(mmax, sm[:, h % 2, :].rearrange("p (s t) -> p s t", s=2), AX.X, MAX))
                mark(ts(mnb, mmax, -MEM_DH ** -0.5, None, MUL), "ma_max", h + 1)
                dve.wait_ge(sem("ma_p"), h + 1)
                link(dve.reciprocal(msum, msum))
                mark(tt(pm, pm, bl(msum, T), MUL), "ma_pn", h + 1)
            norms(1, "ln_mem_post", "ln_ffn_pre")
            w0, w1 = VEC_AT["ffn_conv_w"][0], VEC_AT["ffn_conv_w"][0] + 88
            with dve.Fori(0, 22) as i:
                for p in range(2):
                    for s in range(2):
                        j = 2 * p + s
                        u = ub[:, p, s, :]
                        dve.wait_ge(sem("ffn_last_tap"), i * 4 + (j + 1))
                        stt(u[:, 1:T], big[:, j % 2, 0:T - 1], vec[:, bass.ds(i * 4 + (w1 + j), 1)], u[:, 1:T], MUL, ADD) \
                            .then_inc(sem("ffn_mid_tap"), 1)
                        dve.wait_ge(sem("ffn_mid_tap"), i * 4 + (j + 1))
                        stt(u[:, 2:T], big[:, j % 2, 0:T - 2], vec[:, bass.ds(i * 4 + (w0 + j), 1)], u[:, 2:T], MUL, ADD) \
                            .then_inc(sem("chunk_out"), 1)
                    dve.wait_ge(sem("chunk_out"), i * 4 + (N_UP - 96 + 2 * p + 2))
                    dve.wait_ge(sem("ffn_act"), i * 2 + (p + 1))
                    tt(gT[:, bass.ds(i * 2 + p, 1), :], ub[:, p, 0:1, :], ub[:, p, 1:2, :], MUL) \
                        .then_inc(sem("ffn_buffer_free"), 1)
            norms(2, "ln_ffn_post", None)


def tiles(w, m=P):
    k = w.shape[0] // P
    return w.reshape(k, P, w.shape[1] // m, m).transpose(2, 1, 0, 3).reshape(w.shape[1] // m, P, k * m)


def columns(v):
    return v.reshape(-1, P).T


def layout(x):
    z = lambda n: np.zeros(n, np.float32)
    w_in = x["w_in"][0]
    RW, RET, NSA, GATE = 1536, 3520, 6592, 7896
    a = {}
    a["xT"] = x["x"][0].T.reshape(KT, P, T).transpose(1, 0, 2)
    a["memT"] = x["mem"][0].T.reshape(KT, P, T).transpose(1, 0, 2)
    a["positions"] = x["positions"]
    a["w_rw"] = np.concatenate([tiles(w_in[:, RW:RW + 1536]), tiles(w_in[:, RW + 1728:RW + 1984])])
    a["w_zwa"] = tiles(w_in[:, RW + 1536:RW + 1728], 96)
    sc = tiles(w_in[:, :1536])
    a["w_sc"] = sc.reshape(3, 4, P, -1).transpose(1, 0, 2, 3).reshape(12, P, -1)
    a["w_nq"] = tiles(w_in[:, NSA:NSA + 512])
    a["w_kv"] = tiles(w_in[:, NSA + 512:NSA + 1280])
    a["w_ngate"] = tiles(w_in[:, NSA + 1280:NSA + 1304], 24)
    a["w_rq"] = tiles(w_in[:, RET:RET + 512])
    a["w_rk"] = tiles(w_in[:, RET + 512:RET + 1024])
    a["w_rv"] = tiles(w_in[:, RET + 1024:RET + 2048])
    a["w_rg"] = tiles(w_in[:, RET + 2048:RET + 3072])
    for j in range(4):
        a[f"w_g{j}"] = tiles(w_in[:, GATE + j * D:GATE + (j + 1) * D])
    a["w_brab"] = tiles(x["w_branch"][0][:1024])
    a["w_brcd"] = tiles(x["w_branch"][0][1024:])
    a["w_cmp1"] = np.concatenate([tiles(x["nsa_cmp_w1"][0, k]) for k in range(2)])
    w2 = x["nsa_cmp_w2"][0].reshape(2, 2, P, 64).transpose(2, 0, 1, 3)
    a["w_cmp2"] = np.concatenate([w2, w2], -1)
    a["lora_wa"] = np.stack([x["rw_w2"][0], x["rw_a2"][0]], 1)
    a["lora_g"] = x["rw_g2"][0].reshape(2, P, 512).transpose(1, 0, 2)
    a["w_out"], a["w_q"], a["w_o"] = [tiles(x[k][0]) for k in ("w_out", "mem_wq", "mem_wo")]
    a["w_mk"], a["w_mv"] = tiles(x["mem_wkv"][0][:, :D]), tiles(x["mem_wkv"][0][:, D:])
    up = tiles(x["ffn_w_up"][0])
    a["w_up"] = up.reshape(2, FT, P, -1).transpose(1, 0, 2, 3).reshape(2 * FT, P, -1)
    a["w_dn"] = tiles(x["ffn_w_down"][0]).reshape(KT, P, 4, 11 * P).transpose(0, 2, 1, 3).reshape(4 * KT, P, 11 * P)
    mu = x["rw_mu"][0]
    parts = {k: columns(x[k][0]) for k in ("ln_mix_pre", "ln_mix_post", "ln_mem_q", "ln_mem_kv", "ln_mem_post",
                                           "ln_ffn_pre", "ln_ffn_post", "rw_w0", "rw_a0", "rw_k_k", "rw_k_a",
                                           "rw_r_k", "rw_lnx_g", "rw_lnx_b", "sc_conv")}
    parts["rw_mu"] = columns(np.concatenate([mu[:1632], z(32), mu[1632:1728], z(32), mu[1728:]]))
    parts["cmp_pos"] = x["nsa_cmp_pos"][0].reshape(2, 16, P).transpose(2, 0, 1).reshape(P, 32)
    pair = lambda v: v.reshape(-1, 2, FT, P).transpose(3, 0, 2, 1).reshape(P, -1)
    parts["ffn_conv_w"] = pair(x["ffn_conv_w"][0])
    parts["ffn_conv_b"] = pair(x["ffn_conv_b"][0])
    a["vec"] = np.concatenate([parts[n] for n, _ in VEC], 1)
    return {k: np.ascontiguousarray(v) for k, v in a.items()}


def kernel(**inputs):
    import concourse.bacc as bacc
    from concourse.bass_utils import run_bass_kernel_spmd

    arrays = layout({k: np.asarray(v) for k, v in inputs.items()})
    consts, const_at = build_constants()
    arrays["constants"] = consts
    arrays["decay"] = decay_table()
    nc = bacc.Bacc("TRN2", target_bir_lowering=False, num_devices=1)
    A = {k: nc.dram_tensor("in_" + k, v.shape, mybir.dt.from_np(v.dtype), kind="ExternalInput").ap()
         for k, v in arrays.items()}
    out = nc.dram_tensor("out", (P, KT, T), mybir.dt.float32, kind="ExternalOutput").ap()
    program(nc, A, A["constants"], A["decay"], const_at, out)
    r = run_bass_kernel_spmd(nc, [{"in_" + k: v for k, v in arrays.items()}], core_ids=[0])
    y = r.results[0]["out"]
    return np.ascontiguousarray(y.transpose(2, 1, 0).reshape(1, T, D))
```

```python
import math
from contextlib import ExitStack

import numpy as np
import concourse.bass as bass
from concourse import mybir

D = 2048
T = 256
P = 128
KT = D // P
MEM_HEADS, MEM_DH = 4, 512
RW_TILES, RW_CH = 4, 64
NCH = T // RW_CH
RW_DECAY = math.exp(-0.5)
RET_HEADS = 4
NSA_SCALE = 64 ** -0.5
NCMP = (T - 32) // 16 + 1
FFN = 5632
FT = FFN // P
EPS = 1e-6
NSLOT = 4
REGION = 49872
NEG = -1e30
MAGIC = 1.5 * 2.0 ** 23
TWO_PI = (6.28125, 0.0019340515136718750, 1.2556659146e-6)



def constant_columns():
    p = np.arange(P)
    i = np.arange(P)[None, :]
    cols = {}
    cols["ident"] = np.eye(P)
    rot = np.zeros((P, P))
    for m in range(P):
        rot[(m + 64) % P, m] = -1.0 if m < 64 else 1.0
    cols["rot128"] = rot
    rot = np.zeros((P, P))
    for m in range(P):
        b, r = m // 64 * 64, m % 64
        rot[b + (r + 32) % 64, m] = -1.0 if r < 32 else 1.0
    cols["rot64"] = rot
    cols["ones64"] = (p[:, None] // 64 == i // 64).astype(float)
    cols["ones128"] = np.ones((P, P))
    for g in range(2):
        cols[f"dup{g}"] = (p[:, None] == 64 * g + i % 64).astype(float)
    s, t = (p % 64)[:, None], np.arange(64)[None, :]
    cols["strict"] = (s < t).astype(float)
    cols["incl"] = (s <= t).astype(float)
    for n in range(6):
        b = 1 << n
        cols[f"up{n}"] = ((s // (2 * b) == t // (2 * b)) & (s // b % 2 == 0) & (t // b % 2 == 1)).astype(float)
    cols["low0"] = ((s // 2 == t // 2) & (s % 2 == 1) & (t % 2 == 0)).astype(float)
    cols["eye64"] = (s == t).astype(float)
    cols["causal"] = np.where(i <= p[:, None], 0.0, NEG)
    c = np.arange(NCMP)[None, :]
    seen = np.concatenate([(16 * c + 31 <= 128 * k + p[:, None]) for k in range(2)], 1)
    cols["cmp_neg"] = np.where(seen, 0.0, NEG)
    cols["cmp_seen"] = seen.astype(float)
    cols["inv_ret"] = (1.0 / 10000.0 ** np.linspace(0.0, 1.0, 64))[p % 64][:, None]
    cols["inv_nsa"] = (10000.0 ** (-np.arange(0, 64, 2) / 64.0))[p % 32][:, None]
    return cols


def decay_table():
    d = np.arange(T)[None, :] - np.arange(P)[:, None]
    out = []
    for h in range(RET_HEADS):
        lg = math.log(1.0 - 2.0 ** (-5.0 - h))
        dec = np.where(d >= 0, np.exp(np.maximum(d, 0) * lg), 0.0) * 128 ** -0.5
        out += [dec, dec[:, :P]]
    return np.concatenate(out, 1).astype(np.float32)


def build_constants():
    cols = constant_columns()
    at, out = {}, 0
    for k, v in cols.items():
        at[k] = (out, v.shape[1])
        out += v.shape[1]
    return np.concatenate([v for v in cols.values()], 1).astype(np.float32), at


VEC = [("ln_mix_pre", 16), ("ln_mix_post", 16), ("ln_mem_q", 16), ("ln_mem_kv", 16), ("ln_mem_post", 16),
       ("ln_ffn_pre", 16), ("ln_ffn_post", 16), ("rw_mu", 16), ("rw_w0", 4), ("rw_a0", 4), ("rw_k_k", 4),
       ("rw_k_a", 4), ("rw_r_k", 4), ("rw_lnx_g", 4), ("rw_lnx_b", 4), ("sc_conv", 12), ("cmp_pos", 32),
       ("ffn_conv_w", 264), ("ffn_conv_b", 88)]
VEC_AT = {}
for _n, _c in VEC:
    VEC_AT[_n] = (sum(c for _, c in VEC[:len(VEC_AT)]), _c)
NVEC = sum(c for _, c in VEC)

G0_TILES = 3

MIX = ([("rw", i) for i in range(12)] + [("zw", 0), ("za", 0), ("rw", 12), ("rw", 13)]
       + [("sc", i) for i in range(12)] + [("kv", i) for i in range(6)] + [("cmp", i) for i in range(4)]
       + [("q", i) for i in range(4)] + [("gate", 0)]
       + [("rq", i) for i in range(4)] + [("rk", i) for i in range(4)] + [("rv", i) for i in range(8)]
       + [("rg", i) for i in range(8)] + [("g0", i) for i in range(4 * G0_TILES)])
NMIX = len(MIX)
AT = {}
for _n, _c in enumerate(MIX):
    AT[_c] = _n

M_LOOP = 2 * G0_TILES
PAIRS = (KT - G0_TILES) // 2
M_WOUT = M_LOOP + 6 * (KT - G0_TILES)
M_MK = M_WOUT + KT
M_MV = M_MK + KT
M_WQ = M_MV + KT
M_WO = M_WQ + KT
M_UP = M_WO + KT
M_DOWN = M_UP + 2 * FT
M_END = M_DOWN + 4 * KT
R_WOUT = 2 + 4 * (KT - G0_TILES)
R_OFF = M_WOUT - R_WOUT
R_DOWN = M_DOWN - R_OFF


def program(nc, A, const_dram, decay_dram, const_at, out):
    f32, i32 = mybir.dt.float32, mybir.dt.int32
    ALU, ACT, AX = mybir.AluOpType, mybir.ActivationFunctionType, mybir.AxisListType
    MUL, ADD, SUB, MAX, MIN = ALU.mult, ALU.add, ALU.subtract, ALU.max, ALU.min
    ctx = ExitStack()
    with ctx:
        def sb(name, shape, dt=f32):
            return ctx.enter_context(nc.sbuf_tensor(name, shape, dt))

        sems = {}

        def sem(name):
            if name not in sems:
                sems[name] = ctx.enter_context(nc.semaphore(name))
            return sems[name]

        NC = const_dram.shape[1]
        cst = sb("cst", [P, NC])
        vec = sb("vec", [P, NVEC])
        region_at = nc.sbuf_base
        sb("region", [P, REGION])
        rstd = sb("rstd", [P, T])
        small = sb("small", [P, 400])
        placed = [0]

        def part(a, *dims, dt=f32):
            placed[0] += 1
            t = nc.alloc_sbuf_tensor_at(f"part{placed[0]}", [P, math.prod(dims)], dt, offset=region_at + 4 * a)
            names = "abcdef"[:len(dims)]
            return t[:, :].rearrange(f"p ({' '.join(names)}) -> p {' '.join(names)}", **dict(zip(names, dims)))

        def partr(a, *dims):
            return part(a, *dims, dt=mybir.dt.float32r)

        ring = part(0, NSLOT, KT, P)
        lora = part(8192, 4, 512)
        cw2 = part(10240, 2, 2, P)
        trig = part(10752, 2, 2, T)
        posf = part(11776, T)
        hT = part(12288, KT, T)
        obr = part(16384, 20, T)
        hidV = part(21504, 2, 2, 2, 32)
        vcx = part(21760, 2, P)[0:64]
        arena = part(22272, 27600)
        posi = part(12032, T, dt=i32)
        gsig = part(22016, T)[0:32]
        decay = lora.rearrange("p a b -> p (a b)")[:, 0:1536].rearrange("p (h c) -> p h c", h=4)

        def cc(name):
            a, n = const_at[name]
            return cst[:, a:a + n]

        def vv(name, i=0, n=1, rows=P):
            a, _ = VEC_AT[name]
            return vec[0:rows, a + i:a + i + n]

        def slab(a, n, t=None):
            ap = arena[:, a:a + n]
            return ap if t is None else ap.rearrange("p (i t) -> p i t", t=t)

        bank = ctx.enter_context(nc.psum_tensor("bank", [P, 2, 512], f32))
        big = bank[:, :, 0:T]
        sm = ctx.enter_context(nc.psum_tensor("sm", [P, 6, 512], f32))

        xT, sq0 = slab(0, 4096, T), slab(4096, 4096, T)
        kmul = slab(8208, 1024).rearrange("p (a b t) -> p a b t", a=2, b=2)
        zp = slab(0, 4112, 257)
        Z = slab(4112, 4096, T)
        sA = [slab(1024 * i, 1024) for i in range(4)]
        sB = [slab(8208 + 1024 * i, 1024) for i in range(4)]
        QR = slab(12304, 2048).rearrange("p (g two t) -> p g two t", two=2, t=64)
        sD = [slab(14352 + 1024 * i, 1024) for i in range(2)]
        sE = [slab(16400 + 1024 * i, 1024) for i in range(3)]
        scb = slab(19472, 2048).rearrange("p (b s t) -> p b s t", b=2, t=T)
        kvr = slab(21520, 1536, T)
        qn = slab(23056, 1024, T)
        kx = slab(24080, 2048).rearrange("p (b g h t) -> p b g h t", b=2, g=2, h=2)
        vtok = slab(26128, 512).rearrange("p (b s c) -> p b s c", b=2, s=2)
        blk = slab(26640, 960).rearrange("p (k i g c) -> p k i g c", k=2, i=16, g=2)
        s4 = lambda a: a.rearrange("p (i t) -> p i t", t=T)
        g16 = lambda a: a.rearrange("p (g t) -> p g t", t=64)
        sig, cs, dW, aa = sA
        gl, kk, tmp, bonus = sB
        Bd, Cd = sD
        Zr, Zk, Zv, Zl = [slab(4112 + 1024 * i, 1024) for i in range(4)]
        M1, L2, M2, Nm = Zl, sE[0], sE[1], sE[2]
        seg = sE[0]
        Lm, Xm, Zm, P1 = sA
        Vt, Bt, Ct, Yc = kk, tmp, Zr, Zk
        X0, U, S0 = [sD[0][:, 256 * i:256 * i + 256] for i in range(3)]
        scr = sD[1]
        WC = small[:, 0:16]
        gtok = small[:, 32:80].rearrange("p (s c) -> p s c", s=2)
        hidK = small[:, 80:140].rearrange("p (k c) -> p k c", k=2)
        kc0, kcr, krt = small[:, 140:170], small[:, 170:200], small[:, 200:230]
        kcx = small[:, 230:290].rearrange("p (g h c) -> p g h c", g=2, h=2)
        cmx, csum = small[:, 290:306], small[:, 306:322]
        umax, unb, usum, uscl = [small[:, 338 + 4 * i:342 + 4 * i] for i in range(4)]
        mmax, mnb, msum = [small[:, 354 + 2 * i:356 + 2 * i] for i in range(3)]
        esc = slab(0, 240, 15)
        pcs = slab(256, 512, 32)
        pcT = scr[0:64, :].rearrange("p (q t) -> p q t", q=4)
        pu = slab(19472, 768)
        pT = slab(20240, 768)
        rqk = slab(2048, 2048, T)
        rv = slab(4112, 2048).rearrange("p (s c) -> p s c", s=2)
        rg = slab(6160, 2048, T)
        rt1, rt2 = slab(8208, 2048, T), slab(10256, 2048, T)
        sT = slab(12304, 1536).rearrange("p (h c) -> p h c", h=4)
        oc, osq = slab(8208, 2048, T), slab(10256, 2048, T)
        rstd4 = slab(2048, 1024, T)
        g0 = slab(23056, 1024 * G0_TILES).rearrange("p (k j t) -> p k j t", k=G0_TILES, t=T)

        raw = part(0, 2, 2, 8, P)
        wsplit = [partr(8192, 2, 8, P), partr(10240, 2, 8, P), partr(4096, 2, 8, P), partr(6144, 2, 8, P)]
        memn = part(12288, KT, T)
        memK = memn
        mtmp = part(16384, 4, T)
        gts = part(17408, 2, 4, T)
        res = part(16384, KT, T)
        sq = part(20480, 2, T)
        pmT = part(20480, 2, 2, T)
        ub = part(20480, 2, 2, T)
        cross = part(21504, 2, T)
        acc = part(22016, T)
        bcross = part(19456, 2, 2, T)
        X1 = partr(22272, KT, 2 * T)
        yD = part(22272, KT, T)
        merged = part(30480, KT, T)
        msq = merged
        memV = part(30480, 2, D)
        pm = part(34576, 2, T)
        vt = part(34576, 2, T)
        X2 = partr(35088, 20, 2 * T)
        yT = part(45328, KT, T)
        qT = yT
        gA, gB = partr(12288, 8, 2 * T), partr(30464, FT - 8, 2 * T)
        rawu, gtmp = part(48896, 2, T), part(49408, T)

        def bc(ap, n):
            return ap.unsqueeze(1).to_broadcast([ap.shape[0], n, ap.shape[1]])

        def bl(ap, n):
            return ap.unsqueeze(2).to_broadcast([ap.shape[0], ap.shape[1], n])

        def ready(n):
            return sem(f"chunk_loaded{n % NSLOT}"), 16 * (n // NSLOT + 1)

        for name in ([f"chunk_loaded{i}" for i in range(4)] + ["chunk_used", "chunk_out"] + [f"half_loaded{i}" for i in range(4)]):
            sem(name)

        block = ctx.enter_context(nc.Block())

        @block.sync
        def _(sp):
            used, loaded = sem("chunk_used"), [sem(f"chunk_loaded{i}") for i in range(NSLOT)]
            sp.dma_start(xT, A["xT"]).then_inc(sem("x_loaded"), 16)
            sp.dma_start(posi[:, :], A["positions"].to_broadcast([P, T])).then_inc(sem("pos_loaded"), 16)
            flat = ring[:, :, :, :].rearrange("p s k c -> p s (k c)")
            for n, (what, i) in enumerate(MIX):
                if n >= NSLOT:
                    sp.wait_ge(used, n - NSLOT + 1)
                if n == AT[("kv", 0)]:
                    sp.wait_ge(sem("rw_g_mm"), 1)
                    sp.dma_start(decay.rearrange("p h c -> p (h c)"), decay_dram).then_inc(sem("decay_loaded"), 16)
                s = n % NSLOT
                src = {"rw": "w_rw", "zw": "w_zwa", "za": "w_zwa", "sc": "w_sc", "kv": "w_kv", "cmp": "w_cmp1",
                       "q": "w_nq", "gate": "w_ngate", "rq": "w_rq", "rk": "w_rk", "rv": "w_rv", "rg": "w_rg",
                       "g0": f"w_g{i % 4}"}[what]
                j = {"zw": 0, "za": 1, "g0": i // 4}.get(what, i)
                w = A[src][j]
                sp.dma_start(flat[:, s, 0:w.shape[1]], w).then_inc(loaded[s], 16)
                if n == NSLOT - 1:
                    sp.dma_start(lora[0:96, 0:2, :], A["lora_wa"]).then_inc(sem("lora_loaded"), 16)
                    sp.dma_start(lora[:, 2:4, :], A["lora_g"]).then_inc(sem("lora_loaded"), 16)
                    sp.dma_start(cw2[:, :, :, :], A["w_cmp2"]).then_inc(sem("lora_loaded"), 16)

            hl, split = [sem(f"half_loaded{i}") for i in range(4)], sem("lo_done")

            def load(m, w, at):
                cols = w.shape[1]
                first = cols // 2 if cols == 8 * P else 8 * P
                for h in range(2):
                    if m >= 2:
                        sp.wait_ge(split, at(2, 2 * m + h - 3))
                    else:
                        sp.wait_ge(used, NMIX - 2 + m)
                    a, z = (0, first) if h == 0 else (first, cols)
                    sp.dma_start(raw[:, m % 2, h, 0:(z - a) // P, :].rearrange("p k c -> p (k c)"), w[:, a:z])                       .then_inc(hl[2 * (m % 2) + h], 16)

            one = lambda k, v: v

            def loop(base, count, per, sources):
                with sp.Fori(0, count) as i:
                    for j in range(per):
                        load(base + j, sources[j](i), lambda k, v: i * (k * per) + v)

            for t in range(G0_TILES):
                load(2 * t, A["w_brab"][t], one)
                load(2 * t + 1, A["w_brcd"][t], one)
            tile_weights = [A[f"w_g{j}"] for j in range(4)] + [A["w_brab"], A["w_brcd"]]
            loop(M_LOOP, PAIRS, 12, [(lambda i, t=t, w=w: w[i * 2 + (G0_TILES + t)]) for t in range(2)
                                     for w in tile_weights])
            sp.wait_ge(sem("stream_split"), 4)
            sp.dma_start(memn, A["memT"]).then_inc(sem("mem_loaded"), 16)
            for j, w in enumerate(tile_weights):
                load(M_WOUT - 6 + j, w[KT - 1], one)
            for j in range(KT):
                load(M_WOUT + j, A["w_out"][j], one)
                if j == 3:
                    sp.wait_ge(sem("merged"), KT)
                    sp.dma_start(res, A["xT"]).then_inc(sem("x_loaded"), 16)
            for j in range(KT):
                load(M_MK + j, A["w_mk"][j], one)
            for base, name, count in ((M_MV, "w_mv", 4), (M_WQ, "w_q", 4), (M_WO, "w_o", 4), (M_UP, "w_up", 22),
                                      (M_DOWN, "w_dn", 16)):
                loop(base, count, 4, [(lambda i, j=j: A[name][i * 4 + j]) for j in range(4)])
            for q in range(4):
                sp.wait_ge(sem("res_ready"), 8 + q + 1)
                sp.dma_start(out[:, 4 * q:4 * q + 4, :], res[:, 4 * q:4 * q + 4, :]).then_inc(sem("stored"), 16)
            sp.wait_ge(sem("stored"), 64)

        @block.tensor
        def _(pe):
            used, outd = sem("chunk_used"), sem("chunk_out")

            def take(n):
                pe.wait_ge(*ready(n))
                if n >= 2:
                    pe.wait_ge(outd, n - 1)

            def project(n, rhs=None, M=P, rhs_n=T):
                take(n)
                x = hT if rhs is None else rhs
                w = ring[:, n % NSLOT, :, :].rearrange("p k c -> p (k c)")
                for k in range(KT):
                    if n == 0 and k % 4 == 0:
                        pe.wait_ge(sem("h_ready"), k // 4 + 1)
                    mm = pe.matmul(big[0:M, n % 2, 0:rhs_n], w[:, k * M:(k + 1) * M], x[:, k, :],
                                   start=k == 0, stop=k == KT - 1)
                mm.then_inc(used, 1)

            def project_tokens(n, x, dst):
                for s in range(2):
                    for k in range(KT):
                        mm = pe.matmul(dst[:, s * P:(s + 1) * P], x[:, k, s * P:(s + 1) * P],
                                       ring[:, n % NSLOT, k, :], start=k == 0, stop=k == KT - 1)
                mm.then_inc(used, 1)

            def sumsq(src, need, first, done):
                for k in range(KT):
                    if k % 4 == 0:
                        pe.wait_ge(sem(need), first + k // 4)
                    mm = pe.matmul(sm[:, 5, 0:T], cc("ones128"), src[:, k, :], start=k == 0, stop=k == KT - 1)
                mm.then_inc(sem(done), 1)

            def per_head(fn):
                for h in range(2):
                    for g in range(16):
                        mm = fn(slice(64 * h, 64 * h + 64), g)
                return mm

            def b64(base, g, w=64):
                per = 512 // w
                return base + g // per, g % per * w

            def small_mm(base, rows, g, lhsT, rhs, w=64, start=True, stop=True):
                b, c = b64(base, g, w)
                return pe.matmul(sm[rows, b, c:c + w], lhsT, rhs, start=start, stop=stop)

            G = {k: g16(v) for k, v in dict(B=Bd, C=Cd, N=Nm, L=Lm, X=Xm, Z=Zm, P1=P1, V=Vt, Bt=Bt, Ct=Ct,
                                             M1=M1, M2=M2, L2=L2, Vc=Zv).items()}
            eye = lambda r: cst[r, const_at["ident"][0] + r.start:const_at["ident"][0] + r.stop]
            lv = sem("rw_level")

            def rw_lora():
                pe.wait_ge(sem("lora_loaded"), 16 * 3)
                pe.wait_ge(sem("rw_lora_in"), 1)
                for i in range(4):
                    pe.matmul(sm[:, i // 2, i % 2 * T:i % 2 * T + T], lora[0:96, 0, i * P:(i + 1) * P],
                              Z[0:96, 12, :], start=True, stop=True)
                for i in range(4):
                    mm = pe.matmul(sm[:, 2 + i // 2, i % 2 * T:i % 2 * T + T], lora[0:96, 1, i * P:(i + 1) * P],
                                   Z[0:96, 13, :], start=True, stop=True)
                mm.then_inc(sem("rw_lora_mm"), 1)

            def rw_g():
                pe.wait_ge(sem("rw_sigmoids"), 1)
                pe.wait_ge(sem("rw_kk_sq"), 1)
                for i in range(4):
                    for k in range(2):
                        mm = pe.matmul(sm[:, i // 2, i % 2 * T:i % 2 * T + T], lora[:, 2 + k, i * P:(i + 1) * P],
                                       Z[:, 14 + k, :], start=k == 0, stop=k == 1)
                mm.then_inc(sem("rw_g_mm"), 1)
                for j in range(2):
                    mm = pe.matmul(sm[:, 2 + j, :], cc("ones64"), tmp[:, j * 512:(j + 1) * 512], start=True, stop=True)
                mm.then_inc(sem("rw_kk_mm"), 1)

            def rw_bonus():
                pe.wait_ge(sem("rw_g_out"), 1)
                pe.wait_ge(sem("rw_rk"), 1)
                for j in range(2):
                    mm = pe.matmul(sm[:, j, :], cc("ones64"), Zr[:, j * 512:(j + 1) * 512], start=True, stop=True)
                mm.then_inc(sem("rw_bonus_mm"), 1)

            def rw_s1():
                pe.wait_ge(sem("rw_operands"), 1)
                pe.wait_ge(sem("rw_bonus_out"), 1)
                per_head(lambda r, g: small_mm(0, r, g, G["B"][r, g], QR[r, g, :, :], w=128)) \
                    .then_inc(sem("rw_s1_mm"), 1)

            def rw_s2():
                pe.wait_ge(sem("rw_s1_out"), 1)
                per_head(lambda r, g: small_mm(0, r, g, G["C"][r, g], QR[r, g, :, :], w=128)) \
                    .then_inc(sem("rw_s2_mm"), 1)

            def rw_s3():
                pe.wait_ge(sem("rw_s2_out"), 1)
                per_head(lambda r, g: small_mm(0, r, g, QR[r, g, 0, :], G["B"][r, g])).then_inc(sem("rw_s3_mm"), 1)
                per_head(lambda r, g: small_mm(2, r, g, G["Vc"][r, g], eye(r))).then_inc(sem("rw_s3_mm"), 1)

            def rw_s4():
                pe.wait_ge(sem("rw_l_out"), 1)
                pe.wait_ge(sem("rw_v_out"), 1)
                per_head(lambda r, g: small_mm(0, r, g, G["B"][r, g], eye(r))).then_inc(sem("rw_s4_mm"), 1)
                per_head(lambda r, g: small_mm(2, r, g, G["C"][r, g], eye(r))).then_inc(sem("rw_s4_mm"), 1)

            def rw_level(n):
                if n == 1:
                    pe.wait_ge(sem("rw_s4_out"), 2)
                pe.wait_ge(sem("rw_x_ready"), n)
                per_head(lambda r, g: small_mm(0, r, g, G["L"][r, g], G["X"][r, g])).then_inc(sem("rw_p1_mm"), 1)

            def rw_level2(n):
                pe.wait_ge(sem("rw_p1_out"), n)
                per_head(lambda r, g: small_mm(2, r, g, G["Z"][r, g], G["P1"][r, g])).then_inc(sem("rw_p2_mm"), 1)
                if n < 5:
                    per_head(lambda r, g: small_mm(0, r, g, G["P1"][r, g], G["Z"][r, g])) \
                        .then_inc(sem("rw_p2_mm"), 1)

            def four(base, off, fn):
                for h in range(2):
                    r = slice(64 * h, 64 * h + 64)
                    for i in range(4):
                        pairs = fn(r, i)
                        for q, (a, b) in enumerate(pairs):
                            mm = pe.matmul(sm[r, base + i // 2, off + i % 2 * 64:off + i % 2 * 64 + 64], a, b,
                                           start=q == 0, stop=q == len(pairs) - 1)
                return mm

            v4 = lambda a: a.rearrange("p (i t) -> p i t", t=64)
            X04, U4, S4 = v4(X0), v4(U), v4(S0)

            def rw_chunk_a(c):
                if c == 0:
                    pe.wait_ge(sem("rw_x_ready"), 6)
                else:
                    pe.wait_ge(sem("rw_state"), c)
                    pe.wait_ge(sem("rw_y_out"), c)
                four(0, 0, lambda r, i: ([(QR[r, 4 * i + c, 0, :], S4[r, i])] if c else [])
                     + [(G["L2"][r, 4 * i + c], G["V"][r, 4 * i + c])]).then_inc(sem("rw_rhs_mm"), 1)

            def rw_chunk_b(c):
                pe.wait_ge(sem("rw_rhs_out"), c + 1)
                four(2, 0, lambda r, i: [(G["X"][r, 4 * i + c], X04[r, i])]).then_inc(sem("rw_u_mm"), 1)

            def rw_chunk_c(c):
                pe.wait_ge(sem("rw_u_out"), c + 1)
                if c < NCH - 1:
                    four(2, 128, lambda r, i: [(G["Bt"][r, 4 * i + c], U4[r, i]),
                                               (G["Ct"][r, 4 * i + c], G["V"][r, 4 * i + c])]) \
                        .then_inc(sem("rw_ds_mm"), 1)
                four(0, 128, lambda r, i: ([(S4[r, i], QR[r, 4 * i + c, 1, :])] if c else [])
                     + [(U4[r, i], G["M1"][r, 4 * i + c]), (G["V"][r, 4 * i + c], G["M2"][r, 4 * i + c])]) \
                    .then_inc(sem("rw_y_mm"), 1)

            def rw_mean():
                pe.wait_ge(sem("rw_y_out"), NCH)
                for j in range(2):
                    mm = pe.matmul(sm[:, j, :], cc("ones64"), Yc[:, j * 512:(j + 1) * 512], start=True, stop=True)
                mm.then_inc(sem("rw_norm_mm"), 1)

            def rw_var():
                pe.wait_ge(sem("rw_ysq"), 1)
                for j in range(2):
                    mm = pe.matmul(sm[:, 2 + j, :], cc("ones64"), Xm[:, j * 512:(j + 1) * 512], start=True, stop=True)
                mm.then_inc(sem("rw_norm_mm"), 1)

            def nsa_dup():
                pe.wait_ge(outd, AT[("kv", 1)] + 1)
                for kv in range(2):
                    for g in range(2):
                        mm = pe.matmul(sm[:, 4 + kv, g * T:(g + 1) * T], cc(f"dup{g}"), kvr[:, kv, :],
                                       start=True, stop=True)
                mm.then_inc(sem("nsa_dup_mm"), 1)

            def nsa_rot_k():
                pe.wait_ge(outd, AT[("kv", 5)] + 1)
                pe.wait_ge(sem("nsa_blk"), 2)
                pe.matmul(sm[:, 4, 0:T], cc("rot64"), kvr[:, 2, :], start=True, stop=True)
                mm = pe.matmul(sm[:, 4, T:2 * T], cc("rot64"), kvr[:, 4, :], start=True, stop=True)
                mm.then_inc(sem("nsa_rope_mm"), 1)

            def nsa_dup_k():
                pe.wait_ge(sem("nsa_k_roped"), 1)
                for b in range(2):
                    for g in range(2):
                        mm = pe.matmul(sm[:, 4 + b, g * T:(g + 1) * T], cc(f"dup{g}"), kvr[:, 2 + 2 * b, :],
                                       start=True, stop=True)
                mm.then_inc(sem("nsa_dupk_mm"), 1)

            def nsa_vtok():
                pe.wait_ge(sem("nsa_kx"), 1)
                for b in range(2):
                    for s in range(2):
                        mm = pe.matmul(sm[:, 4, (2 * b + s) * P:(2 * b + s + 1) * P], kvr[:, 3 + 2 * b, s * P:(s + 1) * P],
                                       cc("ident"), start=True, stop=True)
                mm.then_inc(sem("nsa_vtok_mm"), 1)

            def nsa_cmp_hidden(i):
                kv, ht = divmod(i, 2)
                n = AT[("cmp", i)]
                take(n)
                if i == 0:
                    pe.wait_ge(sem("nsa_blk"), 2)
                for k in range(16):
                    mm = pe.matmul(big[:, n % 2, 0:30], ring[:, n % NSLOT, k, :],
                                   blk[:, kv, k].rearrange("p g c -> p (g c)"), start=k == 0, stop=k == 15)
                mm.then_inc(used, 1)

            def nsa_cmp_out():
                pe.wait_ge(outd, AT[("cmp", 3)] + 1)
                pe.wait_ge(sem("nsa_hidV"), 1)
                pe.wait_ge(sem("nsa_vtok"), 1)
                for k in range(2):
                    mm = pe.matmul(sm[:, 4, 0:30], cw2[:, 0, k, :], hidK[:, k, :], start=k == 0, stop=k == 1)
                mm.then_inc(sem("nsa_cmp_mm"), 1)
                for g in range(2):
                    for k in range(2):
                        mm = pe.matmul(sm[0:64, 5, g * 64:g * 64 + 64],
                                       hidV[:, k, g].rearrange("p h c -> p (h c)"), cw2[:, 1, k, 0:64],
                                       start=k == 0, stop=k == 1)
                mm.then_inc(sem("nsa_cmp_mm"), 1)

            def nsa_rot_kc():
                pe.wait_ge(sem("nsa_kc0"), 1)
                pe.matmul(sm[:, 4, 64:94], cc("rot64"), kc0, start=True, stop=True).then_inc(sem("nsa_rope_mm"), 1)

            def nsa_rot_q():
                pe.wait_ge(outd, AT[("q", 3)] + 1)
                pe.wait_ge(sem("nsa_kcx"), 1)
                pe.wait_ge(sem("nsa_vcx"), 1)
                for j in range(2):
                    mm = pe.matmul(sm[:, 4 + j, :], cc("rot64"), qn[:, 2 * j:2 * j + 2, :], start=True, stop=True)
                mm.then_inc(sem("nsa_rope_mm"), 1)

            def nsa_cmp_scores():
                pe.wait_ge(sem("nsa_q_roped"), 1)
                pe.wait_ge(outd, AT[("gate", 0)] + 1)
                for s in range(2):
                    mm = pe.matmul(sm[:, 5, 256 + s * 24:256 + s * 24 + 24], gsig[0:24, s * P:(s + 1) * P],
                                   cc("ident")[0:24, 0:24], start=True, stop=True)
                for q in range(4):
                    for s in range(2):
                        mm = pe.matmul(sm[:, 4, (2 * q + s) * 30:(2 * q + s + 1) * 30], qn[:, q, s * P:(s + 1) * P],
                                       kcx[:, q // 2].rearrange("p h c -> p (h c)"), start=True, stop=True)
                mm.then_inc(sem("nsa_cmps_mm"), 1)

            def nsa_cmp_T():
                pe.wait_ge(sem("nsa_pcs"), 1)
                for q in range(4):
                    for s in range(2):
                        u = 4 * q + 2 * s
                        mm = pe.matmul(sm[0:64, 4 + q // 2, (q % 2) * T + s * P:(q % 2) * T + s * P + P],
                                       pcs[:, u:u + 2].rearrange("p h c -> p (h c)"), cc("ident"), start=True, stop=True)
                mm.then_inc(sem("nsa_cmpT_mm"), 1)

            def unit_scores(u):
                q, b = divmod(u, 2)
                if u:
                    pe.wait_ge(sem("nsa_p"), u)
                k = kx[:, b, q // 2]
                pe.matmul(sm[:, 0, 0:256], qn[:, q, 0:P], k[:, :, 0:P], start=True, stop=True)
                pe.matmul(sm[:, 1, :], qn[:, q, P:T], k, start=True, stop=True).then_inc(sem("nsa_s_mm"), 1)

            def unit_T(u):
                pe.wait_ge(sem("nsa_p_scaled"), u + 1)
                if u:
                    pe.wait_ge(sem("nsa_pT"), u)
                for h in range(2):
                    pe.matmul(sm[:, 2, h * T:h * T + P], pu[:, h * P:(h + 1) * P], cc("ident"), start=True, stop=True)
                    pe.matmul(sm[:, 2, h * T + P:h * T + T], pu[:, 256 + h * T:256 + h * T + P], cc("ident"),
                              start=True, stop=True)
                    mm = pe.matmul(sm[:, 3, h * P:(h + 1) * P], pu[:, 256 + h * T + P:256 + h * T + T], cc("ident"),
                                   start=True, stop=True)
                mm.then_inc(sem("nsa_T_mm"), 1)

            def unit_pv(u):
                q, b = divmod(u, 2)
                g = q // 2
                if b == 0:
                    if q == 0:
                        pe.wait_ge(sem("nsa_pcT"), 1)
                    if q >= 2:
                        pe.wait_ge(sem("nsa_o"), q - 1)
                pe.wait_ge(sem("nsa_pT"), u + 1)
                for h in range(2):
                    r = slice(64 * h, 64 * h + 64)
                    pe.matmul(sm[r, 4 + q % 2, 0:T], vtok[:, b, 0, 64 * g:64 * g + 64], pT[:, h * T:(h + 1) * T],
                              start=b == 0, stop=False, skip_group_check=True)
                    mm = pe.matmul(sm[r, 4 + q % 2, P:T], vtok[:, b, 1, 64 * g:64 * g + 64],
                                   pT[:, 512 + h * P:512 + (h + 1) * P], start=False, stop=False,
                                   skip_group_check=True)
                if b == 1:
                    mm = pe.matmul(sm[:, 4 + q % 2, 0:T], vcx[:, g, :], pcT[:, q, :], start=False, stop=True,
                                   skip_group_check=True)
                mm.then_inc(sem("nsa_pv_mm"), 1)

            def ret_rot():
                pe.wait_ge(sem("nsa_o"), 4)
                for j in range(4):
                    mm = pe.matmul(sm[:, j, :], cc("rot128"), rqk[:, 2 * j:2 * j + 2, :], start=True, stop=True)
                mm.then_inc(sem("ret_mm"), 1)

            def ret_scores():
                pe.wait_ge(sem("ret_vector"), 1)
                for h in range(4):
                    pe.matmul(sm[:, h, 0:T], rqk[:, 4 + h, 0:P], rqk[:, h, :], start=True, stop=True)
                    mm = pe.matmul(sm[:, h, T:T + P], rqk[:, 4 + h, P:T], rqk[:, h, P:T], start=True, stop=True)
                mm.then_inc(sem("ret_mm"), 1)

            def ret_out():
                pe.wait_ge(sem("ret_sT"), 4)
                for i in range(8):
                    h = i // 2
                    d = sm[:, i // 2, i % 2 * T:i % 2 * T + T]
                    pe.matmul(d[:, 0:P], rv[:, 0, i * P:(i + 1) * P], sT[:, h, 0:P], start=True, stop=True)
                    pe.matmul(d[:, P:], rv[:, 0, i * P:(i + 1) * P], sT[:, h, P:T], start=True, stop=False)
                    mm = pe.matmul(d[:, P:T], rv[:, 1, i * P:(i + 1) * P], sT[:, h, T:T + P], start=False, stop=True)
                mm.then_inc(sem("ret_mm"), 1)

            def ret_sum(src, need, val, name):
                pe.wait_ge(sem(need), val)
                for h in range(4):
                    for j in range(2):
                        mm = pe.matmul(sm[:, 4 + h // 2, h % 2 * T:h % 2 * T + T], cc("ones128"), src[:, 2 * h + j, :],
                                       start=j == 0, stop=j == 1)
                mm.then_inc(sem(name), 1)

            pe.wait_ge(sem("consts_loaded"), 16 * 2)
            sumsq(sq0, "x_sq", 1, "norm_mm")
            steps = {
                ("sc", 0): [rw_lora], ("sc", 1): [rw_g], ("sc", 3): [rw_bonus, rw_s1],
                ("sc", 4): [rw_s2], ("sc", 5): [rw_s3], ("sc", 6): [rw_s4],
                ("sc", 7): [lambda: rw_level(1)], ("sc", 8): [lambda: rw_level2(1)],
                ("sc", 9): [lambda: rw_level(2)], ("sc", 10): [lambda: rw_level2(2)],
                ("sc", 11): [lambda: rw_level(3)], ("kv", 0): [lambda: rw_level2(3)],
                ("kv", 1): [lambda: rw_level(4)], ("kv", 2): [lambda: rw_level2(4), nsa_dup],
                ("kv", 3): [lambda: rw_level(5)], ("kv", 4): [lambda: rw_level2(5)],
                ("kv", 5): [lambda: rw_chunk_a(0)],
                ("cmp", 0): [nsa_rot_k, lambda: rw_chunk_b(0)], ("cmp", 1): [lambda: rw_chunk_c(0)],
                ("cmp", 2): [nsa_dup_k, lambda: rw_chunk_a(1)], ("cmp", 3): [lambda: rw_chunk_b(1)],
                ("q", 0): [lambda: rw_chunk_c(1), nsa_vtok], ("q", 1): [lambda: rw_chunk_a(2)],
                ("q", 2): [lambda: rw_chunk_b(2), nsa_cmp_out], ("q", 3): [lambda: rw_chunk_c(2), nsa_rot_kc],
                ("gate", 0): [lambda: rw_chunk_a(3), nsa_rot_q],
                ("rq", 0): [lambda: rw_chunk_b(3), nsa_cmp_scores], ("rq", 1): [lambda: rw_chunk_c(3)],
                ("rq", 2): [rw_mean, nsa_cmp_T], ("rq", 3): [rw_var],
                ("g0", 0): [ret_rot], ("g0", 2): [ret_scores], ("g0", 4): [ret_out],
                ("g0", 6): [lambda: ret_sum(oc, "ret_scalar", 1, "ret_mm")],
                ("g0", 9): [lambda: ret_sum(osq, "ret_scalar", 2, "ret_mm")],
            }
            order = [c for c in MIX if c[0] in ("rk", "rv", "rg")]
            for u in range(8):
                steps.setdefault(order[2 * u + 1], []).append(lambda u=u: unit_scores(u))
                if u:
                    steps[order[2 * u + 1]].insert(0, lambda u=u: unit_pv(u - 1))
                steps.setdefault(order[2 * u + 2], []).append(lambda u=u: unit_T(u))
            steps.setdefault(order[18], []).append(lambda: unit_pv(7))
            for n, (what, i) in enumerate(MIX):
                for s in steps.get((what, i), []):
                    s()
                if what in ("zw", "za"):
                    project(n, M=96)
                elif what == "gate":
                    project(n, M=24)
                elif what == "cmp":
                    nsa_cmp_hidden(i)
                elif what == "rv":
                    take(n)
                    project_tokens(n, hT, big[:, n % 2, :])
                else:
                    project(n)

            pe.wait_ge(outd, NMIX)
            half_used, prod_out, lo_done = sem("half_used"), sem("prod_out"), sem("lo_done")
            one = lambda k, v: v

            def half(m, h, at, x, k0, n, dst, start=True, stop=True):
                pe.wait_ge(lo_done, at(2, 2 * m + h + 1))
                w = wsplit[(2 * m + h) % 4]
                for k in range(n):
                    last = stop and k == n - 1
                    for term in ("cross", "high") if last else ("high", "cross"):
                        if term == "high":
                            mm = pe.matmul(dst, w[:, 0, k, :], x[:, k0 + k, :], start=start and k == 0, stop=last,
                                           skip_group_check=True)
                        else:
                            mm = pe.matmul(dst[:, T:2 * T], w[:, 1, k, :], x[:, k0 + k, 0:T], start=False, stop=False,
                                           skip_group_check=True)
                mm.then_inc(half_used, 1)

            def chunk(m, at, x, split=None):
                pe.wait_ge(prod_out, at(1, m - R_OFF - 1))
                if split:
                    pe.wait_ge(sem("stream_split"), split[0])
                half(m, 0, at, x, 0, 8, bank[:, m % 2, :], True, False)
                if split:
                    pe.wait_ge(sem("stream_split"), split[1])
                half(m, 1, at, x, 8, 8, bank[:, m % 2, :], False, True)

            def branches(m, at, pair, atp):
                for x in range(2):
                    if pair + x >= 2:
                        pe.wait_ge(sem("branch_out"), atp(pair + x - 1))
                    for h in range(2):
                        k0, n = [(8, 4), (12, 4), (0, 8), (16, 4)][2 * x + h]
                        half(m + x, h, at, X2, k0, n, sm[:, 2 * x + h, :])

            def loop(base, count, x, split=None):
                with pe.Fori(0, count) as i:
                    for j in range(4):
                        chunk(base + j, lambda k, v: i * (4 * k) + v, x, split if j == 0 else None)

            def sumsq(src, need, first, done, tiles=KT):
                for k in range(tiles):
                    if k % 4 == 0:
                        pe.wait_ge(sem(need), first + k // 4)
                    mm = pe.matmul(sm[:, 5, 0:T], cc("ones128"), src[:, k, :], start=k == 0, stop=k == tiles - 1)
                mm.then_inc(sem(done), 1)

            def y_norm(step):
                pe.wait_ge(sem("y_acc"), 17 * step + 17)
                pe.matmul(sm[:, 5, 0:T], cc("ones128"), acc, start=True, stop=True).then_inc(sem("norm_mm"), 1)

            for t in range(G0_TILES):
                if t == 0:
                    pe.wait_ge(sem("obr_split"), 4)
                branches(2 * t, one, 2 * t, lambda v: v)
            pe.wait_ge(sem("stream_split"), 4)
            def merge(i, tiles):
                at = lambda k, v: i * (12 * k) + v
                for t in range(tiles):
                    for j in range(4):
                        m = M_LOOP + 6 * t + j
                        pe.wait_ge(prod_out, i * 8 + (4 * t + j + 1))
                        half(m, 0, at, X1, 0, 8, bank[:, j % 2, :], True, False)
                        half(m, 1, at, X1, 8, 8, bank[:, j % 2, :], False, True)
                    branches(M_LOOP + 6 * t + 4, at, 2 * (G0_TILES + t), lambda v: i * 4 + v)

            with pe.Fori(0, PAIRS) as i:
                merge(i, 2)
            merge(PAIRS, 1)

            for j in range(KT):
                chunk(M_WOUT + j, one, X1, (6, 8) if j == 0 else None)
                if j == 6:
                    sumsq(msq, "quarter_sums", 1, "norm_mm", 4)
            pe.wait_ge(sem("stream_split"), 12)
            for j in range(KT):
                chunk(M_MK + j, one, X2)
                if j == 0:
                    y_norm(0)
                elif j == 8:
                    sumsq(yT, "quarter_sums", 2, "norm_mm", 4)
            def v_turned(j):
                pe.wait_ge(prod_out, M_MV + j - R_OFF + 1)
                if j >= 2:
                    pe.wait_ge(sem("v_out"), j - 1)
                for s in range(2):
                    mm = pe.matmul(sm[:, j % 2, s * P:(s + 1) * P], vt[:, j % 2, s * P:(s + 1) * P], cc("ident"),
                                   start=True, stop=True)
                mm.then_inc(sem("v_T_mm"), 1)

            for j in range(KT):
                chunk(M_MV + j, one, X2)
                if j:
                    v_turned(j - 1)
            def scores(h):
                pe.wait_ge(prod_out, M_WQ + 4 * h + 4 - R_OFF)
                if h == 0:
                    pe.wait_ge(sem("v_out"), KT)
                if h >= 2:
                    pe.wait_ge(sem("ma_p"), h - 1)
                for s in range(2):
                    for k in range(4):
                        mm = pe.matmul(sm[:, h % 2, s * T:(s + 1) * T], qT[:, 4 * h + k, s * P:(s + 1) * P],
                                       memK[:, 4 * h + k, :], start=k == 0, stop=k == 3)
                mm.then_inc(sem("ma_s_mm"), 1)

            def turned(h):
                pe.wait_ge(sem("ma_pn"), h + 1)
                for m in range(2):
                    for s in range(2):
                        mm = pe.matmul(sm[:, 2, m * T + s * P:m * T + (s + 1) * P], pm[:, s, m * P:(m + 1) * P],
                                       cc("ident"), start=True, stop=True)
                mm.then_inc(sem("ma_T_mm"), 1)

            def values(h):
                pe.wait_ge(sem("ma_pT"), h + 1)
                if h:
                    pe.wait_ge(sem("ma_o"), h)
                for k in range(4):
                    for m in range(2):
                        mm = pe.matmul(sm[:, 3 + k // 2, k % 2 * T:k % 2 * T + T],
                                       memV[:, m, (4 * h + k) * P:(4 * h + k + 1) * P], pmT[:, h % 2, m, :],
                                       start=m == 0, stop=m == 1)
                mm.then_inc(sem("ma_o_mm"), 1)

            for j in range(KT):
                chunk(M_WQ + j, one, X1, (14, 16) if j == 0 else None)
                if j == 0:
                    v_turned(KT - 1)
                if j >= 4 and j % 4 == 0:
                    if j >= 8:
                        values(j // 4 - 2)
                    scores(j // 4 - 1)
                elif j >= 4 and j % 4 == 3:
                    turned(j // 4 - 1)
            values(2)
            scores(3)
            turned(3)
            values(3)
            pe.wait_ge(sem("ma_o"), 4)
            loop(M_WO, 4, X2)
            y_norm(1)
            sumsq(yT, "res_sq", 9, "norm_mm")
            loop(M_UP, 22, X1, (18, 20))
            with pe.Fori(0, 8) as i:
                for t in range(2):
                    pe.wait_ge(prod_out, i * 2 + (R_DOWN + t - 1))
                    for j in range(4):
                        if t == 0:
                            pe.wait_ge(sem("g_split"), 11 * j + 11)
                        for h, n in ((0, 8), (1, 3)):
                            k = 11 * j + 8 * h
                            x, k0 = (gA, k) if k < 8 else (gB, k - 8)
                            half(M_DOWN + 4 * t + j, h, lambda k, v: i * (8 * k) + v, x, k0, n, bank[:, t, :],
                                 j == 0 and h == 0, j == 3 and h == 1)
            y_norm(2)

        @block.scalar
        def _(act):
            used, outd = sem("chunk_used"), sem("chunk_out")
            act.sem_inc(sem("prod_out"), 2)
            act.dma_start(cst[:, :], const_dram).then_inc(sem("consts_loaded"), 16)
            act.dma_start(vec[:, :], A["vec"]).then_inc(sem("consts_loaded"), 16)
            cp, idt = ACT.Copy, ACT.Identity

            def std(k):
                act.wait_ge(sem("norm_var"), k)
                act.activation(rstd[:, :], rstd[:, :], ACT.Sqrt).then_inc(sem("norm_std"), 1)

            act.wait_ge(sem("x_loaded"), 16)
            for q in range(4):
                act.activation(sq0[:, 4 * q:4 * q + 4, :], xT[:, 4 * q:4 * q + 4, :], ACT.Square) \
                   .then_inc(sem("x_sq"), 1)
            std(1)
            act.wait_ge(sem("trig_arg"), 1)
            act.activation(trig[:, :, :, :], trig[:, :, :, :], ACT.Sin).then_inc(sem("trig_ready"), 1)

            def chunk(n, dst, src=None, func=cp, **kw):
                act.wait_ge(used, n + 1)
                act.activation(dst, big[:, n % 2, :] if src is None else src, func, **kw).then_inc(outd, 1)

            def rw_lora_in():
                act.wait_ge(sem("rw_mixed"), 3)
                act.activation(Z[0:96, 12, :], Z[0:96, 12, :], ACT.Tanh).then_inc(sem("rw_lora_in"), 1)
                act.activation(Z[:, 14:16, :], Z[:, 14:16, :], ACT.Sigmoid).then_inc(sem("rw_zg"), 1)

            def rw_sigmoids():
                act.wait_ge(sem("rw_lora_mm"), 1)
                for i in range(4):
                    act.activation(s4(sig)[:, i, :], sm[:, i // 2, i % 2 * T:i % 2 * T + T], ACT.Sigmoid,
                                   bias=vv("rw_w0", i))
                for i in range(4):
                    mm = act.activation(s4(aa)[:, i, :], sm[:, 2 + i // 2, i % 2 * T:i % 2 * T + T], ACT.Sigmoid,
                                        bias=vv("rw_a0", i))
                mm.then_inc(sem("rw_sigmoids"), 1)

            def rw_exps():
                act.wait_ge(sem("rw_cum"), 2)
                act.activation(dW, cs, ACT.Exp, scale=-RW_DECAY)
                act.activation(sig, sig, ACT.Exp, scale=-RW_DECAY).then_inc(sem("rw_exps"), 1)
                act.wait_ge(sem("rw_exps"), 1)
                act.activation(cs, cs, ACT.Exp, scale=RW_DECAY).then_inc(sem("rw_exps"), 1)

            def rw_gout():
                act.wait_ge(sem("rw_g_mm"), 1)
                act.activation(gl, sm[:, 0:2, :].rearrange("p b t -> p (b t)"), cp).then_inc(sem("rw_g_out"), 1)
                act.wait_ge(sem("rw_kk_mm"), 1)
                act.activation(bonus, sm[:, 2:4, :].rearrange("p b t -> p (b t)"), ACT.Sqrt) \
                   .then_inc(sem("rw_kk_norm"), 1)

            def wide(b, w=64):
                return sm[:, b:b + 2, :].rearrange("p b (g t) -> p (b g) t", t=w)

            def rw_v_out():
                act.wait_ge(sem("rw_s3_mm"), 2)
                act.activation(g16(Vt), wide(2), cp).then_inc(sem("rw_v_out"), 1)

            def rw_c_out():
                act.wait_ge(sem("rw_s4_mm"), 2)
                act.activation(g16(Ct), wide(2), cp).then_inc(sem("rw_s4_out"), 1)

            def quad(base, off):
                return sm[:, base:base + 2, off:off + 128]

            q2 = lambda a: a.rearrange("p (b t) -> p b t", b=2)

            def rw_rhs_out(c):
                act.wait_ge(sem("rw_rhs_mm"), c + 1)
                act.activation(q2(X0), quad(0, 0), cp).then_inc(sem("rw_rhs_out"), 1)

            def rw_y_out(c):
                act.wait_ge(sem("rw_y_mm"), c + 1)
                for b in range(2):
                    mm = act.activation(g16(Yc).rearrange("p (i c) t -> p i c t", c=4)[:, 2 * b:2 * b + 2, c, :],
                                        sm[:, b, 128:256].rearrange("p (j t) -> p j t", t=64), cp)
                mm.then_inc(sem("rw_y_out"), 1)

            def rw_finish():
                act.wait_ge(sem("rw_yc"), 1)
                act.activation(Xm, Yc, ACT.Square).then_inc(sem("rw_ysq"), 1)

            def rw_finish2():
                act.wait_ge(sem("rw_var"), 1)
                act.activation(Nm, Nm, ACT.Sqrt).then_inc(sem("rw_std"), 1)

            def nsa_kx():
                act.wait_ge(sem("nsa_dupk_mm"), 1)
                act.wait_ge(sem("zeroed"), 1)
                for h in range(2):
                    r = slice(64 * h, 64 * h + 64)
                    for b in range(2):
                        mm = act.activation(kx[r, b, :, h, :], sm[r, 4 + b, :].rearrange("p (g t) -> p g t", g=2), cp)
                mm.then_inc(sem("nsa_kx"), 1)

            def nsa_vt():
                act.wait_ge(sem("nsa_vtok_mm"), 1)
                act.activation(vtok.rearrange("p b s c -> p (b s c)"), sm[:, 4, :], cp).then_inc(sem("nsa_vtok"), 1)

            def nsa_vcx():
                act.wait_ge(sem("nsa_cmp_mm"), 2)
                for h in range(2):
                    r = slice(32 * h, 32 * h + 32)
                    mm = act.activation(vcx[r, :, 64 * h:64 * h + 64],
                                        sm[r, 5, 0:128].rearrange("p (g t) -> p g t", g=2), cp)
                mm.then_inc(sem("nsa_vcx"), 1)

            def nsa_cmp_exp():
                act.wait_ge(sem("nsa_cmp_arg"), 1)
                act.activation(esc, esc, ACT.Exp, scale=NSA_SCALE).then_inc(sem("nsa_cmp_e"), 1)

            def nsa_pcT():
                act.wait_ge(sem("nsa_cmpT_mm"), 1)
                act.activation(pcT, sm[0:64, 4:6, :].rearrange("p b (q t) -> p (b q) t", t=T), cp) \
                   .then_inc(sem("nsa_pcT"), 1)

            def unit_exp(u):
                act.wait_ge(sem("nsa_max"), u + 1)
                if u:
                    act.wait_ge(sem("nsa_T_mm"), u)
                for h in range(2):
                    act.activation(pu[:, h * P:(h + 1) * P], sm[:, 0, h * P:(h + 1) * P], ACT.Exp,
                                   bias=unb[:, h:h + 1], scale=NSA_SCALE, accum_out=usum[:, h:h + 1])
                for h in range(2):
                    mm = act.activation(pu[:, 256 + h * T:256 + (h + 1) * T], sm[:, 1, h * T:(h + 1) * T], ACT.Exp,
                                        bias=unb[:, 2 + h:3 + h], scale=NSA_SCALE, accum_out=usum[:, 2 + h:3 + h])
                mm.then_inc(sem("nsa_p"), 1)

            def unit_pT(u):
                act.wait_ge(sem("nsa_T_mm"), u + 1)
                if u:
                    act.wait_ge(sem("nsa_pv_mm"), u)
                act.activation(pT[:, 0:512], sm[:, 2, :], cp)
                act.activation(pT[:, 512:768], sm[:, 3, 0:256], cp).then_inc(sem("nsa_pT"), 1)
                if u % 2 == 0 and u:
                    unit_o(u // 2 - 1)

            def unit_o(q):
                act.wait_ge(sem("nsa_pv_mm"), 2 * q + 2)
                act.activation(obr[:, 16 + q, :], sm[:, 4 + q % 2, 0:T], cp).then_inc(sem("nsa_o"), 1)
            def obr_high(a, n, x, name, need):
                act.wait_ge(sem(name), need)
                act.activation(X2[:, x:x + n, 0:T], obr[:, a:a + n, :], cp).then_inc(sem("obr_high"), 1)

            def ret_o():
                act.wait_ge(sem("ret_mm"), 3)
                act.activation(oc.rearrange("p i t -> p (i t)"), sm[:, 0:4, :].rearrange("p b t -> p (b t)"), cp) \
                   .then_inc(sem("ret_scalar"), 1)

            def ret_sq():
                act.wait_ge(sem("ret_vector"), 2)
                act.activation(osq, oc, ACT.Square).then_inc(sem("ret_scalar"), 1)

            def ret_std():
                act.wait_ge(sem("ret_vector"), 3)
                act.activation(rstd4, rstd4, ACT.Sqrt).then_inc(sem("ret_scalar"), 1)

            half_loaded, half_used = [sem(f"half_loaded{i}") for i in range(4)], sem("half_used")
            one = lambda k, v: v

            def high(m, h, at, n=8):
                act.wait_ge(half_loaded[2 * (m % 2) + h], at(8, 16 * (m // 2 + 1)))
                if m >= 2:
                    act.wait_ge(half_used, at(2, 2 * m + h - 3))
                act.activation(wsplit[(2 * m + h) % 4][:, 0, 0:n, :], raw[:, m % 2, h, 0:n, :], cp)                    .then_inc(sem("hi_done"), 1)

            def width(m, h):
                return (((4, 4), (8, 4))[m % 2])[h] if m < M_LOOP else 8

            steps = {
                ("sc", 0): [rw_lora_in, rw_sigmoids], ("sc", 1): [rw_exps, rw_gout], 
                ("sc", 5): [rw_v_out], ("sc", 6): [rw_c_out],
                ("kv", 5): [lambda: rw_rhs_out(0)], ("cmp", 1): [lambda: rw_y_out(0)],
                ("cmp", 2): [nsa_kx, lambda: rw_rhs_out(1)], ("q", 0): [lambda: rw_y_out(1), nsa_vt],
                ("q", 1): [lambda: rw_rhs_out(2)], ("q", 2): [nsa_vcx], ("q", 3): [lambda: rw_y_out(2)],
                ("gate", 0): [lambda: rw_rhs_out(3)], ("rq", 0): [nsa_cmp_exp], ("rq", 1): [lambda: rw_y_out(3)],
                ("rq", 2): [rw_finish, nsa_pcT], ("rq", 3): [rw_finish2],
                ("g0", 4): [ret_o], ("g0", 7): [ret_sq], ("g0", 9): [ret_std],
                ("g0", 1): [lambda: obr_high(0, 4, 8, "sc_done", 4)], ("g0", 2): [lambda: obr_high(4, 4, 12, "rw_done", 1)],
                ("g0", 3): [lambda: obr_high(16, 4, 16, "nsa_o", 4)],
            }
            order = [c for c in MIX if c[0] in ("rk", "rv", "rg")]
            for u in range(8):
                steps.setdefault(order[2 * u + 1], []).append(lambda u=u: unit_exp(u))
                steps.setdefault(order[2 * u + 2], []).append(lambda u=u: unit_pT(u))
            steps.setdefault(order[18], []).append(lambda: unit_o(3))
            for n, (what, i) in enumerate(MIX):
                for s in steps.get((what, i), []):
                    s()
                if what == "rw":
                    t = i if i < 12 else i + 2
                    if n == 0:
                        act.wait_ge(sem("h_ready"), 4)
                    chunk(n, zp[:, t, 1:257])
                elif what in ("zw", "za"):
                    chunk(n, zp[0:96, 12 + (what == "za"), 1:257], big[0:96, n % 2, :])
                elif what == "sc":
                    if i >= 6 and i % 3 == 0:
                        act.wait_ge(sem("sc_done"), i // 3 - 1)
                    chunk(n, scb[:, i // 3 % 2, i % 3, :])
                elif what == "kv":
                    chunk(n, kvr[:, i, :])
                elif what == "cmp":
                    act.wait_ge(used, n + 1)
                    kv, ht = divmod(i, 2)
                    if kv:
                        act.wait_ge(sem("zeroed"), 1)
                        src = big[:, n % 2, 0:30].rearrange("p (g c) -> p g c", g=2)
                        act.activation(hidV[:, ht, :, 0, 0:NCMP], src, ACT.Gelu_apprx_tanh).then_inc(outd, 1)
                    else:
                        act.activation(hidK[:, ht, :], big[:, n % 2, 0:30], ACT.Gelu_apprx_tanh).then_inc(outd, 1)
                elif what == "q":
                    chunk(n, qn[:, i, :])
                elif what == "gate":
                    chunk(n, gsig[0:24, :], big[0:24, n % 2, :], ACT.Sigmoid)
                elif what == "rq":
                    if i == 0:
                        act.wait_ge(sem("rw_x_ready"), 6)
                    chunk(n, rqk[:, i, :])
                elif what == "rk":
                    chunk(n, rqk[:, 4 + i, :])
                elif what == "rv":
                    if i == 0:
                        act.wait_ge(sem("rw_done"), 1)
                    chunk(n, rv[:, :, i * P:(i + 1) * P], big[:, n % 2, :].rearrange("p (s c) -> p s c", s=2))
                elif what == "rg":
                    chunk(n, rg[:, i, :], func=ACT.Silu)
                elif what == "g0":
                    if i == 4 * G0_TILES - 1:
                        obr_high(8, 8, 0, "ret_vector", 4)
                        high(0, 0, one, 4)
                        high(0, 1, one, 4)
                    if i == 0:
                        act.wait_ge(sem("nsa_pv_mm"), 8)
                    chunk(n, g0[:, i // 4, i % 4, :], func=ACT.Sigmoid)

            def cross_out(m, at, b):
                act.wait_ge(half_used, at(2, 2 * m + 2))
                act.activation(cross[:, b, :], bank[:, b, T:2 * T], cp).then_inc(sem("cross_out"), 1)

            def branch_cross(m, at, x):
                act.wait_ge(half_used, at(2, 2 * m + 2))
                act.activation(bcross[:, x], sm[:, 2 * x:2 * x + 2, T:2 * T], cp).then_inc(sem("branch_cross"), 1)

            def quarters(dst, src, need, first, done):
                for q in range(4):
                    act.wait_ge(sem(need), first + q)
                    act.activation(dst[:, 4 * q:4 * q + 4, 0:T], src[:, 4 * q:4 * q + 4, :], cp).then_inc(sem(done), 1)

            high(1, 0, one, 8)
            high(1, 1, one, 4)
            for t in range(G0_TILES):
                for x in range(2):
                    m = 2 * t + x
                    high(m + 2, 0, one, width(m + 2, 0))
                    branch_cross(m, one, x)
                    high(m + 2, 1, one, width(m + 2, 1))
                for q in (2 * t, 2 * t + 1) if t < 2 else ():
                    act.activation(X1[:, 4 * q:4 * q + 4, 0:T], hT[:, 4 * q:4 * q + 4, :], cp) \
                       .then_inc(sem("stream_high"), 1)
            def merged_high(q):
                act.wait_ge(sem("merged"), 4 * q + 4)
                act.activation(X1[:, 4 * q:4 * q + 4, 0:T], merged[:, 4 * q:4 * q + 4, :], cp) \
                   .then_inc(sem("stream_high"), 1)

            def merge(i, tiles):
                at = lambda k, v: i * (12 * k) + v
                for t in range(tiles):
                    for j in range(6):
                        m = M_LOOP + 6 * t + j
                        high(m + 2, 0, at)
                        if j < 4:
                            cross_out(m, at, j % 2)
                        else:
                            if j == 4:
                                act.wait_ge(sem("prod_out"), i * 8 + (2 + 4 * t + 4))
                                act.activation(gts[:, t], gts[:, t], ACT.Sigmoid).then_inc(sem("gates"), 1)
                            branch_cross(m, at, j - 4)
                        high(m + 2, 1, at)
                        if tiles == 1 and j == 4:
                            for q in range(3):
                                merged_high(q)

            with act.Fori(0, PAIRS) as i:
                merge(i, 2)
            merge(PAIRS, 1)

            def std(k):
                act.wait_ge(sem("norm_var"), k)
                act.activation(rstd[:, :], rstd[:, :], ACT.Sqrt).then_inc(sem("norm_std"), 1)

            def position(m, at):
                high(m + 2, 0, at)
                cross_out(m, at, m % 2)
                high(m + 2, 1, at)

            merged_high(3)
            for j in range(KT):
                position(M_WOUT + j, one)
                if j < 4:
                    if j == 0:
                        act.wait_ge(sem("stream_split"), 8)
                        act.wait_ge(sem("mem_loaded"), 16)
                    act.activation(msq[:, 4 * j:4 * j + 4, :], memn[:, 4 * j:4 * j + 4, :], ACT.Square) \
                       .then_inc(sem("res_sq"), 1)
                elif j == 7:
                    std(2)
                elif 8 <= j < 12:
                    q = j - 8
                    act.wait_ge(sem("mem_n"), q + 1)
                    act.activation(X2[:, 4 * q:4 * q + 4, 0:T], memn[:, 4 * q:4 * q + 4, :], cp) \
                       .then_inc(sem("stream_high"), 1)
            for j in range(KT):
                position(M_MK + j, one)
                if j == 1:
                    std(3)
                elif 2 <= j < 6:
                    q = j - 2
                    act.wait_ge(sem("res_ready"), q + 1)
                    act.activation(yT[:, 4 * q:4 * q + 4, :], res[:, 4 * q:4 * q + 4, :], ACT.Square) \
                       .then_inc(sem("res_sq"), 1)
                elif j == 9:
                    std(4)
                elif 11 <= j < 15:
                    q = j - 11
                    act.wait_ge(sem("h_ready"), q + 5)
                    act.activation(X1[:, 4 * q:4 * q + 4, 0:T], yT[:, 4 * q:4 * q + 4, :], cp) \
                       .then_inc(sem("stream_high"), 1)

            def loop(base, count):
                with act.Fori(0, count) as i:
                    for j in range(4):
                        position(base + j, lambda k, v: i * (4 * k) + v)

            def v_out(j):
                act.wait_ge(sem("v_T_mm"), j + 1)
                act.activation(memV[:, :, j * P:(j + 1) * P], sm[:, j % 2, 0:T].rearrange("p (s t) -> p s t", s=2), cp) \
                   .then_inc(sem("v_out"), 1)

            def softmax(h):
                act.wait_ge(sem("ma_max"), h + 1)
                if h:
                    act.wait_ge(sem("ma_T_mm"), h)
                for s in range(2):
                    mm = act.activation(pm[:, s, :], sm[:, h % 2, s * T:(s + 1) * T], ACT.Exp,
                                        bias=mnb[:, s:s + 1], scale=MEM_DH ** -0.5, accum_out=msum[:, s:s + 1])
                mm.then_inc(sem("ma_p"), 1)

            def turned(h):
                act.wait_ge(sem("ma_T_mm"), h + 1)
                act.activation(pmT[:, h % 2].rearrange("p s t -> p (s t)"), sm[:, 2, :], cp).then_inc(sem("ma_pT"), 1)

            def values_high(h):
                act.wait_ge(sem("ma_o_mm"), h + 1)
                act.activation(X2[:, 4 * h:4 * h + 4, 0:T], sm[:, 3:5, :].rearrange("p b (k t) -> p (b k) t", t=T), cp) \
                   .then_inc(sem("ma_o_high"), 1)

            for j in range(KT):
                position(M_MV + j, one)
                if j:
                    v_out(j - 1)
            for j in range(KT):
                position(M_WQ + j, one)
                if j == 0:
                    v_out(KT - 1)
                if j >= 8 and j % 4 == 0:
                    values_high(j // 4 - 2)
                elif j >= 4 and j % 4 == 1:
                    softmax(j // 4 - 1)
                elif j >= 4 and j % 4 == 3:
                    turned(j // 4 - 1)
            values_high(2)
            softmax(3)
            turned(3)
            values_high(3)
            loop(M_WO, 4)
            std(5)
            for q in range(4):
                act.wait_ge(sem("res_ready"), 4 + q + 1)
                act.activation(yT[:, 4 * q:4 * q + 4, :], res[:, 4 * q:4 * q + 4, :], ACT.Square).then_inc(sem("res_sq"), 1)
            std(6)
            quarters(X1, yT, "h_ready", 9, "stream_high")
            w2, b0 = VEC_AT["ffn_conv_w"][0] + 176, VEC_AT["ffn_conv_b"][0]
            for first, count, g in ((0, 4, gA), (4, 18, gB)):
                with act.Fori(0, count) as i:
                    for p in range(2):
                        for s in range(2):
                            j = 2 * p + s
                            m = M_UP + 4 * first + j
                            at = lambda k, v: i * (4 * k) + v
                            col = lambda w: vec[:, bass.ds(i * 4 + (w + 4 * first + j), 1)]
                            high(m + 2, 0, at)
                            cross_out(m, at, s)
                            if s == 1:
                                act.wait_ge(sem("ffn_tap"), at(2, 2 * (4 * first + j)))
                                act.activation(ub[:, p, 0, :], ub[:, p, 0, :], ACT.Gelu_apprx_tanh) \
                                   .then_inc(sem("ffn_act"), 1)
                            high(m + 2, 1, at)
                            act.wait_ge(sem("prod_out"), at(1, m - R_OFF + 1))
                            act.activation(ub[:, p, s, :], rawu[:, s, :], ACT.Identity, bias=col(b0), scale=col(w2)) \
                               .then_inc(sem("ffn_last_tap"), 1)
                        act.wait_ge(sem("ffn_product"), i * 2 + (2 * first + p + 1))
                        act.activation(g[:, bass.ds(i * 2 + p, 1), 0:T], gtmp.unsqueeze(1), cp).then_inc(sem("g_high"), 1)

            def down(i, ahead):
                for t in range(2):
                    for j in range(4):
                        m = M_DOWN + 4 * t + j
                        at = lambda k, v: i * (8 * k) + v
                        if m + 2 < ahead:
                            high(m + 2, 0, at)
                        if j == 3:
                            cross_out(m, at, t)
                        if m + 2 < ahead:
                            high(m + 2, 1, at)

            with act.Fori(0, 7) as i:
                down(i, M_END)
            down(7, M_DOWN + 8)
            std(7)

        @block.gpsimd
        def _(pool):
            count = [0]

            def link(ins):
                count[0] += 1
                ins.then_inc(sem("pool_step"), 1)
                pool.wait_ge(sem("pool_step"), count[0])

            for z in (kcx, hidV[:, :, :, :, :], vcx[:, :, :], kx):
                link(pool.memset(z, 0.0))
            pool.memset(seg, 1.0).then_inc(sem("zeroed"), 1)
            pool.wait_ge(sem("zeroed"), 1)
            link(pool.memset(g16(seg)[:, :, 0:1], 0.0))
            pool.wait_ge(sem("h_ready"), 4)
            pool.memset(zp[:, :, 0:1], 0.0).then_inc(sem("zeroed"), 1)
            pool.wait_ge(sem("zeroed"), 2)
            for a, b, rows, last in ((0, 8, P, ("rw", 7)), (8, 12, P, ("rw", 11)), (12, 14, 96, ("za", 0)),
                                     (14, 16, P, ("rw", 13))):
                pool.wait_ge(sem("chunk_out"), AT[last] + 1)
                pool.tensor_tensor(Z[0:rows, a:b, :], zp[0:rows, a:b, 0:256], zp[0:rows, a:b, 1:257], SUB) \
                    .then_inc(sem("rw_diff"), 1)
            pool.wait_ge(sem("rw_kk"), 1)
            pool.tensor_tensor(tmp, kk, kk, MUL).then_inc(sem("rw_kk_sq"), 1)

            def short_conv(i):
                b, c, x, t = [scb[:, i % 2, s, :] for s in range(4)]
                w = [vv("sc_conv", 4 * j + i) for j in range(3)]
                pool.wait_ge(sem("chunk_out"), AT[("sc", 3 * i + 2)] + 1)
                link(pool.tensor_tensor(c, c, x, MUL))
                link(pool.tensor_scalar(x, c, w[2], None, MUL))
                link(pool.tensor_scalar(t, c, w[1], None, MUL))
                link(pool.tensor_tensor(x[:, 1:], x[:, 1:], t[:, :T - 1], ADD))
                link(pool.tensor_scalar(t, c, w[0], None, MUL))
                link(pool.tensor_tensor(x[:, 2:], x[:, 2:], t[:, :T - 2], ADD))
                pool.tensor_tensor(obr[:, i, :], x, b, MUL).then_inc(sem("sc_done"), 1)

            for i in range(4):
                short_conv(i)
            pool.wait_ge(sem("sc_done"), 4)
            pool.sem_inc(sem("branches"), 1)
            pool.wait_ge(sem("chunk_out"), AT[("cmp", 3)] + 1)
            pool.tensor_copy(hidV[:, :, :, 1, :].rearrange("p k g c -> p (k g) c"),
                             hidV[:, :, :, 0, :].rearrange("p k g c -> p (k g) c")).then_inc(sem("nsa_hidV"), 1)
            pool.wait_ge(sem("rw_x_ready"), 6)
            pool.memset(pcs, 0.0).then_inc(sem("pcs_zeroed"), 1)
            pool.wait_ge(sem("chunk_out"), AT[("rk", 3)] + 1)
            pool.wait_ge(sem("rw_done"), 1)
            pool.tensor_tensor(rt1, rqk, bc(trig[:, 0, 0, :], 8), MUL).then_inc(sem("ret_cos"), 1)

            def sum_quarters(x, need, first, done):
                for q in range(1, 4):
                    pool.wait_ge(sem(need), first + q)
                    ins = pool.tensor_tensor(x[:, 0:4, :], x[:, 0:4, :], x[:, 4 * q:4 * q + 4, :], ADD)
                    if q < 3:
                        link(ins)
                ins.then_inc(sem(done), 1)

            def y_tile(step, i, n, value, tile):
                pool.wait_ge(sem("prod_out"), value)
                pool.tensor_tensor(sq[:, n % 2:n % 2 + 1, :], tile, tile, MUL).then_inc(sem("y_sq"), 1)
                pool.wait_ge(sem("y_sq"), i + (16 * step + n + 1))
                pool.wait_ge(sem("y_acc"), i + (17 * step + n + 1))
                pool.tensor_tensor(acc.unsqueeze(1), acc.unsqueeze(1), sq[:, n % 2:n % 2 + 1, :], ADD).then_inc(sem("y_acc"), 1)

            pool.wait_ge(sem("branches"), 4)
            pool.memset(acc, 0.0).then_inc(sem("y_acc"), 1)
            for j in range(KT):
                y_tile(0, 0, j, M_WOUT + j - R_OFF + 1, yT[:, j:j + 1, :])
                if j == 4:
                    sum_quarters(msq, "res_sq", 1, "quarter_sums")
            sum_quarters(yT, "res_sq", 5, "quarter_sums")
            pool.wait_ge(sem("prod_out"), M_WO - R_OFF)
            pool.memset(acc, 0.0).then_inc(sem("y_acc"), 1)
            with pool.Fori(0, 4) as i:
                for j in range(4):
                    y_tile(1, i * 4, j, i * 4 + (M_WO + j - R_OFF + 1), yT[:, bass.ds(i * 4 + j, 1), :])
            for first, rounds, g in ((0, 4, gA), (4, 18, gB)):
                with pool.Fori(0, rounds) as i:
                    for p in range(2):
                        pair = 2 * first + p + 1
                        pool.wait_ge(sem("ffn_act"), i * 2 + pair)
                        pool.wait_ge(sem("ffn_tap"), i * 8 + 4 * pair)
                        pool.tensor_tensor(gtmp, ub[:, p, 0, :], ub[:, p, 1, :], MUL).then_inc(sem("ffn_product"), 1)
                        pool.wait_ge(sem("ffn_product"), i * 2 + pair)
                        pool.wait_ge(sem("g_high"), i * 2 + pair)
                        gt = bass.ds(i * 2 + p, 1)
                        pool.tensor_tensor(g[:, gt, T:2 * T], gtmp.unsqueeze(1), g[:, gt, 0:T].bitcast(f32), SUB)                             .then_inc(sem("g_split"), 1)
                        pool.wait_ge(sem("g_split"), i * 2 + pair)
            pool.wait_ge(sem("prod_out"), R_DOWN)
            pool.memset(acc, 0.0).then_inc(sem("y_acc"), 1)
            with pool.Fori(0, 4) as i:
                for j in range(4):
                    y_tile(2, i * 4, j, i * 4 + (R_DOWN + j + 1), yD[:, bass.ds(i * 4 + j, 1), :])

        @block.vector
        def _(dve):
            count = [0]

            def link(ins):
                count[0] += 1
                ins.then_inc(sem("dve_step"), 1)
                dve.wait_ge(sem("dve_step"), count[0])

            def mark(ins, name, n):
                ins.then_inc(sem(name), 1)
                dve.wait_ge(sem(name), n)

            stt, tt, ts = dve.scalar_tensor_tensor, dve.tensor_tensor, dve.tensor_scalar

            def inv_std(k):
                dve.wait_ge(sem("norm_mm"), k)
                mark(ts(rstd[:, :], sm[:, 5, 0:T], 1.0 / D, EPS, MUL, ADD), "norm_var", k)
                dve.wait_ge(sem("norm_std"), k)
                link(dve.reciprocal(rstd[:, :], rstd[:, :]))

            def scaled_quarter(dst, src, q, name, done, n):
                for k in range(4 * q, 4 * q + 4):
                    mm = stt(dst[:, k, :], src[:, k, :], vv(name, k), rstd[:, :], MUL, MUL)
                mark(mm, done, n)

            inv_std(1)
            for q in range(4):
                scaled_quarter(hT, xT, q, "ln_mix_pre", "h_ready", q + 1)
            dve.wait_ge(sem("pos_loaded"), 16)
            dve.wait_ge(sem("consts_loaded"), 16 * 2)
            link(dve.tensor_copy(posf[:, :], posi[:, :]))
            for a, name in enumerate(("inv_ret", "inv_nsa")):
                link(ts(trig[:, a], bc(posf[:, :], 2), cc(name), None, MUL))
            link(ts(kmul[:, :, 0], trig[:, :, 0], 1 / (2 * math.pi), 0.25, MUL, ADD))
            link(ts(kmul[:, :, 1], trig[:, :, 1], 1 / (2 * math.pi), None, MUL))
            link(ts(kmul, kmul, MAGIC, None, ADD))
            link(ts(kmul, kmul, MAGIC, None, SUB))
            link(ts(kmul[:, :, 0], kmul[:, :, 0], 0.25, None, SUB))
            tf = trig[:, :, :, :].rearrange("p a b t -> p (a b t)")
            kf = kmul.rearrange("p a b t -> p (a b t)")
            for c in TWO_PI:
                link(stt(tf, kf, -c, tf, MUL, ADD))
            mark(ts(tf, tf, 3.1415925, -3.1415925, MIN, MAX), "trig_arg", 1)

            for m, (a, b, rows, n) in enumerate(((0, 8, P, 1), (8, 12, P, 2), (12, 14, 96, 3), (14, 16, P, 4))):
                dve.wait_ge(sem("rw_diff"), n)
                for i in range(a, b):
                    mm = stt(Z[0:rows, i, :], Z[0:rows, i, :], vv("rw_mu", i, rows=rows), zp[0:rows, i, 1:257], MUL, ADD)
                if m != 2:
                    mm.then_inc(sem("rw_mixed"), 1)
                if m == 0:
                    dve.wait_ge(sem("rw_mixed"), 1)
                    for i in range(4):
                        mm = ts(s4(kk)[:, i, :], s4(Zk)[:, i, :], vv("rw_k_k", i), None, MUL)
                    mark(mm, "rw_kk", 1)
            dve.wait_ge(sem("rw_mixed"), 3)
            dve.wait_ge(sem("rw_sigmoids"), 1)
            mark(dve.tensor_tensor_scan(cs, seg, sig, 0.0, MUL, ADD), "rw_cum", 1)
            mark(tt(sig, cs, sig, SUB), "rw_cum", 2)
            dve.wait_ge(sem("rw_kk_norm"), 1)
            link(ts(bonus, bonus, 1e-12, None, MAX))
            link(dve.reciprocal(bonus, bonus))
            link(tt(kk, kk, bonus, MUL))
            for i in range(4):
                mm = ts(s4(tmp)[:, i, :], s4(aa)[:, i, :], -1.0, vv("rw_k_a", i), ADD, MUL)
            link(mm)
            link(stt(Zk, tmp, 1.0, Zk, ADD, MUL))
            dve.wait_ge(sem("rw_exps"), 2)
            tt(QR[:, :, 0, :], g16(kk), g16(sig), MUL)
            link(tt(QR[:, :, 1, :], g16(Zr), g16(dW), MUL))
            for i in range(4):
                mm = stt(s4(Zr)[:, i, :], s4(Zr)[:, i, :], vv("rw_r_k", i), s4(Zk)[:, i, :], MUL, MUL)
            mark(mm, "rw_rk", 1)
            link(tt(kk, kk, aa, MUL))
            tt(Bd, kk, cs, MUL)
            tt(Cd, Zk, cs, MUL)
            mark(dve.tensor_copy(WC.unsqueeze(2), g16(dW)[:, :, 63:64]), "rw_operands", 1)
            dve.wait_ge(sem("rw_bonus_mm"), 1)
            mark(tt(bonus, sm[:, 0:2, :].rearrange("p b t -> p (b t)"), Zv, MUL), "rw_bonus_out", 1)

            def obr_low(a, n, x, need):
                dve.wait_ge(sem("obr_high"), need)
                tt(X2[:, x:x + n, T:2 * T], obr[:, a:a + n, :], X2[:, x:x + n, 0:T].bitcast(f32), SUB) \
                    .then_inc(sem("obr_split"), 1)

            def masked(dst, src, name):
                return tt(g16(dst), src, bc(cc(name), 16), MUL)

            def wide(b):
                return sm[:, b:b + 2, :].rearrange("p b (g t) -> p (b g) t", t=64)

            quarter = sm[:, 0:4, :].rearrange("p b (g two t) -> p (b g) two t", two=2, t=64)
            dve.wait_ge(sem("rw_s1_mm"), 1)
            stt(g16(M1), quarter[:, :, 1, :], -1.0, bc(cc("incl"), 16), MUL, MUL)
            mark(dve.tensor_copy(g16(Nm), quarter[:, :, 0, :]), "rw_s1_out", 1)
            link(masked(P1, g16(Nm), "up0"))
            tt(g16(Xm), bc(cc("eye64"), 16), g16(P1), SUB)
            dve.wait_ge(sem("rw_s2_mm"), 1)
            masked(L2, quarter[:, :, 0, :], "strict")
            mark(masked(M2, quarter[:, :, 1, :], "incl"), "rw_s2_out", 1)
            dve.wait_ge(sem("rw_s3_mm"), 1)
            mark(dve.tensor_copy(g16(Lm), wide(0)), "rw_l_out", 1)
            link(masked(Zm, g16(Lm), "low0"))
            mark(tt(g16(Zm), bc(cc("eye64"), 16), g16(Zm), SUB), "rw_x_ready", 1)
            dve.wait_ge(sem("rw_s4_mm"), 2)
            ts(g16(Bt), wide(0), -1.0, None, MUL).then_inc(sem("rw_s4_out"), 1)

            def level(n):
                dve.wait_ge(sem("rw_p1_mm"), n)
                masked(P1, wide(0), f"up{n}").then_inc(sem("rw_p1_out"), 1)
                dve.wait_ge(sem("rw_p2_mm"), 2 * n - 1)
                mm = tt(g16(Xm), g16(Xm), wide(2), SUB)
                if n < 5:
                    dve.wait_ge(sem("rw_p2_mm"), 2 * n)
                    mm = tt(g16(Zm), g16(Zm), wide(0), SUB)
                mark(mm, "rw_x_ready", n + 1)

            def nsa_blocks():
                dve.wait_ge(sem("nsa_dup_mm"), 1)
                for kv in range(2):
                    src = sm[:, 4 + kv, :].rearrange("p (g c l o) -> p g c l o", g=2, l=8, o=2)
                    for o in range(2):
                        r = slice(64 * o, 64 * o + 64)
                        for hi in range(2):
                            for g in range(2):
                                pos = vv("cmp_pos", 16 * kv + 8 * hi, 8)[r]
                                mm = tt(blk[r, kv, 8 * hi:8 * hi + 8, g, :],
                                        src[r, g, hi:hi + NCMP, :, o].rearrange("p c l -> p l c"),
                                        bl(pos, NCMP), ADD)
                    mm.then_inc(sem("nsa_blk"), 1)

            def u_out(c):
                dve.wait_ge(sem("rw_u_mm"), c + 1)
                dve.tensor_copy(q2(U), sm[:, 2:4, 0:128]).then_inc(sem("rw_u_out"), 1)

            q2 = lambda a: a.rearrange("p (b t) -> p b t", b=2)
            wc = WC.rearrange("p (i c) -> p i c", c=4)

            def state(c):
                dve.wait_ge(sem("rw_ds_mm"), c + 1)
                dve.wait_ge(sem("rw_y_mm"), c + 1)
                if c:
                    link(tt(q2(S0), q2(S0), sm[:, 2:4, 128:256], ADD))
                else:
                    link(dve.tensor_copy(q2(S0), sm[:, 2:4, 128:256]))
                s = S0.rearrange("p (i v) -> p i v", v=64)
                mark(tt(s, s, bl(wc[:, :, c], 64), MUL), "rw_state", c + 1)

            def rope_k():
                dve.wait_ge(sem("nsa_rope_mm"), 1)
                t = scr[:, 0:512].rearrange("p (a t) -> p a t", t=T)
                tt(t, sm[:, 4, :].rearrange("p (a t) -> p a t", t=T), bc(trig[:, 1, 1, :], 2), MUL)
                k = kvr.rearrange("p (a b) t -> p a b t", b=2)[:, 1:3, 0, :]
                link(tt(k, k, bc(trig[:, 1, 0, :], 2), MUL))
                mark(tt(k, k, t, ADD), "nsa_k_roped", 1)

            def kc_out():
                dve.wait_ge(sem("nsa_cmp_mm"), 1)
                mark(dve.tensor_copy(kc0, sm[:, 4, 0:30]), "nsa_kc0", 1)

            def at_end(a):
                e = trig[:, 1, a, :].rearrange("p (c l) -> p c l", l=16)[:, 1:16, 15]
                return bc(e, 2)

            def kc_rope():
                dve.wait_ge(sem("nsa_rope_mm"), 2)
                two = lambda a: a.rearrange("p (g c) -> p g c", g=2)
                tt(two(krt), two(sm[:, 4, 64:94]), at_end(1), MUL)
                link(tt(two(kcr), two(kc0), at_end(0), MUL))
                link(tt(kcr, kcr, krt, ADD))
                dve.tensor_copy(kcx[0:64, :, 0, :], two(kcr)[0:64])
                dve.tensor_copy(kcx[64:128, :, 1, :], two(kcr)[64:128]).then_inc(sem("nsa_kcx"), 1)

            def rope_q():
                dve.wait_ge(sem("nsa_rope_mm"), 3)
                t = s4(scr)
                tt(t, sm[:, 4:6, :].rearrange("p b (i t) -> p (b i) t", t=T), bc(trig[:, 1, 1, :], 4), MUL)
                link(tt(qn, qn, bc(trig[:, 1, 0, :], 4), MUL))
                mark(tt(qn, qn, t, ADD), "nsa_q_roped", 1)

            e5 = esc.rearrange("p (q s h) c -> p q s h c", q=4, s=2)

            def cmp_arg():
                dve.wait_ge(sem("nsa_cmps_mm"), 1)
                link(dve.tensor_copy(gtok.rearrange("p s c -> p (s c)"), sm[:, 5, 256:304]))
                src = sm[:, 4, 0:240].rearrange("p (q s h c) -> p q s h c", q=4, s=2, h=2)
                for s in range(2):
                    for h in range(2):
                        mm = tt(e5[:, :, s, h, :], src[:, :, s, h, :], bc(cc("cmp_neg")[:, 15 * s:15 * s + 15], 4), ADD)
                link(mm)
                link(dve.tensor_reduce(cmx, esc, AX.X, MAX))
                mark(tt(esc, esc, bl(cmx, 15), SUB), "nsa_cmp_arg", 1)

            def cmp_p():
                dve.wait_ge(sem("nsa_cmp_e"), 1)
                for s in range(2):
                    for h in range(2):
                        mm = tt(e5[:, :, s, h, :], e5[:, :, s, h, :], bc(cc("cmp_seen")[:, 15 * s:15 * s + 15], 4), MUL)
                link(mm)
                link(dve.tensor_reduce(csum, esc, AX.X, ADD))
                link(ts(csum, csum, 1e-30, None, MAX))
                link(dve.reciprocal(csum, csum))
                c4 = csum.rearrange("p (q s h) -> p q s h", q=4, s=2)
                g = gtok.rearrange("p s (q h b) -> p s q h b", h=2, b=3)
                for s in range(2):
                    mm = tt(c4[:, :, s, :], c4[:, :, s, :], g[:, s, :, :, 0], MUL)
                link(mm)
                dve.wait_ge(sem("pcs_zeroed"), 1)
                mark(tt(pcs[:, :, 0:15], esc, bl(csum, 15), MUL), "nsa_pcs", 1)

            def unit_max(u):
                dve.wait_ge(sem("nsa_s_mm"), u + 1)
                two = lambda a: a.rearrange("p (h t) -> p h t", h=2)
                t0, t1 = two(sm[:, 0, 0:256]), two(sm[:, 1, :])
                tt(t0, t0, bc(cc("causal"), 2), ADD)
                link(tt(t1[:, :, P:T], t1[:, :, P:T], bc(cc("causal"), 2), ADD))
                dve.tensor_reduce(umax[:, 0:2], t0, AX.X, MAX)
                link(dve.tensor_reduce(umax[:, 2:4], t1, AX.X, MAX))
                mark(ts(unb, umax, -NSA_SCALE, None, MUL), "nsa_max", u + 1)

            def unit_scale(u):
                q, b = divmod(u, 2)
                dve.wait_ge(sem("nsa_p"), u + 1)
                link(dve.reciprocal(uscl, usum))
                g = gtok.rearrange("p s (q h b) -> p s q h b", h=2, b=3)[:, :, q, :, b + 1]
                us = uscl.rearrange("p (s h) -> p s h", s=2)
                link(tt(us, us, g, MUL))
                p0 = pu[:, 0:256].rearrange("p (h t) -> p h t", h=2)
                p1 = pu[:, 256:768].rearrange("p (h t) -> p h t", h=2)
                tt(p0, p0, bl(uscl[:, 0:2], P), MUL)
                mark(tt(p1, p1, bl(uscl[:, 2:4], T), MUL), "nsa_p_scaled", u + 1)

            for n in range(1, 5):
                level(n)
            nsa_blocks()
            level(5)
            rope_k()
            u_out(0)
            state(0)
            u_out(1)
            state(1)
            u_out(2)
            kc_out()
            state(2)
            kc_rope()
            rope_q()
            u_out(3)
            cmp_arg()
            cmp_p()
            dve.wait_ge(sem("rw_norm_mm"), 1)
            flat2 = lambda b: sm[:, b:b + 2, :].rearrange("p b t -> p (b t)")
            mark(stt(Yc, flat2(0), -1.0 / 64, Yc, MUL, ADD), "rw_yc", 1)
            dve.wait_ge(sem("rw_norm_mm"), 2)
            mark(ts(Nm, flat2(2), 1.0 / 64, 64e-5, MUL, ADD), "rw_var", 1)
            dve.wait_ge(sem("rw_std"), 1)
            link(dve.reciprocal(Nm, Nm))
            link(tt(Yc, Yc, Nm, MUL))
            for i in range(4):
                mm = ts(s4(Yc)[:, i, :], s4(Yc)[:, i, :], vv("rw_lnx_g", i), vv("rw_lnx_b", i), MUL, ADD)
            link(mm)
            link(tt(Yc, Yc, bonus, ADD))
            mark(tt(obr[:, 4:8, :], s4(Yc), s4(gl), MUL), "rw_done", 1)
            dve.sem_inc(sem("branches"), 1)
            for u in range(8):
                unit_max(u)
                unit_scale(u)
            dve.wait_ge(sem("ret_mm"), 1)
            link(tt(rt2, sm[:, 0:4, :].rearrange("p b (i t) -> p (b i) t", t=T), bc(trig[:, 0, 1, :], 8), MUL))
            dve.wait_ge(sem("ret_cos"), 1)
            mark(tt(rqk, rt1, rt2, ADD), "ret_vector", 1)
            dve.wait_ge(sem("ret_mm"), 2)
            dve.wait_ge(sem("decay_loaded"), 16)
            for h in range(4):
                tt(sT[:, h, :], sm[:, h, 0:384], decay[:, h, :], MUL).then_inc(sem("ret_sT"), 1)
            obr_low(0, 4, 8, 1)
            obr_low(4, 4, 12, 2)
            obr_low(16, 4, 16, 3)
            dve.wait_ge(sem("ret_mm"), 4)
            o2 = oc.rearrange("p (h j) t -> p h j t", j=2)
            four = sm[:, 4:6, :].rearrange("p b (i t) -> p (b i) t", t=T)
            for j in range(2):
                mm = stt(o2[:, :, j, :], four, -1.0 / 256, o2[:, :, j, :], MUL, ADD)
            mark(mm, "ret_vector", 2)
            dve.wait_ge(sem("ret_mm"), 5)
            mark(ts(rstd4, four, 1.0 / 256, 1e-5, MUL, ADD), "ret_vector", 3)
            dve.wait_ge(sem("ret_scalar"), 3)
            link(dve.reciprocal(rstd4, rstd4))
            for j in range(2):
                mm = tt(o2[:, :, j, :], o2[:, :, j, :], rstd4, MUL)
            link(mm)
            mark(tt(obr[:, 8:16, :], oc, rg, MUL), "ret_vector", 4)
            dve.wait_ge(sem("nsa_o"), 4)
            dve.sem_inc(sem("branches"), 2)

            one = lambda k, v: v

            def ma_low(h):
                s = slice(4 * h, 4 * h + 4)
                dve.wait_ge(sem("ma_o_high"), h + 1)
                tt(X2[:, s, T:2 * T], sm[:, 3:5, :].rearrange("p b (k t) -> p (b k) t", t=T),
                   X2[:, s, 0:T].bitcast(f32), SUB).then_inc(sem("ma_o"), 1)

            def low(m, h, at, n=8):
                dve.wait_ge(sem("hi_done"), at(2, 2 * m + h + 1))
                w = wsplit[(2 * m + h) % 4]
                tt(w[:, 1, 0:n, :], raw[:, m % 2, h, 0:n, :], w[:, 0, 0:n, :].bitcast(f32), SUB).then_inc(sem("lo_done"), 1)

            def width(m, h):
                return (((4, 4), (8, 4))[m % 2])[h] if m < M_LOOP else 8

            def add_cross(dst, number, b):
                dve.wait_ge(sem("cross_out"), number)
                tt(dst, bank[:, b:b + 1, 0:T], cross[:, b:b + 1, :], ADD).then_inc(sem("prod_out"), 1)

            def branch(x, number, gates, step):
                dve.wait_ge(sem("branch_cross"), number)
                m2 = mtmp[:, 2 * x:2 * x + 2, :]
                ins = tt(m2, sm[:, 2 * x:2 * x + 2, 0:T], bcross[:, x], ADD)
                ins.then_inc(sem("branch_out"), 1)
                dve.wait_ge(sem("branch_out"), number)
                step(tt(m2, m2, gates[:, 2 * x:2 * x + 2, :], MUL))

            def merge_tile(tile, number, step):
                step(tt(mtmp[:, 0:2, :], mtmp[:, 0:2, :], mtmp[:, 2:4, :], ADD))
                tt(merged[:, tile, :], mtmp[:, 0:1, :], mtmp[:, 1:2, :], ADD).then_inc(sem("merged"), 1)
                dve.wait_ge(sem("merged"), number)

            def lows(dst, src, need, first, done):
                for q in range(4):
                    low_quarter(dst, src, q, need, first, done)

            def low_quarter(dst, src, q, need, first, done):
                s = slice(4 * q, 4 * q + 4)
                dve.wait_ge(sem(need), first + q)
                tt(dst[:, s, T:2 * T], src[:, s, :], dst[:, s, 0:T].bitcast(f32), SUB).then_inc(sem(done), 1)

            low(0, 0, one, 4)
            low(0, 1, one, 4)
            obr_low(8, 8, 0, 4)
            low(1, 0, one, 8)
            low(1, 1, one, 4)
            merges = [0]

            def mstep(ins):
                merges[0] += 1
                ins.then_inc(sem("merge_step"), 1)
                dve.wait_ge(sem("merge_step"), merges[0])

            for t in range(G0_TILES):
                for x in range(2):
                    m = 2 * t + x
                    low(m + 2, 0, one, width(m + 2, 0))
                    branch(x, m + 1, g0[:, t], mstep)
                    low(m + 2, 1, one, width(m + 2, 1))
                merge_tile(slice(t, t + 1), t + 1, mstep)
                for q in (2 * t, 2 * t + 1) if t < 2 else ():
                    low_quarter(X1, hT, q, "stream_high", 1, "stream_split")
            def merge(i, tiles):
                at = lambda k, v: i * (12 * k) + v
                before = merges[0]

                def lstep(ins):
                    merges[0] += 1
                    ins.then_inc(sem("merge_step"), 1)
                    dve.wait_ge(sem("merge_step"), i * 6 + merges[0])

                for t in range(tiles):
                    for j in range(6):
                        m = M_LOOP + 6 * t + j
                        low(m + 2, 0, at)
                        if j < 4:
                            add_cross(gts[:, t, j:j + 1, :], i * 8 + (4 * t + j + 1), j % 2)
                        else:
                            if j == 4:
                                dve.wait_ge(sem("gates"), i * 2 + (t + 1))
                            branch(j - 4, i * 4 + (2 * G0_TILES + 2 * t + j - 4 + 1), gts[:, t], lstep)
                        low(m + 2, 1, at)
                        if tiles == 1 and j == 4:
                            for q in range(3):
                                low_quarter(X1, merged, q, "stream_high", 5, "stream_split")
                    tile = G0_TILES + t
                    tile = slice(i * 2 + tile, i * 2 + tile + 1) if tiles == 1 else bass.ds(i * 2 + tile, 1)
                    merge_tile(tile, i * 2 + (G0_TILES + t + 1), lstep)
                assert merges[0] - before == 3 * tiles
                merges[0] = before

            with dve.Fori(0, PAIRS) as i:
                merge(i, 2)
            merge(PAIRS, 1)
            low_quarter(X1, merged, 3, "stream_high", 5, "stream_split")

            def position(m, at, dst):
                low(m + 2, 0, at)
                add_cross(dst, at(1, m - R_OFF - 1), m % 2)
                low(m + 2, 1, at)

            def res_quarter(q, step, y, post):
                for k in range(4 * q, 4 * q + 4):
                    mm = stt(y[:, k, :], y[:, k, :], vv(post, k), rstd[:, :], MUL, MUL)
                link(mm)
                mark(tt(res[:, 4 * q:4 * q + 4, :], res[:, 4 * q:4 * q + 4, :], y[:, 4 * q:4 * q + 4, :], ADD),
                     "res_ready", 4 * step + q + 1)

            for j in range(KT):
                position(M_WOUT + j, one, yT[:, j:j + 1, :])
                if j == 7:
                    inv_std(2)
                elif 8 <= j < 12:
                    scaled_quarter(memn, memn, j - 8, "ln_mem_kv", "mem_n", j - 7)
                    low_quarter(X2, memn, j - 8, "stream_high", 9, "stream_split")
            for j in range(KT):
                position(M_MK + j, one, memK[:, j:j + 1, :])
                if j == 1:
                    inv_std(3)
                    dve.wait_ge(sem("x_loaded"), 32)
                elif 2 <= j < 6:
                    res_quarter(j - 2, 0, yT, "ln_mix_post")
                elif j == 9:
                    inv_std(4)
                elif 10 <= j < 14:
                    scaled_quarter(yT, res, j - 10, "ln_mem_q", "h_ready", j - 5)
                if 11 <= j < 15:
                    low_quarter(X1, yT, j - 11, "stream_high", 13, "stream_split")
            for j in range(KT):
                position(M_MV + j, one, vt[:, j % 2:j % 2 + 1, :])

            def loop(base, dst):
                with dve.Fori(0, 4) as i:
                    for j in range(4):
                        position(base + j, lambda k, v: i * (4 * k) + v, dst[:, bass.ds(i * 4 + j, 1), :])

            def softmax(h):
                dve.wait_ge(sem("ma_s_mm"), h + 1)
                if h:
                    dve.wait_ge(sem("ma_p"), h)
                link(dve.tensor_reduce(mmax, sm[:, h % 2, :].rearrange("p (s t) -> p s t", s=2), AX.X, MAX))
                mark(ts(mnb, mmax, -MEM_DH ** -0.5, None, MUL), "ma_max", h + 1)
                dve.wait_ge(sem("ma_p"), h + 1)
                link(dve.reciprocal(msum, msum))
                mark(tt(pm, pm, bl(msum, T), MUL), "ma_pn", h + 1)

            for j in range(KT):
                position(M_WQ + j, one, qT[:, j:j + 1, :])
                if j >= 8 and j % 4 == 0:
                    ma_low(j // 4 - 2)
                elif j >= 4 and j % 4 == 1:
                    softmax(j // 4 - 1)
            ma_low(2)
            softmax(3)
            ma_low(3)
            loop(M_WO, yT)
            inv_std(5)
            for q in range(4):
                res_quarter(q, 1, yT, "ln_mem_post")
            inv_std(6)
            for q in range(5):
                if q < 4:
                    scaled_quarter(yT, res, q, "ln_ffn_pre", "h_ready", 9 + q)
                if q:
                    low_quarter(X1, yT, q - 1, "stream_high", 17, "stream_split")
            w0, w1 = [VEC_AT["ffn_conv_w"][0] + 88 * j for j in range(2)]
            for first, rounds, g in ((0, 4, gA), (4, 18, gB)):
                with dve.Fori(0, rounds) as i:
                    for p in range(2):
                        for s in range(2):
                            j = 2 * p + s
                            m = M_UP + 4 * first + j
                            at = lambda k, v: i * (4 * k) + v
                            n0 = 2 * (4 * first + j)
                            u, r = ub[:, p, s, :], rawu[:, s, :]
                            col = lambda w: vec[:, bass.ds(i * 4 + (w + 4 * first + j), 1)]
                            low(m + 2, 0, at)
                            add_cross(rawu[:, s:s + 1, :], at(1, m - R_OFF - 1), s)
                            low(m + 2, 1, at)
                            dve.wait_ge(sem("prod_out"), at(1, m - R_OFF + 1))
                            dve.wait_ge(sem("ffn_last_tap"), at(1, 4 * first + j + 1))
                            stt(u[:, 1:T], r[:, 0:T - 1], col(w1), u[:, 1:T], MUL, ADD).then_inc(sem("ffn_tap"), 1)
                            dve.wait_ge(sem("ffn_tap"), at(2, n0 + 1))
                            stt(u[:, 2:T], r[:, 0:T - 2], col(w0), u[:, 2:T], MUL, ADD).then_inc(sem("ffn_tap"), 1)
                            dve.wait_ge(sem("ffn_tap"), at(2, n0 + 2))

            def down(i, ahead):
                for t in range(2):
                    for j in range(4):
                        m = M_DOWN + 4 * t + j
                        at = lambda k, v: i * (8 * k) + v
                        if m + 2 < ahead:
                            low(m + 2, 0, at)
                        if j == 3:
                            tile = slice(2 * i + t, 2 * i + t + 1) if ahead < M_END else bass.ds(i * 2 + t, 1)
                            add_cross(yD[:, tile, :], i * 2 + (R_DOWN + t - 1), t)
                        if m + 2 < ahead:
                            low(m + 2, 1, at)

            with dve.Fori(0, 7) as i:
                down(i, M_END)
            down(7, M_DOWN + 8)
            inv_std(7)
            for q in range(4):
                res_quarter(q, 2, yD, "ln_ffn_post")


def tiles(w, m=P):
    k = w.shape[0] // P
    return w.reshape(k, P, w.shape[1] // m, m).transpose(2, 1, 0, 3).reshape(w.shape[1] // m, P, k * m)


def columns(v):
    return v.reshape(-1, P).T


def layout(x):
    z = lambda n: np.zeros(n, np.float32)
    w_in = x["w_in"][0]
    RW, RET, NSA, GATE = 1536, 3520, 6592, 7896
    a = {}
    a["xT"] = x["x"][0].T.reshape(KT, P, T).transpose(1, 0, 2)
    a["memT"] = x["mem"][0].T.reshape(KT, P, T).transpose(1, 0, 2)
    a["positions"] = x["positions"]
    a["w_rw"] = np.concatenate([tiles(w_in[:, RW:RW + 1536]), tiles(w_in[:, RW + 1728:RW + 1984])])
    a["w_zwa"] = tiles(w_in[:, RW + 1536:RW + 1728], 96)
    sc = tiles(w_in[:, :1536])
    a["w_sc"] = sc.reshape(3, 4, P, -1).transpose(1, 0, 2, 3).reshape(12, P, -1)
    a["w_nq"] = tiles(w_in[:, NSA:NSA + 512])
    a["w_kv"] = tiles(w_in[:, NSA + 512:NSA + 1280])
    a["w_ngate"] = tiles(w_in[:, NSA + 1280:NSA + 1304], 24)
    a["w_rq"] = tiles(w_in[:, RET:RET + 512])
    a["w_rk"] = tiles(w_in[:, RET + 512:RET + 1024])
    a["w_rv"] = tiles(w_in[:, RET + 1024:RET + 2048])
    a["w_rg"] = tiles(w_in[:, RET + 2048:RET + 3072])
    for j in range(4):
        a[f"w_g{j}"] = tiles(w_in[:, GATE + j * D:GATE + (j + 1) * D])
    a["w_brab"] = tiles(x["w_branch"][0][:1024])
    a["w_brcd"] = tiles(x["w_branch"][0][1024:])
    a["w_cmp1"] = np.concatenate([tiles(x["nsa_cmp_w1"][0, k]) for k in range(2)])
    w2 = x["nsa_cmp_w2"][0].reshape(2, 2, P, 64).transpose(2, 0, 1, 3)
    a["w_cmp2"] = np.concatenate([w2, w2], -1)
    a["lora_wa"] = np.stack([x["rw_w2"][0], x["rw_a2"][0]], 1)
    a["lora_g"] = x["rw_g2"][0].reshape(2, P, 512).transpose(1, 0, 2)
    a["w_out"], a["w_q"], a["w_o"] = [tiles(x[k][0]) for k in ("w_out", "mem_wq", "mem_wo")]
    a["w_mk"], a["w_mv"] = tiles(x["mem_wkv"][0][:, :D]), tiles(x["mem_wkv"][0][:, D:])
    up = tiles(x["ffn_w_up"][0])
    a["w_up"] = up.reshape(2, FT, P, -1).transpose(1, 0, 2, 3).reshape(2 * FT, P, -1)
    a["w_dn"] = tiles(x["ffn_w_down"][0]).reshape(KT, P, 4, 11 * P).transpose(0, 2, 1, 3).reshape(4 * KT, P, 11 * P)
    mu = x["rw_mu"][0]
    parts = {k: columns(x[k][0]) for k in ("ln_mix_pre", "ln_mix_post", "ln_mem_q", "ln_mem_kv", "ln_mem_post",
                                           "ln_ffn_pre", "ln_ffn_post", "rw_w0", "rw_a0", "rw_k_k", "rw_k_a",
                                           "rw_r_k", "rw_lnx_g", "rw_lnx_b", "sc_conv")}
    parts["rw_mu"] = columns(np.concatenate([mu[:1632], z(32), mu[1632:1728], z(32), mu[1728:]]))
    parts["cmp_pos"] = x["nsa_cmp_pos"][0].reshape(2, 16, P).transpose(2, 0, 1).reshape(P, 32)
    pair = lambda v: v.reshape(-1, 2, FT, P).transpose(3, 0, 2, 1).reshape(P, -1)
    parts["ffn_conv_w"] = pair(x["ffn_conv_w"][0])
    parts["ffn_conv_b"] = pair(x["ffn_conv_b"][0])
    a["vec"] = np.concatenate([parts[n] for n, _ in VEC], 1)
    return {k: np.ascontiguousarray(v) for k, v in a.items()}


def kernel(**inputs):
    import concourse.bacc as bacc
    from concourse.bass_utils import run_bass_kernel_spmd

    arrays = layout({k: np.asarray(v) for k, v in inputs.items()})
    consts, const_at = build_constants()
    arrays["constants"] = consts
    arrays["decay"] = decay_table()
    nc = bacc.Bacc("TRN2", target_bir_lowering=False, num_devices=1)
    A = {k: nc.dram_tensor("in_" + k, v.shape, mybir.dt.from_np(v.dtype), kind="ExternalInput").ap()
         for k, v in arrays.items()}
    out = nc.dram_tensor("out", (P, KT, T), mybir.dt.float32, kind="ExternalOutput").ap()
    program(nc, A, A["constants"], A["decay"], const_at, out)
    r = run_bass_kernel_spmd(nc, [{"in_" + k: v for k, v in arrays.items()}], core_ids=[0])
    y = r.results[0]["out"]
    return np.ascontiguousarray(y.transpose(2, 1, 0).reshape(1, T, D))
```
